# Optimizing a Trainium2 kernel written in Bass

```python
import jax
import jax.numpy as jnp
from jax import lax
import numpy as np

D_MODEL = 1024
BATCH = 1
SEQ = 1024
DEPTH = 1

HEAD_DIM = 64
RW_HEADS = 8
RW_WIDTH = RW_HEADS * HEAD_DIM
NSA_HEADS = 8
NSA_KV_HEADS = 2
NSA_GROUP = NSA_HEADS // NSA_KV_HEADS
NSA_WIDTH = NSA_HEADS * HEAD_DIM
NSA_KV_WIDTH = NSA_KV_HEADS * HEAD_DIM
MIX_WIDTH = RW_WIDTH + NSA_WIDTH
RW_DECAY_LORA = 64
RW_ICLR_LORA = 64
RW_GATE_LORA = 128
CMP_LEN = 32
CMP_STRIDE = 16
CMP_HIDDEN = 256
SEL_BLOCK = 64
SEL_TOPK = 8
SEL_Q_BLOCK = 64
WINDOW = 256
Q_BLOCK = 128
ROPE_THETA = 10000.0
N_EXPERTS = 32
TOP_K = 4
D_FF = 1024
SWIGLU_LIMIT = 7.0
SWIGLU_ALPHA = 1.702
MOE_ROW_BLOCK = 128
NORM_EPS = 1e-6
LNX_EPS = 64e-5
FORCE_SCORE = 1e6
NEG_INF = -1e30
IN_SPLITS = (RW_WIDTH, RW_WIDTH, RW_WIDTH, NSA_WIDTH, NSA_KV_WIDTH, NSA_KV_WIDTH, NSA_KV_WIDTH, NSA_KV_WIDTH, NSA_KV_WIDTH, NSA_KV_WIDTH, 3 * NSA_HEADS)
N_IN = 3 * RW_WIDTH + NSA_WIDTH + 6 * NSA_KV_WIDTH + 3 * NSA_HEADS

kernel_name = 'hybrid_rwkv7_nsa_moe'

def rmsnorm(x, g, eps=NORM_EPS):
    xf = x.astype(jnp.float32)
    y = xf * lax.rsqrt(jnp.mean(xf * xf, axis=-1, keepdims=True) + eps)
    return (y * g.astype(jnp.float32)).astype(x.dtype)

def token_shift(t):
    return jnp.pad(t, ((0, 0), (1, 0), (0, 0)))[:, :-1]

def rope(t, pos):
    half = t.shape[-1] // 2
    inv = ROPE_THETA ** (-jnp.arange(half, dtype=jnp.float32) / half)
    ang = jnp.asarray(pos, jnp.float32)[:, None] * inv[None, :]
    cos = jnp.cos(ang)[None, :, None, :]
    sin = jnp.sin(ang)[None, :, None, :]
    tf = t.astype(jnp.float32)
    t1, t2 = tf[..., :half], tf[..., half:]
    return jnp.concatenate([t1 * cos - t2 * sin, t2 * cos + t1 * sin], axis=-1).astype(t.dtype)

def masked_softmax(s, mask):
    s = jnp.where(mask, s.astype(jnp.float32), NEG_INF)
    m = jnp.max(s, axis=-1, keepdims=True)
    e = jnp.exp(s - m) * mask
    d = jnp.sum(e, axis=-1, keepdims=True)
    return e / jnp.where(d > 0, d, 1.0)

def rwkv7_mix(xn, r, k, v, mu_rkv, mu_wag, w0, w1, w2, a0, a1, a2, g1, g2, k_k, k_a, r_k, lnx_g, lnx_b):
    B, S, _ = xn.shape
    H, N = RW_HEADS, HEAD_DIM
    f32 = jnp.float32
    r = r + mu_rkv[0] * (token_shift(r) - r)
    k = k + mu_rkv[1] * (token_shift(k) - k)
    v = v + mu_rkv[2] * (token_shift(v) - v)
    dx = token_shift(xn) - xn
    xw = xn + mu_wag[0] * dx
    xa = xn + mu_wag[1] * dx
    xg = xn + mu_wag[2] * dx
    w = -jax.nn.softplus(-(w0 + jnp.tanh(xw @ w1) @ w2)) - 0.5
    a = jax.nn.sigmoid(a0 + (xa @ a1) @ a2)
    g = jax.nn.sigmoid(xg @ g1) @ g2
    kk = (k * k_k).astype(f32).reshape(B, S, H, N)
    kk = kk / jnp.maximum(jnp.sqrt(jnp.sum(kk * kk, axis=-1, keepdims=True)), 1e-12)
    k = k * (1.0 + (a - 1.0) * k_a)
    decay = jnp.exp(-jnp.exp(w.astype(f32))).reshape(B, S, H, N)
    rh = r.astype(f32).reshape(B, S, H, N)
    kh = k.astype(f32).reshape(B, S, H, N)
    vh = v.astype(f32).reshape(B, S, H, N)
    ah = a.astype(f32).reshape(B, S, H, N)
    a_vec = -kk
    b_vec = kk * ah

    def step(state, inp):
        r_t, w_t, k_t, v_t, av_t, bv_t = inp
        sa = jnp.einsum('bhij,bhj->bhi', state, av_t)
        state = state * w_t[:, :, None, :] + sa[..., :, None] * bv_t[..., None, :] + v_t[..., :, None] * k_t[..., None, :]
        y_t = jnp.einsum('bhij,bhj->bhi', state, r_t)
        return state, y_t

    xs = tuple(jnp.swapaxes(t, 0, 1) for t in (rh, decay, kh, vh, a_vec, b_vec))
    _, y = lax.scan(step, jnp.zeros((B, H, N, N), f32), xs)
    y = jnp.swapaxes(y, 0, 1)
    mu = jnp.mean(y, axis=-1, keepdims=True)
    var = jnp.mean(jnp.square(y - mu), axis=-1, keepdims=True)
    y = ((y - mu) * lax.rsqrt(var + LNX_EPS)).reshape(B, S, RW_WIDTH)
    y = y * lnx_g.astype(f32) + lnx_b.astype(f32)
    bonus = jnp.sum(rh * kh * r_k.astype(f32), axis=-1, keepdims=True) * vh
    y = (y + bonus.reshape(B, S, RW_WIDTH)) * g.astype(f32)
    return y.astype(xn.dtype)

def nsa_mix(q, kc, vc, ks, vs, kw, vw, gate_logits, qn_g, kn_g, pe, cmp_w1, cmp_w2):
    B, S, _ = q.shape
    H, Hk, G, d = NSA_HEADS, NSA_KV_HEADS, NSA_GROUP, HEAD_DIM
    f32 = jnp.float32
    scale = HEAD_DIM ** -0.5
    pos = np.arange(S)
    q = rmsnorm(q.reshape(B, S, H, d), qn_g)
    q_rot = rope(q, pos)
    kc, vc, ks, vs, kw, vw = (t.reshape(B, S, Hk, d) for t in (kc, vc, ks, vs, kw, vw))

    n_cmp = (S - CMP_LEN) // CMP_STRIDE + 1
    cmp_start = np.arange(n_cmp) * CMP_STRIDE
    blk_idx = cmp_start[:, None] + np.arange(CMP_LEN)[None, :]

    def compress(t, pe_i, w1_i, w2_i):
        blocks = t[:, blk_idx] + pe_i[None, None, :, None, :]
        hid = jax.nn.gelu(jnp.einsum('bnlkd,ldf->bnkf', blocks, w1_i))
        return jnp.einsum('bnkf,fd->bnkd', hid, w2_i)

    k_cmp = rmsnorm(compress(kc, pe[0], cmp_w1[0], cmp_w2[0]), kn_g[0])
    v_cmp = compress(vc, pe[1], cmp_w1[1], cmp_w2[1])
    qg = q.reshape(B, S, Hk, G, d)
    s_cmp = jnp.einsum('bskgd,bnkd->bkgsn', qg, k_cmp) * scale
    cmp_mask = (cmp_start + CMP_LEN - 1)[None, :] <= pos[:, None]
    p_cmp = masked_softmax(s_cmp, cmp_mask)
    o_cmp = jnp.einsum('bkgsn,bnkd->bskgd', p_cmp, v_cmp.astype(f32)).reshape(B, S, H, d)

    n_sel = S // SEL_BLOCK
    sel_start = np.arange(n_sel) * SEL_BLOCK
    overlap = ((cmp_start[:, None] < sel_start[None, :] + SEL_BLOCK) & (cmp_start[:, None] + CMP_LEN > sel_start[None, :])).astype(np.float32)
    imp = jnp.einsum('bkgsn,nj->bksj', p_cmp, jnp.asarray(overlap))
    cur = pos // SEL_BLOCK
    jj = np.arange(n_sel)
    forced = (jj[None, :] == 0) | (jj[None, :] == cur[:, None]) | (jj[None, :] == cur[:, None] - 1)
    imp = jnp.where(forced, FORCE_SCORE, imp)
    imp = jnp.where(jj[None, :] > cur[:, None], -FORCE_SCORE, imp)
    n_top = min(SEL_TOPK, n_sel)
    _, sel_idx = lax.top_k(imp, n_top)

    ks_r = rope(rmsnorm(ks, kn_g[1]), pos)
    k_blocks = ks_r.reshape(B, n_sel, SEL_BLOCK, Hk, d).transpose(0, 3, 1, 2, 4)
    v_blocks = vs.reshape(B, n_sel, SEL_BLOCK, Hk, d).transpose(0, 3, 1, 2, 4)
    nqs = S // SEL_Q_BLOCK
    q_chunks = q_rot.reshape(B, nqs, SEL_Q_BLOCK, Hk, G, d).transpose(1, 0, 3, 4, 2, 5)
    idx_chunks = sel_idx.reshape(B, Hk, nqs, SEL_Q_BLOCK, n_top).transpose(2, 0, 1, 3, 4)
    qpos_chunks = jnp.asarray(pos.reshape(nqs, SEL_Q_BLOCK))
    bi = jnp.arange(B)[:, None, None, None]
    hi = jnp.arange(Hk)[None, :, None, None]

    def sel_block(args):
        qc, ic, qp = args
        kg = k_blocks[bi, hi, ic]
        vg = v_blocks[bi, hi, ic]
        s = jnp.einsum('bkgqd,bkqnld->bkgqnl', qc, kg) * scale
        kpos = ic[..., None] * SEL_BLOCK + jnp.arange(SEL_BLOCK)
        mask = kpos <= qp[None, None, :, None, None]
        p = masked_softmax(s.reshape(B, Hk, G, SEL_Q_BLOCK, -1), mask.reshape(B, Hk, 1, SEL_Q_BLOCK, -1))
        return jnp.einsum('bkgqm,bkqmd->bkgqd', p, vg.reshape(B, Hk, SEL_Q_BLOCK, -1, d).astype(f32))

    o_sel = lax.map(sel_block, (q_chunks, idx_chunks, qpos_chunks))
    o_sel = o_sel.transpose(1, 0, 4, 2, 3, 5).reshape(B, S, H, d)

    kw_r = rope(rmsnorm(kw, kn_g[2]), pos)
    nb = S // Q_BLOCK
    n_band = WINDOW // Q_BLOCK + 1

    def band(t):
        tb = t.reshape(B, nb, Q_BLOCK, Hk, d).transpose(0, 3, 1, 2, 4)
        tp = jnp.pad(tb, ((0, 0), (0, 0), (n_band - 1, 0), (0, 0), (0, 0)))
        return jnp.concatenate([tp[:, :, i:i + nb] for i in range(n_band)], axis=3)

    k_band = band(kw_r)
    v_band = band(vw)
    qw = q_rot.reshape(B, nb, Q_BLOCK, Hk, G, d).transpose(0, 3, 4, 1, 2, 5)
    s_win = jnp.einsum('bkgiqd,bkird->bkgiqr', qw, k_band) * scale
    qpos = pos.reshape(nb, Q_BLOCK)
    kpos = (np.arange(nb)[:, None] - (n_band - 1)) * Q_BLOCK + np.arange(n_band * Q_BLOCK)[None, :]
    win_mask = (kpos[:, None, :] <= qpos[:, :, None]) & (kpos[:, None, :] > qpos[:, :, None] - WINDOW) & (kpos[:, None, :] >= 0)
    p_win = masked_softmax(s_win, win_mask)
    o_win = jnp.einsum('bkgiqr,bkird->bkgiqd', p_win, v_band.astype(f32))
    o_win = o_win.transpose(0, 3, 4, 1, 2, 5).reshape(B, S, H, d)

    gates = jax.nn.sigmoid(gate_logits.astype(f32)).reshape(B, S, H, 3)
    o = gates[..., 0:1] * o_cmp + gates[..., 1:2] * o_sel + gates[..., 2:3] * o_win
    return o.reshape(B, S, NSA_WIDTH).astype(q.dtype)

def moe_ffn(h, wr, br, w1, b1, w2, b2):
    B, S, D = h.shape
    T = B * S
    M = MOE_ROW_BLOCK
    hf = h.reshape(T, D)
    logits = (hf @ wr + br).astype(jnp.float32)
    top_v, top_e = lax.top_k(logits, TOP_K)
    gate = jax.nn.softmax(top_v, axis=-1)
    flat_e = top_e.reshape(-1)
    flat_t = jnp.arange(T * TOP_K) // TOP_K
    flat_g = gate.reshape(-1)
    order = jnp.argsort(flat_e)
    se, st, sg = flat_e[order], flat_t[order], flat_g[order]
    counts = jnp.bincount(flat_e, length=N_EXPERTS)
    padded = ((counts + M - 1) // M) * M
    pad_end = jnp.cumsum(padded)
    pad_start = pad_end - padded
    sort_start = jnp.cumsum(counts) - counts
    dest = pad_start[se] + jnp.arange(T * TOP_K) - sort_start[se]
    n_rows = T * TOP_K + N_EXPERTS * M
    n_blk = n_rows // M
    row_tok = jnp.full((n_rows,), T, jnp.int32).at[dest].set(st)
    row_gate = jnp.zeros((n_rows,), jnp.float32).at[dest].set(sg)
    blk_e = jnp.minimum(jnp.searchsorted(pad_end, jnp.arange(n_blk) * M, side='right'), N_EXPERTS - 1)
    h_pad = jnp.concatenate([hf, jnp.zeros((1, D), hf.dtype)], axis=0)

    def expert_block(args):
        tok, g, e = args
        u = h_pad[tok] @ w1[e] + b1[e]
        glu = jnp.minimum(u[:, :D_FF], SWIGLU_LIMIT)
        lin = jnp.clip(u[:, D_FF:], -SWIGLU_LIMIT, SWIGLU_LIMIT)
        act = glu * jax.nn.sigmoid(SWIGLU_ALPHA * glu) * (lin + 1.0)
        y = act @ w2[e] + b2[e]
        return y * g[:, None].astype(y.dtype)

    y_rows = lax.map(expert_block, (row_tok.reshape(n_blk, M), row_gate.reshape(n_blk, M), blk_e))
    out = jnp.zeros((T + 1, D), y_rows.dtype).at[row_tok].add(y_rows.reshape(n_rows, D))
    return out[:T].reshape(B, S, D).astype(h.dtype)

def hybrid_layer(x, ln1_g, w_in, rw_mu_rkv, rw_mu_wag, rw_w0, rw_w1, rw_w2, rw_a0, rw_a1, rw_a2, rw_g1, rw_g2, rw_k_k, rw_k_a, rw_r_k, rw_lnx_g, rw_lnx_b, nsa_qn_g, nsa_kn_g, nsa_pe, nsa_cmp_w1, nsa_cmp_w2, w_out, ln2_g, moe_wr, moe_br, moe_w1, moe_b1, moe_w2, moe_b2):
    xn = rmsnorm(x, ln1_g)
    proj = xn @ w_in
    cuts = np.cumsum(np.array(IN_SPLITS))[:-1].tolist()
    r, k, v, q, kc, vc, ks, vs, kw, vw, gl = jnp.split(proj, cuts, axis=-1)
    y_rw = rwkv7_mix(xn, r, k, v, rw_mu_rkv, rw_mu_wag, rw_w0, rw_w1, rw_w2, rw_a0, rw_a1, rw_a2, rw_g1, rw_g2, rw_k_k, rw_k_a, rw_r_k, rw_lnx_g, rw_lnx_b)
    y_nsa = nsa_mix(q, kc, vc, ks, vs, kw, vw, gl, nsa_qn_g, nsa_kn_g, nsa_pe, nsa_cmp_w1, nsa_cmp_w2)
    x = x + jnp.concatenate([y_rw, y_nsa], axis=-1) @ w_out
    x = x + moe_ffn(rmsnorm(x, ln2_g), moe_wr, moe_br, moe_w1, moe_b1, moe_w2, moe_b2)
    return x

def setup_inputs(seed: int = 0) -> dict:
    key = jax.random.key(seed)
    kk = jax.random.split(key, 32)
    f32 = jnp.float32
    L, D = DEPTH, D_MODEL

    def nrm(k, shape, s):
        return jax.random.normal(k, shape, f32) * s

    def uni(k, shape, lo, hi):
        return jax.random.uniform(k, shape, f32, lo, hi)

    return {
        'x': nrm(kk[0], (BATCH, SEQ, D), 1.0),
        'ln1_g': 1.0 + nrm(kk[1], (L, D), 0.02),
        'w_in': nrm(kk[2], (L, D, N_IN), D ** -0.5),
        'rw_mu_rkv': uni(kk[3], (L, 3, RW_WIDTH), 0.0, 1.0),
        'rw_mu_wag': uni(kk[4], (L, 3, D), 0.0, 1.0),
        'rw_w0': uni(kk[5], (L, RW_WIDTH), -4.0, 1.0),
        'rw_w1': nrm(kk[6], (L, D, RW_DECAY_LORA), 0.5 * D ** -0.5),
        'rw_w2': nrm(kk[7], (L, RW_DECAY_LORA, RW_WIDTH), 0.5 * RW_DECAY_LORA ** -0.5),
        'rw_a0': nrm(kk[8], (L, RW_WIDTH), 0.1),
        'rw_a1': nrm(kk[9], (L, D, RW_ICLR_LORA), 0.5 * D ** -0.5),
        'rw_a2': nrm(kk[10], (L, RW_ICLR_LORA, RW_WIDTH), 0.5 * RW_ICLR_LORA ** -0.5),
        'rw_g1': nrm(kk[11], (L, D, RW_GATE_LORA), D ** -0.5),
        'rw_g2': nrm(kk[12], (L, RW_GATE_LORA, RW_WIDTH), RW_GATE_LORA ** -0.5),
        'rw_k_k': 0.85 + nrm(kk[13], (L, RW_WIDTH), 0.05),
        'rw_k_a': 1.0 + nrm(kk[14], (L, RW_WIDTH), 0.05),
        'rw_r_k': nrm(kk[15], (L, RW_HEADS, HEAD_DIM), 0.1),
        'rw_lnx_g': 1.0 + nrm(kk[16], (L, RW_WIDTH), 0.02),
        'rw_lnx_b': nrm(kk[17], (L, RW_WIDTH), 0.01),
        'nsa_qn_g': 1.0 + nrm(kk[18], (L, HEAD_DIM), 0.02),
        'nsa_kn_g': 1.0 + nrm(kk[19], (L, 3, HEAD_DIM), 0.02),
        'nsa_pe': nrm(kk[20], (L, 2, CMP_LEN, HEAD_DIM), 0.02),
        'nsa_cmp_w1': nrm(kk[21], (L, 2, CMP_LEN, HEAD_DIM, CMP_HIDDEN), (CMP_LEN * HEAD_DIM) ** -0.5),
        'nsa_cmp_w2': nrm(kk[22], (L, 2, CMP_HIDDEN, HEAD_DIM), CMP_HIDDEN ** -0.5),
        'w_out': nrm(kk[23], (L, MIX_WIDTH, D), MIX_WIDTH ** -0.5),
        'ln2_g': 1.0 + nrm(kk[24], (L, D), 0.02),
        'moe_wr': nrm(kk[25], (L, D, N_EXPERTS), D ** -0.5),
        'moe_br': nrm(kk[26], (L, N_EXPERTS), 0.01),
        'moe_w1': nrm(kk[27], (L, N_EXPERTS, D, 2 * D_FF), D ** -0.5),
        'moe_b1': nrm(kk[28], (L, N_EXPERTS, 2 * D_FF), 0.01),
        'moe_w2': nrm(kk[29], (L, N_EXPERTS, D_FF, D), D_FF ** -0.5),
        'moe_b2': nrm(kk[30], (L, N_EXPERTS, D), 0.01),
    }

def reference(x, ln1_g, w_in, rw_mu_rkv, rw_mu_wag, rw_w0, rw_w1, rw_w2, rw_a0, rw_a1, rw_a2, rw_g1, rw_g2, rw_k_k, rw_k_a, rw_r_k, rw_lnx_g, rw_lnx_b, nsa_qn_g, nsa_kn_g, nsa_pe, nsa_cmp_w1, nsa_cmp_w2, w_out, ln2_g, moe_wr, moe_br, moe_w1, moe_b1, moe_w2, moe_b2):
    for l in range(DEPTH):
        x = hybrid_layer(x, ln1_g[l], w_in[l], rw_mu_rkv[l], rw_mu_wag[l], rw_w0[l], rw_w1[l], rw_w2[l], rw_a0[l], rw_a1[l], rw_a2[l], rw_g1[l], rw_g2[l], rw_k_k[l], rw_k_a[l], rw_r_k[l], rw_lnx_g[l], rw_lnx_b[l], nsa_qn_g[l], nsa_kn_g[l], nsa_pe[l], nsa_cmp_w1[l], nsa_cmp_w2[l], w_out[l], ln2_g[l], moe_wr[l], moe_br[l], moe_w1[l], moe_b1[l], moe_w2[l], moe_b2[l])
    return x


_drawn_inputs = setup_inputs


def setup_inputs(seed=0):
    import zlib

    import numpy as np

    out = dict(_drawn_inputs(seed))
    spreads = {}
    factors = {'rw_lnx_b': 3.499,
     'nsa_qn_g': 4.75,
     'nsa_kn_g': 4.225,
     'nsa_pe': 3.392,
     'moe_b1': 8.0,
     'moe_b2': 8.0}
    for name, (base, spread) in spreads.items():
        noise = np.random.default_rng([zlib.crc32(name.encode()), seed]).standard_normal(out[name].shape)
        drawn = base * np.exp(spread * noise) if base else spread * noise
        out[name] = jnp.asarray(drawn.astype(out[name].dtype))
    for name, factor in factors.items():
        out[name] = (out[name] * factor).astype(out[name].dtype)
    return out
```

```python
import concourse.bass as bass
from concourse import mybir
from contextlib import ExitStack
import numpy as np

F32 = mybir.dt.float32
I32 = mybir.dt.int32
ALU = mybir.AluOpType
ACT = mybir.ActivationFunctionType
AX = mybir.AxisListType

P = 128
D = 1024
S = 1024
NT = S // P
DC = D // P
BANK = 512
EPS = 1e-6
N_EXP = 32
TOP_K = 4
D_FF = 1024
PAD_ROWS = P
LIST_K = S // P
N_SLOTS = N_EXP * LIST_K
LIMIT = 7.0
ALPHA = 1.702


def sem_list(nc, ctx, names):
    out = [nc.alloc_semaphore(n) for n in names]

    def over():
        nc.clear_and_free_semaphores(out)
        nc.all_engine_barrier(sem_only=True)
    ctx.callback(over)
    return out


def sems(nc, ctx, names, prefix=""):
    names = names.split()
    return dict(zip(names, sem_list(nc, ctx, [prefix + n for n in names])))


def chained(eng, sem):
    count = [0]

    def link(ins):
        count[0] += 1
        ins.then_inc(sem, 1)
        eng.wait_ge(sem, count[0])
    return link


def route_phase(nc, T):
    with ExitStack() as ctx:
        sb = lambda n, s, dt=F32: ctx.enter_context(nc.sbuf_tensor(n, s, dt))
        pb = lambda n, s: ctx.enter_context(nc.psum_tensor(n, s, F32))
        wout = sb("wout", [P, DC, D])
        x2 = sb("x2", [P, NT, D])
        hrow = sb("hrow", [P, 2, D])
        hT = sb("hT", [P, 2, DC, P])
        g2 = sb("g2", [P, D])
        wr = sb("wr", [P, DC, N_EXP])
        br = sb("br", [P, N_EXP])
        junk = sb("junk", [P, D])
        zero = sb("zero", [P, D])
        st = sb("st", [P, 3, NT])
        L = sb("L", [P, NT, N_EXP])
        cmp1 = sb("cmp1", [P, N_EXP, N_EXP])
        cmp2 = sb("cmp2", [P, N_EXP, N_EXP])
        lower = sb("lower", [P, N_EXP, N_EXP])
        rank = sb("rank", [P, NT, N_EXP])
        sel = sb("sel", [P, NT, N_EXP])
        G = sb("G", [P, NT, N_EXP])
        mx = sb("mx", [P, NT])
        den = sb("den", [P, NT])
        upper = sb("upper", [P, P])
        ones = sb("ones", [P, P])
        ecol = sb("ecol", [P, N_EXP])
        posi = sb("posi", [P, NT, N_EXP], I32)
        posk = sb("posk", [P, NT, N_EXP], I32)
        posf = sb("posf", [P, NT, N_EXP])
        poskf = sb("poskf", [P, NT, N_EXP])
        pick = sb("pick", [P, NT, N_EXP])
        dst = sb("dst", [P, TOP_K, NT])
        dsti = sb("dsti", [P, TOP_K, NT], I32)
        entry = sb("entry", [P, TOP_K, NT, 2], I32)
        gsel = sb("gsel", [P, TOP_K, NT])
        tok = sb("tok", [P, NT], I32)
        padlist = sb("padlist", [P, N_SLOTS, 2], I32)
        PO = pb("PO", [P, 2, D])
        PT = pb("PT", [P, 2, BANK])
        PL = pb("PL", [P, BANK])
        PC = pb("PC", [P, BANK])
        q = sems(nc, ctx, "r_ld_w r_ld_x r_ld_c r_po r_x2 r_ss r_ms r_sq r_h r_st_x r_st_ha r_st_hb r_st_x0 r_st_h0 r_tp r_hT r_lg "
                          "r_logit r_pool r_padst r_sel r_pos r_exp r_ent r_scat r_back r_dve r_mxn r_cnt")
        block = ctx.enter_context(nc.Block())
        h_stored = (q["r_st_ha"], q["r_st_hb"])
        x_rows = T["x"].rearrange("o (t p) d -> (o t) p d", p=P)

        @block.sync
        def _(sp):
            for k in range(DC):
                sp.dma_start(wout[:, k, :], T["w_out"][0, k * P:(k + 1) * P, :]).then_inc(q["r_ld_w"], 16)
            sp.dma_start(wr[:, :, :], T["moe_wr"][0].rearrange("(k p) e -> p k e", p=P)).then_inc(q["r_ld_c"], 16)
            sp.dma_start(upper[:, :], T["c_upper"]).then_inc(q["r_ld_c"], 16)
            sp.dma_start(lower[:, :, :].rearrange("p a b -> p (a b)"),
                         T["c_lower"].broadcast_to([P, N_EXP * N_EXP])).then_inc(q["r_ld_c"], 16)
            for i in range(NT):
                sp.wait_ge(q["r_x2"], i + 1)
                sp.dma_start(T["out"][i * P:(i + 1) * P, :], x2[:, i, :]).then_inc(q["r_st_x"], 16)
                sp.wait_ge(q["r_h"], i + 1)
                sp.dma_start(T["h_rows"][i * P:(i + 1) * P, :], hrow[:, i % 2, :]).then_inc(h_stored[i % 2], 16)
            sp.wait_ge(q["r_st_x"], 16 * NT)
            for s_h in h_stored:
                sp.wait_ge(s_h, 16 * NT // 2)

        @block.scalar
        def _(act):
            for i in range(NT):
                act.dma_start(x2[:, i, :], x_rows[i]).then_inc(q["r_ld_x"], 16)
            act.dma_start(g2[:, :], T["ln2_g"].broadcast_to([P, D])).then_inc(q["r_ld_c"], 16)
            act.dma_start(br[:, :], T["moe_br"].broadcast_to([P, N_EXP])).then_inc(q["r_ld_c"], 16)
            for i in range(NT):
                act.wait_ge(q["r_x2"], i + 1)
                if i:
                    act.wait_ge(q["r_ss"], i)
                nc.scalar.activation(junk[:, :], x2[:, i, :], ACT.Square,
                                     accum_out=st[:, 0, i:i + 1]).then_inc(q["r_ss"], 1)
                act.wait_ge(q["r_ms"], i + 1)
                nc.scalar.activation(st[:, 2, i:i + 1], st[:, 1, i:i + 1], ACT.Sqrt).then_inc(q["r_sq"], 1)
                for g in range(2):
                    act.wait_ge(q["r_tp"], 2 * i + g + 1)
                    if i >= 2:
                        act.wait_ge(q["r_lg"], i - 1)
                    nc.scalar.activation(hT[:, i % 2, 4 * g:4 * g + 4, :], PT[:, g, :].rearrange("p (a b) -> p a b", b=P),
                                         ACT.Copy).then_inc(q["r_hT"], 1)
            act.wait_ge(q["r_mxn"], 1)
            nc.scalar.activation(G[:, :, :], G[:, :, :], ACT.Exp).then_inc(q["r_exp"], 1)

        @block.tensor
        def _(pe):
            def project(i):
                if i == 0:
                    pe.wait_ge(q["r_ld_w"], 16 * DC)
                if i >= 2:
                    pe.wait_ge(q["r_x2"], i - 1)
                for n in range(2):
                    for k in range(DC):
                        last = nc.tensor.matmul(PO[:, i % 2, n * BANK:(n + 1) * BANK], T["yT"][:, k, i * P:(i + 1) * P],
                                                wout[:, k, n * BANK:(n + 1) * BANK], start=(k == 0), stop=(k == DC - 1))
                last.then_inc(q["r_po"], 1)

            def logits(i):
                pe.wait_ge(q["r_h"], i + 1)
                for g in range(2):
                    if i:
                        pe.wait_ge(q["r_hT"], 2 * (i - 1) + g + 1)
                    for c in range(4):
                        last = nc.tensor.transpose(PT[:, g, c * P:(c + 1) * P],
                                                   hrow[:, i % 2, (4 * g + c) * P:(4 * g + c + 1) * P], T["ident"][:, :])
                    last.then_inc(q["r_tp"], 1)
                pe.wait_ge(q["r_hT"], 2 * i + 2)
                if i == 0:
                    pe.wait_ge(q["r_ld_c"], 16 * 5)
                else:
                    pe.wait_ge(q["r_logit"], i)
                for k in range(DC):
                    last = nc.tensor.matmul(PL[:, 0:N_EXP], hT[:, i % 2, k, :], wr[:, k, :],
                                            start=(k == 0), stop=(k == DC - 1))
                last.then_inc(q["r_lg"], 1)

            project(0)
            for i in range(NT):
                if i + 1 < NT:
                    project(i + 1)
                logits(i)
            pe.wait_ge(q["r_pool"], 3)
            pe.wait_ge(q["r_sel"], 1)
            for i in range(NT):
                for j in range(i + 1):
                    last = nc.tensor.matmul(PC[:, i * N_EXP:(i + 1) * N_EXP], upper[:, :] if j == i else ones[:, :],
                                            sel[:, j, :], start=(j == 0), stop=(j == i))
            last.then_inc(q["r_pos"], 1)
            for j in range(NT):
                last = nc.tensor.matmul(PL[:, 0:N_EXP], ones[:, :], sel[:, j, :], start=(j == 0), stop=(j == NT - 1))
            last.then_inc(q["r_pos"], 1)

        @block.vector
        def _(dve):
            link = chained(dve, q["r_dve"])
            dve.wait_ge(q["r_ld_c"], 16 * 5)
            for i in range(NT):
                dve.wait_ge(q["r_po"], i + 1)
                if i == 0:
                    dve.wait_ge(q["r_ld_x"], 16 * NT)
                nc.vector.tensor_tensor(x2[:, i, :], PO[:, i % 2, :], x2[:, i, :], ALU.add).then_inc(q["r_x2"], 1)
                dve.wait_ge(q["r_ss"], i + 1)
                nc.vector.tensor_scalar(st[:, 1, i:i + 1], st[:, 0, i:i + 1], 1.0 / D, EPS,
                                        ALU.mult, ALU.add).then_inc(q["r_ms"], 1)
                dve.wait_ge(q["r_sq"], i + 1)
                link(nc.vector.reciprocal(st[:, 0, i:i + 1], st[:, 2, i:i + 1]))
                if i >= 2:
                    dve.wait_ge(h_stored[i % 2], 16 * (i // 2))
                    dve.wait_ge(q["r_tp"], 2 * (i - 1))
                nc.vector.scalar_tensor_tensor(out=hrow[:, i % 2, :], in0=x2[:, i, :], scalar=st[:, 0, i:i + 1],
                                               in1=g2[:, :], op0=ALU.mult, op1=ALU.mult).then_inc(q["r_h"], 1)
                if i:
                    dve.wait_ge(q["r_lg"], i)
                    nc.vector.tensor_tensor(L[:, i - 1, :], PL[:, 0:N_EXP], br[:, :], ALU.add).then_inc(q["r_logit"], 1)
            dve.wait_ge(q["r_lg"], NT)
            nc.vector.tensor_tensor(L[:, NT - 1, :], PL[:, 0:N_EXP], br[:, :], ALU.add).then_inc(q["r_logit"], 1)
            dve.wait_ge(q["r_logit"], NT)
            for i in range(NT):
                row = L[:, i, :]
                other = row[:, None, :].broadcast_to([P, N_EXP, N_EXP])
                own = row[:, :, None].broadcast_to([P, N_EXP, N_EXP])
                nc.vector.tensor_tensor(cmp1[:, :, :], other, own, ALU.is_gt)
                link(nc.vector.tensor_tensor(cmp2[:, :, :], other, own, ALU.is_equal))
                link(nc.vector.tensor_tensor(cmp2[:, :, :], cmp2[:, :, :], lower[:, :, :], ALU.mult))
                link(nc.vector.tensor_tensor(cmp1[:, :, :], cmp1[:, :, :], cmp2[:, :, :], ALU.add))
                link(nc.vector.tensor_reduce(rank[:, i, :], cmp1[:, :, :], AX.X, ALU.add))
            nc.vector.tensor_scalar(sel[:, :, :], rank[:, :, :], TOP_K - 0.5, None, ALU.is_lt).then_inc(q["r_sel"], 1)
            link(nc.vector.tensor_reduce(mx[:, :], L[:, :, :], AX.X, ALU.max))
            nc.vector.tensor_tensor(G[:, :, :], L[:, :, :], mx[:, :, None].broadcast_to([P, NT, N_EXP]),
                                    ALU.subtract).then_inc(q["r_mxn"], 1)
            dve.wait_ge(q["r_exp"], 1)
            dve.wait_ge(q["r_sel"], 1)
            link(nc.vector.tensor_tensor(G[:, :, :], G[:, :, :], sel[:, :, :], ALU.mult))
            link(nc.vector.tensor_reduce(den[:, :], G[:, :, :], AX.X, ALU.add))
            link(nc.vector.reciprocal(den[:, :], den[:, :]))
            link(nc.vector.tensor_tensor(G[:, :, :], G[:, :, :], den[:, :, None].broadcast_to([P, NT, N_EXP]), ALU.mult))
            dve.wait_ge(q["r_pos"], 1)
            dve.wait_ge(q["r_pool"], 4)
            link(nc.vector.tensor_copy(posi[:, :, :], PC[:, 0:NT * N_EXP].rearrange("p (t e) -> p t e", e=N_EXP)))
            link(nc.vector.tensor_scalar(posk[:, :, :], posi[:, :, :], 7, None, ALU.logical_shift_right))
            link(nc.vector.tensor_scalar(posi[:, :, :], posi[:, :, :], P - 1, None, ALU.bitwise_and))
            link(nc.vector.tensor_copy(poskf[:, :, :], posk[:, :, :]))
            link(nc.vector.tensor_copy(posf[:, :, :], posi[:, :, :]))
            link(nc.vector.scalar_tensor_tensor(out=posf[:, :, :], in0=posf[:, :, :], scalar=float(N_SLOTS),
                                                in1=poskf[:, :, :], op0=ALU.mult, op1=ALU.add))
            link(nc.vector.tensor_tensor(posf[:, :, :], posf[:, :, :], ecol[:, None, :].broadcast_to([P, NT, N_EXP]),
                                         ALU.add))
            for j in range(TOP_K):
                link(nc.vector.tensor_scalar(pick[:, :, :], rank[:, :, :], float(j), None, ALU.is_equal))
                link(nc.vector.tensor_tensor(poskf[:, :, :], pick[:, :, :], posf[:, :, :], ALU.mult))
                link(nc.vector.tensor_reduce(dst[:, j, :], poskf[:, :, :], AX.X, ALU.add))
                link(nc.vector.tensor_tensor(poskf[:, :, :], pick[:, :, :], G[:, :, :], ALU.mult))
                link(nc.vector.tensor_reduce(gsel[:, j, :], poskf[:, :, :], AX.X, ALU.add))
                link(nc.vector.tensor_copy(entry[:, j, :, 0], tok[:, :]))
                link(nc.vector.tensor_copy(entry[:, j, :, 1].bitcast(F32), gsel[:, j, :]))
            nc.vector.tensor_copy(dsti[:, :, :], dst[:, :, :]).then_inc(q["r_ent"], 1)
            dve.wait_ge(q["r_pos"], 2)
            nc.vector.tensor_copy(T["counts"][:, :], PL[0:1, 0:N_EXP]).then_inc(q["r_cnt"], 1)
            dve.wait_ge(q["r_cnt"], 1)

        @block.gpsimd
        def _(pool):
            nc.gpsimd.memset(zero[:, :], 0.0).then_inc(q["r_pool"], 1)
            nc.gpsimd.memset(ones[:, :], 1.0).then_inc(q["r_pool"], 1)
            nc.gpsimd.iota(tok[:, :], pattern=[[P, NT]], base=0, channel_multiplier=1).then_inc(q["r_pool"], 1)
            nc.gpsimd.iota(ecol[:, :], pattern=[[LIST_K, N_EXP]], base=0, channel_multiplier=0,
                           allow_small_or_imprecise_dtypes=True).then_inc(q["r_pool"], 1)
            nc.gpsimd.memset(padlist[:, :, 1].bitcast(F32), 0.0).then_inc(q["r_pool"], 1)
            nc.gpsimd.iota(padlist[:, :, 0], pattern=[[0, N_SLOTS]], base=S, channel_multiplier=1).then_inc(q["r_pool"], 1)
            pool.wait_ge(q["r_pool"], 6)
            nc.gpsimd.dma_start(T["token_list"], padlist[:, :, :]).then_inc(q["r_padst"], 16)
            nc.gpsimd.dma_start(T["out"][S:S + PAD_ROWS, :], zero[:, :]).then_inc(q["r_st_x0"], 16)
            nc.gpsimd.dma_start(T["h_rows"][S:S + PAD_ROWS, :], zero[:, :]).then_inc(q["r_st_h0"], 16)
            pool.wait_ge(q["r_padst"], 16)
            pool.wait_ge(q["r_ent"], 1)
            for j in range(TOP_K):
                for i in range(NT):
                    nc.gpsimd.indirect_dma_start(
                        out=T["token_list"].rearrange("p s c -> (p s) c"),
                        out_offset=bass.IndirectOffsetOnAxis(ap=dsti[:, j, i:i + 1], axis=0),
                        in_=entry[:, j, i, :], in_offset=None).then_inc(q["r_scat"], 16)
            pool.wait_ge(q["r_scat"], 16 * TOP_K * NT)
            nc.gpsimd.dma_start(T["slots"][:, :, :], T["token_list"]).then_inc(q["r_back"], 16)
            pool.wait_ge(q["r_back"], 16)
            pool.wait_ge(q["r_st_x0"], 16)
            pool.wait_ge(q["r_st_h0"], 16)


def expert_phase(nc, T):
    with ExitStack() as ctx:
        sb = lambda n, s, dt=F32: ctx.enter_context(nc.sbuf_tensor(n, s, dt))
        pb = lambda n, s: ctx.enter_context(nc.psum_tensor(n, s, F32))
        w1 = [sb(f"w1_{n}", [P, DC, BANK]) for n in range(4)]
        w2 = [sb(f"w2_{n}", [P, 4, D]) for n in range(2)]
        b1 = sb("b1", [P, 2 * D_FF])
        b2 = sb("b2", [P, D])
        hg = sb("hg", [P, D])
        hT = sb("ehT", [P, DC, P])
        glu = sb("glu", [P, D_FF])
        lin = sb("lin", [P, D_FF])
        sig = sb("sig", [P, D_FF])
        aT = sb("aT", [P, DC, P])
        ysb = sb("ysb", [P, D])
        gate = sb("gate", [P, 1])
        idx_in = sb("idx_in", [P, 1], I32)
        idx_out = sb("idx_out", [P, 1], I32)
        PU = pb("PU", [P, 4, BANK])
        PY = pb("PY", [P, 2, BANK])
        PT = pb("PTe", [P, 2, BANK])
        q = sems(nc, ctx, "e_gathered e_xposed e_hT e_u e_glu e_sig e_act e_aTp e_aT e_yp e_y e_scat e_bias "
                          "e_bias_free e_pool e_held e_dve e_init")
        loaded = sem_list(nc, ctx, [f"e_loaded{j}" for j in range(6)])
        free = sem_list(nc, ctx, [f"e_free{j}" for j in range(6)])
        ORDER = (0, 2, 1, 3)
        block = ctx.enter_context(nc.Block())

        def blocks_of_expert(eng, one_block):
            with eng.Fori(0, N_EXP) as e:
                count = eng.value_load(T["counts"][0:1, bass.ds(e, 1)], min_val=0, max_val=S)
                with eng.If(count > 2 * P):
                    with eng.Fori(2, LIST_K) as k:
                        one_block(e, k, False)
                    eng.nop()
                with eng.If(count > P):
                    one_block(e, 1, False)
                one_block(e, 0, True)

        @block.sync
        def _(sp):
            for j in range(6):
                sp.sem_inc(free[j], 1)
            sp.sem_inc(q["e_bias_free"], 1)
            with sp.Fori(0, N_EXP) as e:
                w1_e = T["moe_w1"][0][bass.ds(e, 1)].rearrange("o (k p) f -> p (o k) f", p=P)
                w2_e = T["moe_w2"][0][bass.ds(e, 1)].rearrange("o (k p) f -> p (o k) f", p=P)
                for j, n in enumerate(ORDER):
                    sp.wait_ge(free[j], e + 1)
                    sp.dma_start(w1[n][:, :, :], w1_e[:, :, n * BANK:(n + 1) * BANK]).then_inc(loaded[j], 16)
                    if j == 0:
                        sp.wait_ge(q["e_bias_free"], e + 1)
                        sp.dma_start(b1[:, :], T["moe_b1"][0][bass.ds(e, 1)].broadcast_to([P, 2 * D_FF])).then_inc(q["e_bias"], 16)
                        sp.dma_start(b2[:, :], T["moe_b2"][0][bass.ds(e, 1)].broadcast_to([P, D])).then_inc(q["e_bias"], 16)
                for n in range(2):
                    sp.wait_ge(free[4 + n], e + 1)
                    sp.dma_start(w2[n][:, :, :], w2_e[:, 4 * n:4 * n + 4, :]).then_inc(loaded[4 + n], 16)

        @block.tensor
        def _(pe):
            done = pe.alloc_register("pe_blocks")
            pe.reg_mov(done, 0)

            def one_block(e, k, last_block):
                nb = pe.snap(done)
                pe.wait_ge(q["e_gathered"], 16 * nb + 16)
                for g in range(2):
                    for c in range(4):
                        last = nc.tensor.transpose(PT[:, g, c * P:(c + 1) * P], hg[:, (4 * g + c) * P:(4 * g + c + 1) * P],
                                                   T["ident"][:, :])
                last.then_inc(q["e_xposed"], 1)
                pe.wait_ge(q["e_hT"], 2 * nb + 2)
                for j, n in enumerate(ORDER):
                    pe.wait_ge(loaded[j], 16 * e + 16)
                    for c in range(DC):
                        last = nc.tensor.matmul(PU[:, n, :], hT[:, c, :], w1[n][:, c, :], start=(c == 0), stop=(c == DC - 1))
                        if c == 0 and j and last_block:
                            last.then_inc(free[j - 1], 1)
                    last.then_inc(q["e_u"], 1)
                for g in range(2):
                    pe.wait_ge(q["e_act"], 2 * nb + g + 1)
                    for c in range(4):
                        last = nc.tensor.transpose(PT[:, g, c * P:(c + 1) * P], lin[:, (4 * g + c) * P:(4 * g + c + 1) * P],
                                                   T["ident"][:, :])
                        if c == 0 and last_block:
                            last.then_inc(free[3 + g], 1)
                    last.then_inc(q["e_aTp"], 1)
                    pe.wait_ge(q["e_aT"], 2 * nb + g + 1)
                    pe.wait_ge(loaded[4 + g], 16 * e + 16)
                    if g == 0:
                        pe.wait_ge(q["e_y"], nb + 1)
                    for n in range(2):
                        for c in range(4):
                            last = nc.tensor.matmul(PY[:, n, :], aT[:, 4 * g + c, :], w2[g][:, c, n * BANK:(n + 1) * BANK],
                                                    start=(g == 0 and c == 0), stop=(g == 1 and c == 3))
                    if g == 1:
                        last.then_inc(q["e_yp"], 1)
                pe.reg_add(done, done, 1)

            blocks_of_expert(pe, one_block)

        @block.scalar
        def _(act):
            done = act.alloc_register("act_blocks")
            act.reg_mov(done, 0)

            def one_block(e, k, last_block):
                nb = act.snap(done)
                act.wait_ge(q["e_xposed"], nb + 2)
                for g in range(2):
                    nc.scalar.activation(hT[:, 4 * g:4 * g + 4, :], PT[:, g, :].rearrange("p (a b) -> p a b", b=P),
                                         ACT.Copy).then_inc(q["e_hT"], 1)
                for g in range(2):
                    half = slice(g * BANK, (g + 1) * BANK)
                    act.wait_ge(q["e_glu"], 2 * nb + g + 1)
                    nc.scalar.activation(sig[:, half], glu[:, half], ACT.Sigmoid, scale=ALPHA).then_inc(q["e_sig"], 1)
                    act.wait_ge(q["e_aTp"], 2 * nb + g + 1)
                    nc.scalar.activation(aT[:, 4 * g:4 * g + 4, :], PT[:, g, :].rearrange("p (a b) -> p a b", b=P),
                                         ACT.Copy).then_inc(q["e_aT"], 1)
                act.reg_add(done, done, 1)

            blocks_of_expert(act, one_block)

        @block.vector
        def _(dve):
            done = dve.alloc_register("dve_blocks")
            dve.reg_mov(done, 0)
            LINKS = 13

            def one_block(e, k, last_block):
                nb = dve.snap(done)
                count = [0]

                def link(ins):
                    count[0] += 1
                    ins.then_inc(q["e_dve"], 1)
                    dve.wait_ge(q["e_dve"], LINKS * nb + count[0])

                slot = e * LIST_K + k
                link(nc.vector.tensor_copy(gate[:, :], T["slots"][:, bass.ds(slot, 1), 1].bitcast(F32)))
                dve.wait_ge(q["e_bias"], 32 * e + 32)
                for g in range(2):
                    half = slice(g * BANK, (g + 1) * BANK)
                    upper = slice(D_FF + g * BANK, D_FF + (g + 1) * BANK)
                    dve.wait_ge(q["e_u"], 4 * nb + 2 * g + 2)
                    link(nc.vector.tensor_tensor(glu[:, half], PU[:, g, :], b1[:, half], ALU.add))
                    link(nc.vector.tensor_tensor(lin[:, half], PU[:, 2 + g, :], b1[:, upper], ALU.add))
                    nc.vector.tensor_scalar(glu[:, half], glu[:, half], LIMIT, None, ALU.min).then_inc(q["e_glu"], 1)
                    link(nc.vector.tensor_scalar(lin[:, half], lin[:, half], LIMIT, -LIMIT, ALU.min, ALU.max))
                    link(nc.vector.scalar_tensor_tensor(out=lin[:, half], in0=lin[:, half], scalar=1.0, in1=glu[:, half],
                                                        op0=ALU.add, op1=ALU.mult))
                    dve.wait_ge(q["e_sig"], 2 * nb + g + 1)
                    nc.vector.tensor_tensor(lin[:, half], lin[:, half], sig[:, half], ALU.mult).then_inc(q["e_act"], 1)
                dve.wait_ge(q["e_yp"], nb + 1)
                if last_block:
                    dve.sem_inc(free[5], 1)
                dve.wait_ge(q["e_scat"], 16 * nb + 32)
                link(nc.vector.tensor_tensor(ysb[:, :], PY[:, :, :].rearrange("p a b -> p (a b)"), b2[:, :], ALU.add))
                nc.vector.tensor_scalar(ysb[:, :], ysb[:, :], gate[:, 0:1], None, ALU.mult).then_inc(q["e_y"], 1)
                for _ in range(LINKS - count[0] - 1):
                    dve.sem_inc(q["e_dve"], 1)
                dve.wait_ge(q["e_y"], nb + 2)
                dve.sem_inc(q["e_dve"], 1)
                if last_block:
                    dve.sem_inc(q["e_bias_free"], 1)
                dve.reg_add(done, done, 1)

            blocks_of_expert(dve, one_block)

        @block.gpsimd
        def _(pool):
            done = pool.alloc_register("pool_blocks")
            pool.reg_mov(done, 0)
            nc.gpsimd.memset(ysb[:, :], 0.0).then_inc(q["e_y"], 1)
            nc.gpsimd.iota(idx_in[:, :], pattern=[[0, 1]], base=S, channel_multiplier=1).then_inc(q["e_init"], 1)
            nc.gpsimd.iota(idx_out[:, :], pattern=[[0, 1]], base=S, channel_multiplier=1).then_inc(q["e_init"], 1)
            pool.wait_ge(q["e_init"], 2)
            pool.wait_ge(q["e_y"], 1)
            pool.sem_inc(q["e_xposed"], 1)

            def hold(sem, value):
                pool.wait_ge(sem, value)
                pool.sem_inc(q["e_held"], 1)

            def add_rows():
                nc.gpsimd.indirect_dma_start(
                    out=T["out"], out_offset=bass.IndirectOffsetOnAxis(ap=idx_out[:, 0:1], axis=0),
                    in_=ysb[:, :], in_offset=None, compute_op=ALU.add).then_inc(q["e_scat"], 16)

            add_rows()

            def one_block(e, k, last_block):
                nb = pool.snap(done)
                hold(q["e_xposed"], nb + 1)
                hold(q["e_scat"], 16 * nb + 16)
                nc.gpsimd.tensor_copy(idx_out[:, :], idx_in[:, :]).then_inc(q["e_pool"], 1)
                hold(q["e_pool"], 2 * nb + 1)
                slot = e * LIST_K + k
                nc.gpsimd.tensor_copy(idx_in[:, :], T["slots"][:, bass.ds(slot, 1), 0]).then_inc(q["e_pool"], 1)
                hold(q["e_pool"], 2 * nb + 2)
                nc.gpsimd.indirect_dma_start(
                    out=hg[:, :], out_offset=None, in_=T["h_rows"],
                    in_offset=bass.IndirectOffsetOnAxis(ap=idx_in[:, 0:1], axis=0)).then_inc(q["e_gathered"], 16)
                hold(q["e_y"], nb + 1)
                add_rows()
                pool.reg_add(done, done, 1)

            blocks_of_expert(pool, one_block)
            nb = pool.snap(done)
            hold(q["e_scat"], 16 * nb + 16)
            nc.gpsimd.tensor_copy(idx_out[:, :], idx_in[:, :]).then_inc(q["e_pool"], 1)
            hold(q["e_pool"], 2 * nb + 1)
            hold(q["e_y"], nb + 1)
            add_rows()
            hold(q["e_scat"], 16 * nb + 32)


HD = 64
RW = 512
NSA_COLS = 1304
QH = 8
HEADS12 = 12
N_CMP = 63
CMP_H = 256
SCALE = HD ** -0.5
NEG = -1e30


def norm_phase(nc, T):
    with ExitStack() as ctx:
        sb = lambda n, s, dt=F32: ctx.enter_context(nc.sbuf_tensor(n, s, dt))
        xt = sb("xt", [P, NT, D])
        junk = sb("n_junk", [P, D])
        st = sb("n_st", [P, 2, NT])
        g1 = sb("n_g1", [P, DC])
        PT = ctx.enter_context(nc.psum_tensor("n_PT", [P, 4, BANK], F32))
        q = sems(nc, ctx, "n_c n_ss n_ms n_sq n_rs n_xn n_tp n_ev_a n_ev_d")
        loaded = sem_list(nc, ctx, [f"n_x{i}" for i in range(NT)])
        block = ctx.enter_context(nc.Block())

        @block.sync
        def _(sp):
            for i in range(NT):
                sp.dma_start(xt[:, i, :], T["x"][0, i * P:(i + 1) * P, :]).then_inc(loaded[i], 16)
            sp.dma_start(T["ident"][:, :], T["c_ident"]).then_inc(q["n_c"], 16)
            sp.dma_start(g1[:, :], T["ln1_cols"]).then_inc(q["n_c"], 16)

        @block.scalar
        def _(act):
            for i in range(NT):
                act.wait_ge(loaded[i], 16)
                if i:
                    act.wait_ge(q["n_ss"], i)
                nc.scalar.activation(junk[:, :], xt[:, i, :], ACT.Square, accum_out=st[:, 0, i:i + 1]).then_inc(q["n_ss"], 1)
            act.wait_ge(q["n_ms"], 1)
            nc.scalar.activation(st[:, 1, :], st[:, 1, :], ACT.Sqrt).then_inc(q["n_sq"], 1)
            act.wait_ge(q["n_c"], 32)
            for u in range(1, 2 * DC, 2):
                act.wait_ge(q["n_tp"], u + 1)
                c, half = u // 2, u % 2
                nc.scalar.activation(T["xnT"][:, c, 1 + half * BANK:1 + (half + 1) * BANK], PT[:, u % 4, :], ACT.Copy,
                                     scale=g1[:, c:c + 1]).then_inc(q["n_ev_a"], 1)

        @block.vector
        def _(dve):
            nc.vector.memset(T["xnT"][:, :, 0], 0.0)
            dve.wait_ge(q["n_ss"], NT)
            nc.vector.tensor_scalar(st[:, 1, :], st[:, 0, :], 1.0 / D, EPS, ALU.mult, ALU.add).then_inc(q["n_ms"], 1)
            dve.wait_ge(q["n_sq"], 1)
            nc.vector.reciprocal(st[:, 0, :], st[:, 1, :]).then_inc(q["n_rs"], 1)
            dve.wait_ge(q["n_rs"], 1)
            for i in range(NT):
                nc.vector.tensor_scalar(xt[:, i, :], xt[:, i, :], st[:, 0, i:i + 1], None, ALU.mult).then_inc(q["n_xn"], 1)
            dve.wait_ge(q["n_c"], 32)
            for u in range(0, 2 * DC, 2):
                dve.wait_ge(q["n_tp"], u + 1)
                c = u // 2
                nc.vector.tensor_scalar(T["xnT"][:, c, 1:1 + BANK], PT[:, u % 4, :], g1[:, c:c + 1], None,
                                        ALU.mult).then_inc(q["n_ev_d"], 1)

        @block.tensor
        def _(pe):
            pe.wait_ge(q["n_c"], 32)
            for u in range(2 * DC):
                c, half = u // 2, u % 2
                pe.wait_ge(q["n_xn"], 4 * half + 4 if u < 2 else NT)
                if u >= 4:
                    pe.wait_ge(q["n_ev_a"] if u % 2 else q["n_ev_d"], (u - 4) // 2 + 1)
                for t in range(4):
                    i = 4 * half + t
                    last = nc.tensor.transpose(PT[:, u % 4, t * P:(t + 1) * P], xt[:, i, c * P:(c + 1) * P], T["ident"][:, :])
                last.then_inc(q["n_tp"], 1)


def nsa_project_phase(nc, T, N):
    with ExitStack() as ctx:
        sb = lambda n, s, dt=F32: ctx.enter_context(nc.sbuf_tensor(n, s, dt))
        pb = lambda n, s: ctx.enter_context(nc.psum_tensor(n, s, F32))
        W = sb("p_W", [P, DC, NSA_COLS])
        heads = sb("p_heads", [P, 2, HEADS12, HD])
        rot = sb("p_rot", [P, 2, HEADS12, HD])
        tmp = sb("p_tmp", [P, HEADS12, HD])
        cmp_in = sb("p_cmpin", [P, 2, 4, 2, HD])
        rotk = sb("p_rotk", [P, 2, 4, 2, HD])
        rs = sb("p_rs", [P, 2, HEADS12])
        ms = sb("p_ms", [P, 2, HEADS12])
        gain = sb("p_gain", [P, 3, HD])
        cos = sb("p_cos", [P, NT, HD // 2])
        sin = sb("p_sin", [P, NT, HD // 2])
        PP = pb("p_PP", [P, 3, BANK])
        PT = pb("p_PT", [P, 4, BANK])
        q = sems(nc, ctx, "p_w p_c p_mm p_eva p_evd p_sum p_sq p_dve p_n p_r p_tp p_out p_gate p_gl")
        block = ctx.enter_context(nc.Block())
        c0 = 3 * RW
        bounds = ((0, 512), (512, 1024), (1024, NSA_COLS))

        @block.sync
        def _(sp):
            for k in range(DC):
                sp.dma_start(W[:, k, :], T["w_in"][0, k * P:(k + 1) * P, c0:c0 + NSA_COLS]).then_inc(q["p_w"], 16)
            sp.dma_start(gain[:, 0, :], T["nsa_qn_g"].broadcast_to([P, HD])).then_inc(q["p_c"], 16)
            for j in (1, 2):
                sp.dma_start(gain[:, j, :], T["nsa_kn_g"][0, j:j + 1, :].broadcast_to([P, HD])).then_inc(q["p_c"], 16)
            sp.dma_start(cos[:, :, :], T["c_cos"].rearrange("(t p) k -> p t k", p=P)).then_inc(q["p_c"], 16)
            sp.dma_start(sin[:, :, :], T["c_sin"].rearrange("(t p) k -> p t k", p=P)).then_inc(q["p_c"], 16)

        @block.tensor
        def _(pe):
            def project(i):
                if i == 0:
                    pe.wait_ge(q["p_w"], 16 * DC)
                else:
                    pe.wait_ge(q["p_eva"], i)
                    pe.wait_ge(q["p_evd"], i)
                for n, (a, b) in enumerate(bounds):
                    for k in range(DC):
                        last = nc.tensor.matmul(PP[:, n, 0:b - a], T["xnT"][:, k, 1 + i * P:1 + (i + 1) * P], W[:, k, a:b],
                                                start=(k == 0), stop=(k == DC - 1))
                last.then_inc(q["p_mm"], 1)

            def transposes(i):
                s = i % 2
                pe.wait_ge(q["p_n"], i + 1)
                pe.wait_ge(q["p_r"], i + 1)
                pe.wait_ge(q["p_eva"], i + 1)
                if i:
                    pe.wait_ge(q["p_out"], 5 * i)
                twice = lambda v: v.rearrange("p a b -> p (a b)")
                for p in range(4):
                    nc.tensor.transpose(PT[:, 0, p * P:(p + 1) * P],
                                        heads[:, s, 2 * p:2 * p + 2, :].rearrange("p a b -> p (a b)"), T["ident"][:, :])
                    nc.tensor.transpose(PT[:, 1, p * P:(p + 1) * P],
                                        rot[:, s, 2 * p:2 * p + 2, :].rearrange("p a b -> p (a b)"), T["ident"][:, :])
                    nc.tensor.transpose(PT[:, 2, p * P:(p + 1) * P], twice(rotk[:, s, p, :, :]), T["ident"][:, :])
                    last = nc.tensor.transpose(PT[:, 3, p * P:(p + 1) * P],
                                               twice(cmp_in[:, s, p, :, :]), T["ident"][:, :])
                last.then_inc(q["p_tp"], 1)

            project(0)
            for i in range(NT):
                if i + 1 < NT:
                    project(i + 1)
                transposes(i)

        @block.scalar
        def _(act):
            for i in range(NT):
                s = i % 2
                act.wait_ge(q["p_mm"], i + 1)
                if i >= 2:
                    act.wait_ge(q["p_tp"], i - 1)
                for c in range(2):
                    nc.scalar.activation(cmp_in[:, s, :, c, :], PP[:, 1, 0:256].rearrange("p (a b) -> p a b", b=HD), ACT.Copy)
                nc.scalar.activation(heads[:, s, 8:10, :].rearrange("p a b -> p (a b)"), PP[:, 1, 256:384], ACT.Copy)
                nc.scalar.activation(heads[:, s, 10:12, :].rearrange("p a b -> p (a b)"), PP[:, 2, 0:128], ACT.Copy)
                nc.scalar.activation(N["vs"][:, i, :], PP[:, 1, 384:512], ACT.Copy)
                nc.scalar.activation(N["vw"][:, i, :], PP[:, 2, 128:256], ACT.Copy)
                nc.scalar.activation(N["gates"][:, i, :], PP[:, 2, 256:280], ACT.Copy).then_inc(q["p_eva"], 1)
                act.wait_ge(q["p_sum"], i + 1)
                nc.scalar.activation(rs[:, s, :], ms[:, s, :], ACT.Sqrt).then_inc(q["p_sq"], 1)
                act.wait_ge(q["p_tp"], i + 1)
                tok = slice(i * P, (i + 1) * P)
                view = lambda g: PT[:, g, :].rearrange("p (a b) -> p a b", b=P)
                nc.scalar.activation(N["qT"][:, :, tok], view(0), ACT.Copy).then_inc(q["p_out"], 1)
                nc.scalar.activation(N["qrT"][:, :, tok], view(1), ACT.Copy).then_inc(q["p_out"], 1)
                nc.scalar.activation(N["kT"][:, :, tok], view(2), ACT.Copy).then_inc(q["p_out"], 1)
                nc.scalar.activation(N["cT"][0:HD, :, 1 + i * P:1 + (i + 1) * P], PT[0:HD, 3, :].rearrange("p (a b) -> p a b", b=P),
                                     ACT.Copy).then_inc(q["p_out"], 1)
                nc.scalar.activation(N["cT"][HD:P, :, i * P:(i + 1) * P], PT[HD:P, 3, :].rearrange("p (a b) -> p a b", b=P),
                                     ACT.Copy).then_inc(q["p_out"], 1)
            act.wait_ge(q["p_eva"], NT)
            nc.scalar.activation(N["gates"][:, :, :], N["gates"][:, :, :], ACT.Sigmoid)

        @block.vector
        def _(dve):
            link = chained(dve, q["p_dve"])
            dve.wait_ge(q["p_c"], 16 * 5)
            for i in range(NT):
                s = i % 2
                H = heads[:, s, :, :]
                dve.wait_ge(q["p_mm"], i + 1)
                if i >= 2:
                    dve.wait_ge(q["p_tp"], i - 1)
                nc.vector.tensor_copy(heads[:, s, 0:8, :].rearrange("p a b -> p (a b)"), PP[:, 0, :]).then_inc(q["p_evd"], 1)
                dve.wait_ge(q["p_evd"], i + 1)
                dve.wait_ge(q["p_eva"], i + 1)
                link(nc.vector.tensor_tensor(tmp[:, :, :], H, H, ALU.mult))
                link(nc.vector.tensor_reduce(ms[:, s, :], tmp[:, :, :], AX.X, ALU.add))
                nc.vector.tensor_scalar(ms[:, s, :], ms[:, s, :], 1.0 / HD, EPS, ALU.mult, ALU.add).then_inc(q["p_sum"], 1)
                dve.wait_ge(q["p_sq"], i + 1)
                link(nc.vector.reciprocal(rs[:, s, :], rs[:, s, :]))
                link(nc.vector.tensor_tensor(H, H, rs[:, s, :, None].broadcast_to([P, HEADS12, HD]), ALU.mult))
                for j, (a, b) in enumerate(((0, QH), (QH, QH + 2), (QH + 2, HEADS12))):
                    last = nc.vector.tensor_tensor(H[:, a:b, :], H[:, a:b, :], gain[:, j, None, :].broadcast_to([P, b - a, HD]),
                                                   ALU.mult)
                last.then_inc(q["p_n"], 1)
                dve.wait_ge(q["p_n"], i + 1)
                half = HD // 2
                lo, hi = H[:, :, 0:half], H[:, :, half:HD]
                cs = cos[:, i, None, :].broadcast_to([P, HEADS12, half])
                sn = sin[:, i, None, :].broadcast_to([P, HEADS12, half])
                R = rot[:, s, :, :]
                link(nc.vector.tensor_tensor(tmp[:, :, 0:half], hi, sn, ALU.mult))
                link(nc.vector.tensor_tensor(tmp[:, :, half:HD], lo, sn, ALU.mult))
                link(nc.vector.tensor_tensor(R[:, :, 0:half], lo, cs, ALU.mult))
                link(nc.vector.tensor_tensor(R[:, :, half:HD], hi, cs, ALU.mult))
                link(nc.vector.tensor_tensor(R[:, :, 0:half], R[:, :, 0:half], tmp[:, :, 0:half], ALU.subtract))
                link(nc.vector.tensor_tensor(R[:, :, half:HD], R[:, :, half:HD], tmp[:, :, half:HD], ALU.add))
                nc.vector.tensor_copy(rotk[:, s, :, 0, :], R[:, QH:HEADS12, :])
                nc.vector.tensor_copy(rotk[:, s, :, 1, :], R[:, QH:HEADS12, :]).then_inc(q["p_r"], 1)
                dve.wait_ge(q["p_r"], i + 1)


def compress_phase(nc, T, N):
    with ExitStack() as ctx:
        sb = lambda n, s, dt=F32: ctx.enter_context(nc.sbuf_tensor(n, s, dt))
        pb = lambda n, s: ctx.enter_context(nc.psum_tensor(n, s, F32))
        W1 = sb("c_W1", [P, 2, 16, CMP_H])
        W2 = sb("c_W2", [P, 2, 2, HD])
        pe_rows = sb("c_pe", [32, P])
        peT = sb("c_peT", [P, 32])
        bias = sb("c_bias", [P, 4])
        hid = sb("c_hid", [P, 4, 2 * N_CMP])
        kg = sb("c_kg", [N_CMP, HD])
        kc = sb("c_kc", [N_CMP, 2, HD])
        kc2 = sb("c_kc2", [N_CMP, 2, 2, HD])
        tmp = sb("c_tmp", [N_CMP, 2, HD])
        ms = sb("c_ms", [N_CMP, 2])
        PH = pb("c_PH", [P, 4, BANK])
        PB = pb("c_PB", [P, BANK])
        PO = pb("c_PO", [P, BANK])
        PT = pb("c_PT", [P, BANK])
        q = sems(nc, ctx, "c_w c_pet c_pete c_b c_be c_h c_g c_o c_v c_ms c_sq c_k c_kt c_dve")
        block = ctx.enter_context(nc.Block())

        @block.sync
        def _(sp):
            for i in range(2):
                sp.dma_start(W1[:, i, :, :], T["nsa_cmp_w1"][0, i].rearrange("(m two) d f -> (two d) m f", two=2)).then_inc(q["c_w"], 16)
                sp.dma_start(W2[:, i, :, :], T["nsa_cmp_w2"][0, i].rearrange("(c p) d -> p c d", p=P)).then_inc(q["c_w"], 16)
            sp.dma_start(pe_rows[:, :], T["nsa_pe"][0].rearrange("i (m two) d -> (i m) (two d)", two=2)).then_inc(q["c_w"], 16)
            sp.dma_start(kg[:, :], T["nsa_kn_g"][0, 0:1, :].broadcast_to([N_CMP, HD])).then_inc(q["c_w"], 16)

        @block.tensor
        def _(pe):
            pe.wait_ge(q["c_w"], 16 * 6)
            nc.tensor.transpose(PT[:, 0:32], pe_rows[:, :], T["ident"][0:32, 0:32]).then_inc(q["c_pet"], 1)
            pe.wait_ge(q["c_pete"], 1)
            for i in range(2):
                for f in range(2):
                    u = 2 * i + f
                    for m in range(16):
                        w = W1[:, i, m, f * P:(f + 1) * P]
                        last = nc.tensor.matmul(PB[:, u:u + 1], w, peT[:, 16 * i + m:16 * i + m + 1],
                                                start=(m == 0), stop=(m == 15))
            last.then_inc(q["c_b"], 1)
            for i in range(2):
                for f in range(2):
                    u = 2 * i + f
                    for m in range(16):
                        last = nc.tensor.matmul(PH[:, u, 0:2 * N_CMP], W1[:, i, m, f * P:(f + 1) * P],
                                                N["cT"][:, 2 * i:2 * i + 2, 1 + 2 * m:1 + 2 * m + 16 * (N_CMP - 1) + 1:16],
                                                start=(m == 0), stop=(m == 15))
                    last.then_inc(q["c_h"], 1)
            pe.wait_ge(q["c_g"], 4)
            for i in range(2):
                for h in range(2):
                    u = 2 * i + h
                    for f in range(2):
                        last = nc.tensor.matmul(PO[0:N_CMP, u * HD:(u + 1) * HD],
                                                hid[:, 2 * i + f, h * N_CMP:(h + 1) * N_CMP], W2[:, i, f, :],
                                                start=(f == 0), stop=(f == 1))
            last.then_inc(q["c_o"], 1)
            pe.wait_ge(q["c_k"], 1)
            for h in range(2):
                last = nc.tensor.transpose(PT[:, BANK // 2 + h * N_CMP:BANK // 2 + (h + 1) * N_CMP],
                                           kc2[:, h, :, :].rearrange("p a b -> p (a b)"), T["ident"][0:N_CMP, 0:N_CMP])
            last.then_inc(q["c_kt"], 1)

        @block.scalar
        def _(act):
            act.wait_ge(q["c_be"], 1)
            for u in range(4):
                act.wait_ge(q["c_h"], u + 1)
                nc.scalar.activation(hid[:, u, :], PH[:, u, 0:2 * N_CMP], ACT.Gelu_apprx_tanh,
                                     bias=bias[:, u:u + 1]).then_inc(q["c_g"], 1)
            act.wait_ge(q["c_ms"], 1)
            nc.scalar.activation(ms[:, :], ms[:, :], ACT.Sqrt).then_inc(q["c_sq"], 1)

        @block.vector
        def _(dve):
            link = chained(dve, q["c_dve"])
            dve.wait_ge(q["c_pet"], 1)
            nc.vector.tensor_copy(peT[:, :], PT[:, 0:32]).then_inc(q["c_pete"], 1)
            dve.wait_ge(q["c_b"], 1)
            nc.vector.tensor_copy(bias[:, :], PB[:, 0:4]).then_inc(q["c_be"], 1)
            dve.wait_ge(q["c_o"], 1)
            link(nc.vector.tensor_copy(kc[:, :, :], PO[0:N_CMP, 0:2 * HD].rearrange("p (a b) -> p a b", b=HD)))
            nc.vector.tensor_copy(N["vcmp"][:, :, :], PO[0:N_CMP, 2 * HD:4 * HD].rearrange("p (a b) -> p a b", b=HD))
            link(nc.vector.tensor_tensor(tmp[:, :, :], kc[:, :, :], kc[:, :, :], ALU.mult))
            link(nc.vector.tensor_reduce(ms[:, :], tmp[:, :, :], AX.X, ALU.add))
            nc.vector.tensor_scalar(ms[:, :], ms[:, :], 1.0 / HD, EPS, ALU.mult, ALU.add).then_inc(q["c_ms"], 1)
            dve.wait_ge(q["c_sq"], 1)
            link(nc.vector.reciprocal(ms[:, :], ms[:, :]))
            link(nc.vector.tensor_tensor(kc[:, :, :], kc[:, :, :], ms[:, :, None].broadcast_to([N_CMP, 2, HD]), ALU.mult))
            for c in range(2):
                last = nc.vector.tensor_tensor(kc2[:, :, c, :], kc[:, :, :], kg[:, None, :].broadcast_to([N_CMP, 2, HD]),
                                               ALU.mult)
            last.then_inc(q["c_k"], 1)
            dve.wait_ge(q["c_kt"], 1)
            nc.vector.tensor_copy(N["kcT"][:, :, :], PT[:, BANK // 2:BANK // 2 + 2 * N_CMP].rearrange("p (a b) -> p a b", b=N_CMP))


def attention_phase(nc, T, N):
    KW = S + 3 * P
    with ExitStack() as ctx:
        sb = lambda n, s, dt=F32: ctx.enter_context(nc.sbuf_tensor(n, s, dt))
        pb = lambda n, s: ctx.enter_context(nc.psum_tensor(n, s, F32))
        cmask = sb("a_cmask", [P, NT, N_CMP])
        cpen = sb("a_cpen", [P, NT, N_CMP])
        wpen = sb("a_wpen", [P, 3 * P])
        free16 = sb("a_free", [P, NT, 16])
        force16 = sb("a_force", [P, NT, 16])
        lower16 = sb("a_lower", [P, 16, 16])
        sc = sb("a_sc", [P, 4, N_CMP])
        pc = sb("a_pc", [P, 4, N_CMP])
        pcT = sb("a_pcT", [N_CMP, 4, P])
        small = sb("a_small", [P, 4, 4])
        ps = sb("a_ps", [P, 65])
        imp = sb("a_imp", [P, 16])
        c1 = sb("a_c1", [P, 16, 16])
        c2 = sb("a_c2", [P, 16, 16])
        bpen = sb("a_bpen", [P, 16])
        pen = sb("a_pen", [P, S])
        Sc = sb("a_S", [P, 2, KW])
        pT = sb("a_pT", [P, 2, 11, P])
        mm = sb("a_mm", [P, 2, 2])
        nm = sb("a_nm", [P, 2, 2])
        dn = sb("a_dn", [P, 2, 2])
        rd = sb("a_rd", [P, 2, 2])
        oN = sb("a_oN", [P, 2, QH, HD])
        gsc = sb("a_gsc", [P, 2, 2])
        PSel = pb("a_PSel", [P, 3, BANK])
        PC = pb("a_PC", [P, BANK])
        PT = pb("a_PT", [P, 2, BANK])
        POc = pb("a_POc", [P, BANK])
        PO = pb("a_PO", [P, BANK])
        q = sems(nc, ctx, "a_c a_cs a_csd a_cm a_ce a_cp a_ct a_cte a_co a_pen a_sp a_sd a_m a_e a_tp a_te a_tea a_ted a_po "
                          "a_pod a_od a_oT a_oTe a_dve a_half")
        block = ctx.enter_context(nc.Block())
        steps = [(i, kv) for i in range(NT) for kv in range(2)]

        def banks_of(i):
            tiles = [(j, S * 0 + j) for j in range(i + 1)]
            wins = [j for j in range(max(0, i - 2), i + 1)]
            cols = [("s", j, j * P) for j, _ in tiles] + [("w", j, S + (j - i + 2) * P) for j in wins]
            return [cols[a:a + 4] for a in range(0, len(cols), 4)]

        heads = [(i, kv, g) for i, kv in steps for g in range(4)]
        group_base = {}
        n = 0
        for u, (i, kv, g) in enumerate(heads):
            group_base[u] = n
            n += len(banks_of(i))

        @block.sync
        def _(sp):
            for dst, src in ((cmask, T["c_cmask"]), (cpen, T["c_cpen"]), (free16, T["c_free"]), (force16, T["c_force"])):
                sp.dma_start(dst[:, :, :], src.rearrange("(t p) n -> p t n", p=P)).then_inc(q["a_c"], 16)
            sp.dma_start(wpen[:, :], T["c_wpen"]).then_inc(q["a_c"], 16)
            sp.dma_start(lower16[:, :, :].rearrange("p a b -> p (a b)"), T["c_lower16"].broadcast_to([P, 256])).then_inc(q["a_c"], 16)

        @block.tensor
        def _(pe):
            def cmp_scores(s):
                i, kv = steps[s]
                if s:
                    pe.wait_ge(q["a_csd"], s)
                for g in (0, 2, 1, 3):
                    h = 4 * kv + g
                    r = slice(HD * (h % 2), HD * (h % 2) + HD)
                    if g == 1:
                        last.then_inc(q["a_half"], 1)
                        pe.wait_ge(q["a_half"], s + 1)
                    last = nc.tensor.matmul(PC[:, g * HD:g * HD + N_CMP], N["qT"][r, h // 2, i * P:(i + 1) * P],
                                            N["kcT"][r, kv, :], start=True, stop=True)
                last.then_inc(q["a_cs"], 1)

            def cmp_out(s):
                i, kv = steps[s]
                pe.wait_ge(q["a_cp"], s + 1)
                for g in range(4):
                    last = nc.tensor.transpose(POc[0:N_CMP, g * P:(g + 1) * P], pc[:, g, :], T["ident"][:, :])
                last.then_inc(q["a_ct"], 1)
                pe.wait_ge(q["a_cte"], s + 1)
                for g in range(4):
                    last = nc.tensor.matmul(PC[:, 256 + g * HD:256 + (g + 1) * HD], pcT[:, g, :], N["vcmp"][:, kv, :],
                                            start=True, stop=True)
                last.then_inc(q["a_co"], 1)

            def scores(u):
                i, kv, g = heads[u]
                h = 4 * kv + g
                r = slice(HD * (h % 2), HD * (h % 2) + HD)
                if u:
                    pe.wait_ge(q["a_sd"], u)
                lhs = N["qrT"][r, h // 2, i * P:(i + 1) * P]
                for b in range(0, (i + 1) * P, BANK):
                    n = min(BANK, (i + 1) * P - b)
                    nc.tensor.matmul(PSel[:, b // BANK, 0:n], lhs, N["kT"][r, kv, b:b + n], start=True, stop=True)
                lo = max(0, i - 2)
                last = nc.tensor.matmul(PSel[:, 2, (lo - i + 2) * P:3 * P], lhs, N["kT"][r, 2 + kv, lo * P:(i + 1) * P],
                                        start=True, stop=True)
                last.then_inc(q["a_sp"], 1)

            def out(u):
                i, kv, g = heads[u]
                groups = banks_of(i)
                pe.wait_ge(q["a_e"], 2 * u + 2)

                def turn(n):
                    at = group_base[u] + n
                    if at >= 2:
                        pe.wait_ge(q["a_tea"] if at % 2 else q["a_ted"], (at - 2) // 2 + 1)
                    for c, (_, _, col) in enumerate(groups[n]):
                        last = nc.tensor.transpose(PT[:, at % 2, c * P:(c + 1) * P], Sc[:, u % 2, col:col + P], T["ident"][:, :])
                    last.then_inc(q["a_tp"], 1)

                for n in range(len(groups)):
                    turn(n)
                if u:
                    pe.wait_ge(q["a_pod"], u)
                total = group_base[u] + len(groups)
                pe.wait_ge(q["a_tea"], total // 2)
                pe.wait_ge(q["a_ted"], (total + 1) // 2)
                flat = [x for grp in groups for x in grp]
                for kind, dst in (("s", 0), ("w", HD)):
                    mine = [(c, j) for c, (k, j, _) in enumerate(flat) if k == kind]
                    for m, (c, j) in enumerate(mine):
                        V = N["vs"] if kind == "s" else N["vw"]
                        last = nc.tensor.matmul(PO[:, dst:dst + HD], pT[:, u % 2, c, :], V[:, j, kv * HD:(kv + 1) * HD],
                                                start=(m == 0), stop=(m == len(mine) - 1))
                last.then_inc(q["a_po"], 1)

            def turn_out(i):
                pe.wait_ge(q["a_od"], i + 1)
                for p in range(4):
                    last = nc.tensor.transpose(POc[:, p * P:(p + 1) * P],
                                               oN[:, i % 2, 2 * p:2 * p + 2, :].rearrange("p a b -> p (a b)"), T["ident"][:, :])
                last.then_inc(q["a_oT"], 1)

            cmp_scores(0)
            cmp_out(0)
            scores(0)
            for s, (i, kv) in enumerate(steps):
                for g in range(4):
                    u = 4 * s + g
                    if g == 2 and s + 1 < len(steps):
                        cmp_scores(s + 1)
                    if g == 3 and s + 1 < len(steps):
                        if s % 2 == 0 and i:
                            pe.wait_ge(q["a_oTe"], i)
                        cmp_out(s + 1)
                    if u + 1 < len(heads):
                        scores(u + 1)
                    out(u)
                if kv == 1:
                    turn_out(i)

        @block.scalar
        def _(act):
            def cmp_exp(s):
                for g in range(4):
                    act.wait_ge(q["a_cm"], s + 1)
                    last = nc.scalar.activation(sc[:, g, :], sc[:, g, :], ACT.Exp, bias=small[:, 1, g:g + 1])
                last.then_inc(q["a_ce"], 1)
                act.wait_ge(q["a_ct"], s + 1)
                nc.scalar.activation(pcT[:, :, :], POc[0:N_CMP, :].rearrange("p (a b) -> p a b", b=P),
                                     ACT.Copy).then_inc(q["a_cte"], 1)

            def exps(u):
                i, kv, g = heads[u]
                b = u % 2
                act.wait_ge(q["a_m"], u + 1)
                nc.scalar.activation(Sc[:, b, 0:(i + 1) * P], Sc[:, b, 0:(i + 1) * P], ACT.Exp, bias=nm[:, b, 0:1],
                                     accum_out=dn[:, b, 0:1]).then_inc(q["a_e"], 1)
                lo = S + (max(0, i - 2) - i + 2) * P
                nc.scalar.activation(Sc[:, b, lo:KW], Sc[:, b, lo:KW], ACT.Exp, bias=nm[:, b, 1:2],
                                     accum_out=dn[:, b, 1:2]).then_inc(q["a_e"], 1)

            def evacs(u):
                i, kv, g = heads[u]
                for n, grp in enumerate(banks_of(i)):
                    at = group_base[u] + n
                    if at % 2:
                        act.wait_ge(q["a_tp"], at + 1)
                        nc.scalar.activation(pT[:, u % 2, 4 * n:4 * n + len(grp), :],
                                             PT[:, at % 2, 0:len(grp) * P].rearrange("p (a b) -> p a b", b=P),
                                             ACT.Copy).then_inc(q["a_tea"], 1)

            cmp_exp(0)
            exps(0)
            for s, (i, kv) in enumerate(steps):
                for g in range(4):
                    u = 4 * s + g
                    if g == 3 and s + 1 < len(steps):
                        cmp_exp(s + 1)
                    evacs(u)
                    if u + 1 < len(heads):
                        exps(u + 1)
                if kv == 1:
                    act.wait_ge(q["a_oT"], i + 1)
                    nc.scalar.activation(T["yT"][:, 4:8, i * P:(i + 1) * P], POc[:, :].rearrange("p (a b) -> p a b", b=P),
                                         ACT.Copy).then_inc(q["a_oTe"], 1)

        @block.vector
        def _(dve):
            link = chained(dve, q["a_dve"])
            dve.wait_ge(q["a_c"], 16 * 6)
            link(nc.vector.memset(ps[:, :], 0.0))

            def cmp_softmax(s):
                i, kv = steps[s]
                dve.wait_ge(q["a_cs"], s + 1)
                view = PC[:, 0:4 * HD].rearrange("p (a b) -> p a b", b=HD)[:, :, 0:N_CMP]
                nc.vector.scalar_tensor_tensor(out=sc[:, :, :], in0=view, scalar=SCALE,
                                               in1=cpen[:, i, None, :].broadcast_to([P, 4, N_CMP]),
                                               op0=ALU.mult, op1=ALU.add).then_inc(q["a_csd"], 1)
                dve.wait_ge(q["a_csd"], s + 1)
                link(nc.vector.tensor_reduce(small[:, 0, :], sc[:, :, :], AX.X, ALU.max))
                nc.vector.tensor_scalar(small[:, 1, :], small[:, 0, :], -1.0, None, ALU.mult).then_inc(q["a_cm"], 1)
                dve.wait_ge(q["a_ce"], s + 1)
                link(nc.vector.tensor_tensor(sc[:, :, :], sc[:, :, :], cmask[:, i, None, :].broadcast_to([P, 4, N_CMP]),
                                             ALU.mult))
                link(nc.vector.tensor_reduce(small[:, 2, :], sc[:, :, :], AX.X, ALU.add))
                link(nc.vector.tensor_scalar(small[:, 2, :], small[:, 2, :], 1e-30, None, ALU.max))
                link(nc.vector.reciprocal(small[:, 3, :], small[:, 2, :]))
                nc.vector.tensor_tensor(pc[:, :, :], sc[:, :, :], small[:, 3, :, None].broadcast_to([P, 4, N_CMP]),
                                        ALU.mult).then_inc(q["a_cp"], 1)
                dve.wait_ge(q["a_cp"], s + 1)

            def select(s):
                i, kv = steps[s]
                keys = (i + 1) * P
                causal = wpen[:, 2 * P:3 * P]
                if i < 4:
                    link(nc.vector.memset(bpen[:, :], 0.0))
                else:
                    link(nc.vector.tensor_reduce(ps[:, 1:64], pc[:, :, :].rearrange("p a b -> p b a"), AX.X, ALU.add))
                    link(nc.vector.tensor_reduce(imp[:, :], ps[:, 0:64].rearrange("p (a b) -> p a b", b=4), AX.X, ALU.add))
                    link(nc.vector.tensor_tensor(imp[:, :], imp[:, :], ps[:, 4:65:4], ALU.add))
                    link(nc.vector.tensor_tensor(imp[:, :], imp[:, :], free16[:, i, :], ALU.mult))
                    link(nc.vector.tensor_tensor(imp[:, :], imp[:, :], force16[:, i, :], ALU.add))
                    other = imp[:, None, :].broadcast_to([P, 16, 16])
                    own = imp[:, :, None].broadcast_to([P, 16, 16])
                    link(nc.vector.tensor_tensor(c1[:, :, :], other, own, ALU.is_gt))
                    link(nc.vector.tensor_tensor(c2[:, :, :], other, own, ALU.is_equal))
                    link(nc.vector.tensor_tensor(c2[:, :, :], c2[:, :, :], lower16[:, :, :], ALU.mult))
                    link(nc.vector.tensor_tensor(c1[:, :, :], c1[:, :, :], c2[:, :, :], ALU.add))
                    link(nc.vector.tensor_reduce(bpen[:, :], c1[:, :, :], AX.X, ALU.add))
                    link(nc.vector.tensor_scalar(bpen[:, :], bpen[:, :], 7.5, NEG, ALU.is_gt, ALU.mult))
                nb = keys // HD
                link(nc.vector.tensor_copy(pen[:, 0:keys].rearrange("p (a b) -> p a b", b=HD),
                                           bpen[:, 0:nb, None].broadcast_to([P, nb, HD])))
                link(nc.vector.tensor_tensor(pen[:, i * P:keys], pen[:, i * P:keys], causal, ALU.add))

            def masked(u):
                i, kv, g = heads[u]
                b = u % 2
                keys = (i + 1) * P
                lo = (max(0, i - 2) - i + 2) * P
                dve.wait_ge(q["a_sp"], u + 1)
                nc.vector.scalar_tensor_tensor(
                    out=Sc[:, b, 0:keys], in0=PSel[:, 0:2, :].rearrange("p a b -> p (a b)")[:, 0:keys], scalar=SCALE,
                    in1=pen[:, 0:keys], op0=ALU.mult, op1=ALU.add)
                nc.vector.scalar_tensor_tensor(out=Sc[:, b, S + lo:KW], in0=PSel[:, 2, lo:3 * P], scalar=SCALE,
                                               in1=wpen[:, lo:3 * P], op0=ALU.mult, op1=ALU.add).then_inc(q["a_sd"], 1)
                dve.wait_ge(q["a_sd"], u + 1)
                nc.vector.tensor_reduce(mm[:, b, 0:1], Sc[:, b, 0:keys], AX.X, ALU.max)
                link(nc.vector.tensor_reduce(mm[:, b, 1:2], Sc[:, b, S + lo:KW], AX.X, ALU.max))
                nc.vector.tensor_scalar(nm[:, b, :], mm[:, b, :], -1.0, None, ALU.mult).then_inc(q["a_m"], 1)

            def evacs(u):
                i, kv, g = heads[u]
                for n, grp in enumerate(banks_of(i)):
                    at = group_base[u] + n
                    if at % 2 == 0:
                        dve.wait_ge(q["a_tp"], at + 1)
                        nc.vector.tensor_copy(pT[:, u % 2, 4 * n:4 * n + len(grp), :],
                                              PT[:, at % 2, 0:len(grp) * P].rearrange("p (a b) -> p a b", b=P)
                                              ).then_inc(q["a_ted"], 1)

            def combine(u):
                i, kv, g = heads[u]
                h = 4 * kv + g
                b = u % 2
                o = oN[:, i % 2, h, :]
                dve.wait_ge(q["a_e"], 2 * u + 2)
                link(nc.vector.reciprocal(rd[:, b, :], dn[:, b, :]))
                link(nc.vector.tensor_tensor(gsc[:, b, :], rd[:, b, :], N["gates"][:, i, 3 * h + 1:3 * h + 3], ALU.mult))
                dve.wait_ge(q["a_po"], u + 1)
                link(nc.vector.scalar_tensor_tensor(out=o, in0=PO[:, 0:HD], scalar=gsc[:, b, 0:1], in1=o,
                                                    op0=ALU.mult, op1=ALU.add))
                nc.vector.scalar_tensor_tensor(out=o, in0=PO[:, HD:2 * HD], scalar=gsc[:, b, 1:2], in1=o,
                                               op0=ALU.mult, op1=ALU.add).then_inc(q["a_pod"], 1)
                dve.wait_ge(q["a_pod"], u + 1)

            def cmp_combine(s):
                i, kv = steps[s]
                dve.wait_ge(q["a_co"], s + 1)
                if i >= 2 and kv == 0:
                    dve.wait_ge(q["a_oT"], i - 1)
                for g in range(4):
                    h = 4 * kv + g
                    last = nc.vector.tensor_scalar(oN[:, i % 2, h, :], PC[:, 256 + g * HD:256 + (g + 1) * HD],
                                                   N["gates"][:, i, 3 * h:3 * h + 1], None, ALU.mult)
                link(last)

            cmp_softmax(0)
            select(0)
            cmp_combine(0)
            masked(0)
            for s, (i, kv) in enumerate(steps):
                for g in range(4):
                    u = 4 * s + g
                    if g == 3 and s + 1 < len(steps):
                        cmp_softmax(s + 1)
                        select(s + 1)
                    if g < 3:
                        masked(u + 1)
                        evacs(u)
                        combine(u)
                    else:
                        if s + 1 < len(steps):
                            masked(u + 1)
                            evacs(u)
                            combine(u)
                            cmp_combine(s + 1)
                        else:
                            evacs(u)
                            combine(u)
                if kv == 1:
                    dve.sem_inc(q["a_od"], 1)


HD = 64
RW = 512
PAIRS = 4
CH = 64
NCH = S // CH
LEVELS = 5
LNX_EPS = 64e-5
E_HALF = float(np.exp(-0.5))
(MU_R, MU_K, MU_V, W0, A0, K_K, K_A, R_K) = range(8)


def lora_phase(nc, T, R):
    with ExitStack() as ctx:
        sb = lambda n, s, dt=F32: ctx.enter_context(nc.sbuf_tensor(n, s, dt))
        wl = sb("l_w", [P, DC, 256])
        wb = sb("l_wb", [P, DC, 256])
        mu = sb("l_mu", [P, 3, DC])
        PH = ctx.enter_context(nc.psum_tensor("l_PH", [P, 4, BANK], F32))
        q = sems(nc, ctx, "l_ld l_d l_m")
        block = ctx.enter_context(nc.Block())
        parts = ((0, 0, 64), (1, 64, 128), (2, 128, 256))

        @block.sync
        def _(sp):
            for (_, a, b), src in zip(parts, (T["rw_w1"], T["rw_a1"], T["rw_g1"])):
                sp.dma_start(wl[:, :, a:b], src[0].rearrange("(k p) f -> p k f", p=P)).then_inc(q["l_ld"], 16)
            sp.dma_start(mu[:, :, :], T["mu_wag_cols"]).then_inc(q["l_ld"], 16)
            sp.dma_start(R["cols"][:, :, :], T["rw_cols"]).then_inc(q["l_ld"], 16)
            sp.dma_start(R["w2a2"][0:64, :], T["rw_w2"][0]).then_inc(q["l_ld"], 16)
            sp.dma_start(R["w2a2"][64:P, :], T["rw_a2"][0]).then_inc(q["l_ld"], 16)
            sp.dma_start(R["g2"][:, :], T["rw_g2"][0]).then_inc(q["l_ld"], 16)
            sp.dma_start(R["lng"][:, :], T["rw_lnx_g"].broadcast_to([P, RW])).then_inc(q["l_ld"], 16)
            sp.dma_start(R["lnb"][:, :], T["rw_lnx_b"].broadcast_to([P, RW])).then_inc(q["l_ld"], 16)
            sp.dma_start(R["masks"][:, :, :], T["c_masks"]).then_inc(q["l_ld"], 16)
            sp.dma_start(R["blockones"][:, :], T["c_blockones"]).then_inc(q["l_ld"], 16)
            sp.dma_start(R["ident2"][:, :], T["c_ident2"]).then_inc(q["l_ld"], 16)

        @block.vector
        def _(dve):
            dve.wait_ge(q["l_ld"], 16 * 13)
            for j, a, b in parts:
                last = nc.vector.tensor_tensor(wb[:, :, a:b], wl[:, :, a:b], mu[:, j, :, None].broadcast_to([P, DC, b - a]),
                                               ALU.mult)
            last.then_inc(q["l_d"], 1)
            dve.wait_ge(q["l_d"], 1)
            nc.vector.tensor_tensor(wl[:, :, :], wl[:, :, :], wb[:, :, :], ALU.subtract).then_inc(q["l_d"], 1)
            nc.vector.tensor_scalar(R["omcols"][:, :, :], R["cols"][:, :, :], -1.0, 1.0, ALU.mult, ALU.add)

        @block.tensor
        def _(pe):
            pe.wait_ge(q["l_d"], 2)
            for m in range(2):
                for n in range(2):
                    for k in range(DC):
                        nc.tensor.matmul(PH[:, 2 * m + n, :], wl[:, k, m * P:(m + 1) * P],
                                         T["xnT"][:, k, 1 + n * BANK:1 + (n + 1) * BANK], start=(k == 0), stop=False)
                        last = nc.tensor.matmul(PH[:, 2 * m + n, :], wb[:, k, m * P:(m + 1) * P],
                                                T["xnT"][:, k, n * BANK:(n + 1) * BANK], start=False, stop=(k == DC - 1))
                last.then_inc(q["l_m"], 1)

        @block.scalar
        def _(act):
            act.wait_ge(q["l_m"], 1)
            hid = PH[:, 0:2, :].rearrange("p a b -> p (a b)")
            nc.scalar.activation(R["hwa"][0:64, :], hid[0:64, :], ACT.Tanh)
            nc.scalar.activation(R["hwa"][64:P, :], hid[64:P, :], ACT.Copy)
            act.wait_ge(q["l_m"], 2)
            nc.scalar.activation(R["hg"][:, :], PH[:, 2:4, :].rearrange("p a b -> p (a b)"), ACT.Sigmoid)


def features_phase(nc, T, R, F, p):
    with ExitStack() as ctx:
        sb = lambda n, s, dt=F32: ctx.enter_context(nc.sbuf_tensor(f"f{p}_{n}", s, dt))
        W = sb("W", [P, DC, 3, P])
        raw = sb("raw", [P, 3, S + 1])
        mix = sb("mix", [P, 3, S])
        tmp = sb("tmp", [P, S])
        kk = sb("kk", [P, S])
        a = sb("a", [P, S])
        dec = sb("dec", [P, S])
        cum = sb("cum", [P, NCH, CH + 1])
        inv = sb("inv", [P, S])
        zero = sb("zero", [P, CH])
        PX = ctx.enter_context(nc.psum_tensor(f"f{p}_PX", [P, 4, 2, BANK], F32))
        q = sems(nc, ctx, "ld mm ev sq ss nrm za sga dec d z", f"f{p}_")
        block = ctx.enter_context(nc.Block())
        col = lambda j: R["cols"][:, p, j:j + 1]
        om = lambda j: R["omcols"][:, p, j:j + 1]
        ch = slice(p * P, (p + 1) * P)
        wide = lambda n: PX[:, n, :, :].rearrange("p a b -> p (a b)")

        @block.sync
        def _(sp):
            for j in range(3):
                sp.dma_start(W[:, :, j, :], T["w_in"][0, :, j * RW + p * P:j * RW + (p + 1) * P]
                             .rearrange("(k p) f -> p k f", p=P)).then_inc(q["ld"], 16)

        @block.tensor
        def _(pe):
            for n in range(2):
                nc.tensor.matmul(PX[:, 0, n, :], R["w2a2"][0:64, ch], R["hwa"][0:64, n * BANK:(n + 1) * BANK], start=True, stop=True)
            for n in range(2):
                last = nc.tensor.matmul(PX[:, 1, n, :], R["w2a2"][64:P, ch], R["hwa"][64:P, n * BANK:(n + 1) * BANK],
                                        start=True, stop=True)
            last.then_inc(q["za"], 1)
            pe.wait_ge(q["ld"], 48)
            for j, bank in ((1, 2), (0, 3), (2, 0)):
                if bank == 0:
                    pe.wait_ge(q["sga"], 2)
                for n in range(2):
                    for k in range(DC):
                        last = nc.tensor.matmul(PX[:, bank, n, :], W[:, k, j, :], T["xnT"][:, k, 1 + n * BANK:1 + (n + 1) * BANK],
                                                start=(k == 0), stop=(k == DC - 1))
                last.then_inc(q["mm"], 1)
            pe.wait_ge(q["sq"], 1)
            for n in range(2):
                last = nc.tensor.matmul(PX[:, 1, n, :], R["blockones"][:, :], tmp[:, n * BANK:(n + 1) * BANK], start=True, stop=True)
            last.then_inc(q["ss"], 1)

        @block.scalar
        def _(act):
            act.wait_ge(q["za"], 1)
            nc.scalar.activation(dec[:, :], wide(0), ACT.Sigmoid, bias=col(W0)).then_inc(q["sga"], 1)
            nc.scalar.activation(a[:, :], wide(1), ACT.Sigmoid, bias=col(A0)).then_inc(q["sga"], 1)
            act.wait_ge(q["sga"], 2)
            nc.scalar.activation(dec[:, :], dec[:, :], ACT.Exp, scale=-E_HALF).then_inc(q["dec"], 1)
            for m, (j, bank) in enumerate(((1, 2), (0, 3), (2, 0))):
                act.wait_ge(q["mm"], m + 1)
                if m == 0:
                    act.wait_ge(q["z"], 1)
                nc.scalar.activation(raw[:, j, 1:S + 1], wide(bank), ACT.Copy).then_inc(q["ev"], 1)
            act.wait_ge(q["ss"], 1)
            nc.scalar.activation(inv[:, :], wide(1), ACT.Sqrt).then_inc(q["nrm"], 1)

        @block.vector
        def _(dve):
            link = chained(dve, q["d"])
            nc.vector.memset(raw[:, :, 0], 0.0)
            nc.vector.memset(cum[:, :, 0], 1.0)
            nc.vector.memset(zero[:, :], 0.0).then_inc(q["z"], 1)
            dve.wait_ge(q["z"], 1)
            dve.wait_ge(q["dec"], 1)
            for c in range(NCH):
                last = nc.vector.tensor_tensor_scan(cum[:, c, 1:CH + 1], dec[:, c * CH:(c + 1) * CH], zero[:, :], 1.0,
                                                    ALU.mult, ALU.add)
            link(last)

            def mixed(j, m):
                dve.wait_ge(q["ev"], m)
                link(nc.vector.tensor_scalar(mix[:, j, :], raw[:, j, 0:S], col(j), None, ALU.mult))
                link(nc.vector.scalar_tensor_tensor(out=mix[:, j, :], in0=raw[:, j, 1:S + 1], scalar=om(j), in1=mix[:, j, :],
                                                    op0=ALU.mult, op1=ALU.add))

            r, k, v = mix[:, 0, :], mix[:, 1, :], mix[:, 2, :]
            cs = cum[:, :, 1:CH + 1]
            prev = cum[:, :, 0:CH]
            by = lambda t: t.rearrange("p (c t) -> p c t", t=CH)
            mixed(1, 1)
            link(nc.vector.tensor_scalar(kk[:, :], k, col(K_K), None, ALU.mult))
            nc.vector.tensor_tensor(tmp[:, :], kk[:, :], kk[:, :], ALU.mult).then_inc(q["sq"], 1)
            mixed(0, 2)
            link(nc.vector.tensor_scalar(F["bonus"][:, :], a[:, :], col(K_A), om(K_A), ALU.mult, ALU.add))
            link(nc.vector.tensor_tensor(k, k, F["bonus"][:, :], ALU.mult))
            link(nc.vector.scalar_tensor_tensor(out=F["bonus"][:, :], in0=r, scalar=col(R_K), in1=k, op0=ALU.mult, op1=ALU.mult))
            link(nc.vector.tensor_tensor(by(F["ar"][:, 1, :]), by(r), cs, ALU.mult))
            dve.wait_ge(q["nrm"], 1)
            link(nc.vector.tensor_scalar(inv[:, :], inv[:, :], 1e-12, None, ALU.max))
            link(nc.vector.reciprocal(inv[:, :], inv[:, :]))
            link(nc.vector.tensor_tensor(kk[:, :], kk[:, :], inv[:, :], ALU.mult))
            link(nc.vector.scalar_tensor_tensor(out=by(F["ar"][:, 0, :]), in0=by(kk[:, :]), scalar=-1.0, in1=prev,
                                                op0=ALU.mult, op1=ALU.mult))
            link(nc.vector.reciprocal(by(inv[:, :]), cs))
            link(nc.vector.tensor_tensor(kk[:, :], kk[:, :], a[:, :], ALU.mult))
            link(nc.vector.tensor_tensor(F["bt"][:, :], kk[:, :], inv[:, :], ALU.mult))
            link(nc.vector.tensor_tensor(F["kt"][:, :], k, inv[:, :], ALU.mult))
            last_c = cum[:, :, CH:CH + 1].broadcast_to([P, NCH, CH])
            link(nc.vector.tensor_tensor(by(F["be"][:, :]), by(F["bt"][:, :]), last_c, ALU.mult))
            link(nc.vector.tensor_tensor(by(F["ke"][:, :]), by(F["kt"][:, :]), last_c, ALU.mult))
            link(nc.vector.tensor_tensor(F["dc"][:, :, :], R["ident2"][:, None, :].broadcast_to([P, NCH, CH]), last_c, ALU.mult))
            mixed(2, 3)
            link(nc.vector.tensor_copy(F["v"][:, :], v))


def chunks_phase(nc, T, R, F, p):
    with ExitStack() as ctx:
        sb = lambda n, s, dt=F32: ctx.enter_context(nc.sbuf_tensor(f"k{p}_{n}", s, dt))
        pb = lambda n, s: ctx.enter_context(nc.psum_tensor(f"k{p}_{n}", s, F32))
        tk = sb("tk", [P, 2, 4, P])
        sc = sb("sc", [P, 4, 4, P])
        mt = sb("mt", [P, LEVELS, 4, P])
        Dm = sb("D", [P, 4, P])
        Dt = sb("Dt", [P, 4, P])
        Ps = sb("Ps", [P, 4, P])
        LV = sb("LV", [P, 4, CH])
        WZ = sb("WZ", [P, 4, 2, CH])
        PS = pb("PS", [P, 4, BANK])
        PT = pb("PT", [P, BANK])
        PP = pb("PP", [P, BANK])
        PD = pb("PD", [P, BANK])
        PE_ = pb("PE", [P, BANK])
        q = sems(nc, ctx, "tt te s m lm d0 p pe dd dm d lv lve w we q qe y ye dtr", f"k{p}_")
        block = ctx.enter_context(nc.Block())
        B = NT // 2
        units = [(t, hh) for t in range(2) for hh in range(2)]
        rows = lambda hh: slice(CH * hh, CH * hh + CH)
        quad = lambda bank: bank.rearrange("p (a b) -> p a b", b=P)

        @block.tensor
        def _(pe):
            for b in range(B):
                for t in range(2):
                    tok = slice((2 * b + t) * P, (2 * b + t + 1) * P)
                    if b or t:
                        pe.wait_ge(q["te"], 2 * b + t)
                    for j, src in enumerate((F["ar"][:, 0, tok], F["be"][:, tok], F["ke"][:, tok], F["v"][:, tok])):
                        last = nc.tensor.transpose(PT[:, j * P:(j + 1) * P], src, T["ident"][:, :])
                    last.then_inc(q["tt"], 1)
                if b:
                    pe.wait_ge(q["qe"], 3 * b)
                    pe.wait_ge(q["ye"], b)
                for u, (t, hh) in enumerate(units):
                    tok = slice((2 * b + t) * P, (2 * b + t + 1) * P)
                    nc.tensor.matmul(PS[:, u, 0:2 * P], F["bt"][rows(hh), tok], F["ar"][rows(hh), :, tok], start=True, stop=True)
                    last = nc.tensor.matmul(PS[:, u, 2 * P:4 * P], F["kt"][rows(hh), tok], F["ar"][rows(hh), :, tok],
                                            start=True, stop=True)
                    last.then_inc(q["s"], 1)
                pe.wait_ge(q["d0"], b + 1)
                for u in range(4):
                    last = nc.tensor.transpose(PD[:, u * P:(u + 1) * P], Dt[:, u, :], T["ident"][:, :])
                last.then_inc(q["dtr"], 1)
                for l in range(LEVELS):
                    pe.wait_ge(q["dm"], 6 * b + l + 1)
                    if l == 0:
                        pe.wait_ge(q["lm"], LEVELS * b + LEVELS)
                    for u in range(4):
                        last = nc.tensor.matmul(PP[:, u * P:(u + 1) * P], mt[:, l, u, :], Dm[:, u, :], start=True, stop=True)
                    last.then_inc(q["p"], 1)
                    pe.wait_ge(q["pe"], LEVELS * b + l + 1)
                    for u in range(4):
                        nc.tensor.matmul(PE_[:, u * P:(u + 1) * P], Ps[:, u, :], Dt[:, u, :], start=True, stop=True)
                        if l < LEVELS - 1:
                            last = nc.tensor.matmul(PD[:, u * P:(u + 1) * P], Dt[:, u, :], Ps[:, u, :], start=True, stop=True)
                    if l == LEVELS - 1:
                        last = nc.tensor.matmul(PE_[:, 3 * P:4 * P], Ps[:, 3, :], Dt[:, 3, :], start=True, stop=True)
                    last.then_inc(q["dd"], 1)
                pe.wait_ge(q["te"], 2 * b + 2)
                for u, (t, hh) in enumerate(units):
                    last = nc.tensor.matmul(PS[:, 0, u * CH:(u + 1) * CH], sc[:, u, 2, :], tk[:, t, 3, rows(hh)],
                                            start=True, stop=True)
                last.then_inc(q["lv"], 1)
                pe.wait_ge(q["dm"], 6 * b + 6)
                pe.wait_ge(q["lve"], b + 1)
                for u, (t, hh) in enumerate(units):
                    nc.tensor.matmul(PS[:, 1, 2 * u * CH:(2 * u + 1) * CH], Dt[:, u, :], tk[:, t, 0, rows(hh)],
                                     start=True, stop=True)
                    last = nc.tensor.matmul(PS[:, 1, (2 * u + 1) * CH:(2 * u + 2) * CH], Dt[:, u, :], LV[:, u, :],
                                            start=True, stop=True)
                last.then_inc(q["w"], 1)
                pe.wait_ge(q["we"], b + 1)
                for u, (t, hh) in enumerate(units):
                    tok = slice((2 * b + t) * P, (2 * b + t + 1) * P)
                    o = PS[0:CH, 2, u * P:(u + 1) * P]
                    nc.tensor.matmul(o, WZ[:, u, 0, :], sc[:, u, 1, :], start=True, stop=False)
                    last = nc.tensor.matmul(o, T["ident"][:, rows(hh)], F["ar"][:, 1, tok], start=False, stop=True)
                last.then_inc(q["q"], 1)
                for c in range(2):
                    half = rows(c)
                    for u, (t, hh) in enumerate(units):
                        chunk = 2 * (2 * b + t) + c
                        bank = 3 if c else 0
                        g = PS[0:CH, bank, 2 * u * CH:(2 * u + 1) * CH]
                        nc.tensor.matmul(g, WZ[half, u, 0, :], tk[half, t, 1, rows(hh)], start=True, stop=False)
                        nc.tensor.matmul(g, T["ident"][:, rows(hh)], F["dc"][:, chunk, :], start=False, stop=True)
                        h = PS[0:CH, bank, (2 * u + 1) * CH:(2 * u + 2) * CH]
                        nc.tensor.matmul(h, tk[half, t, 1, rows(hh)], WZ[half, u, 1, :], start=True, stop=False)
                        last = nc.tensor.matmul(h, tk[half, t, 2, rows(hh)], tk[half, t, 3, rows(hh)], start=False, stop=True)
                    last.then_inc(q["q"], 1)
                for u, (t, hh) in enumerate(units):
                    o = PS[:, 1, u * CH:(u + 1) * CH]
                    nc.tensor.matmul(o, sc[:, u, 1, :], WZ[:, u, 1, :], start=True, stop=False)
                    last = nc.tensor.matmul(o, sc[:, u, 3, :], tk[:, t, 3, rows(hh)], start=False, stop=True)
                last.then_inc(q["y"], 1)

        @block.scalar
        def _(act):
            for b in range(B):
                for t in range(2):
                    act.wait_ge(q["tt"], 2 * b + t + 1)
                    if b:
                        act.wait_ge(q["y"], b)
                    nc.scalar.activation(F["vt"][:, 2 * b + t, :], PT[:, 3 * P:4 * P], ACT.Copy)
                    nc.scalar.activation(tk[:, t, :, :], quad(PT[:, :]), ACT.Copy).then_inc(q["te"], 1)
                for l in range(LEVELS):
                    act.wait_ge(q["p"], LEVELS * b + l + 1)
                    nc.scalar.activation(Ps[:, :, :], quad(PP[:, :]), ACT.Copy).then_inc(q["pe"], 1)
                act.wait_ge(q["lv"], b + 1)
                nc.scalar.activation(LV[:, :, :], PS[:, 0, 0:4 * CH].rearrange("p (a b) -> p a b", b=CH), ACT.Copy
                                     ).then_inc(q["lve"], 1)
                act.wait_ge(q["w"], b + 1)
                nc.scalar.activation(WZ[:, :, :, :].rearrange("p a b c -> p (a b c)"), PS[:, 1, :], ACT.Copy
                                     ).then_inc(q["we"], 1)
                act.wait_ge(q["q"], 3 * b + 1)
                nc.scalar.activation(F["qt"][:, 2 * b:2 * b + 2, :, :].rearrange("p a b c -> p (a b) c"),
                                     quad(PS[0:CH, 2, :]), ACT.Copy).then_inc(q["qe"], 1)
                for c in range(2):
                    act.wait_ge(q["q"], 3 * b + 2 + c)
                    nc.scalar.activation(F["gh"][:, 2 * b:2 * b + 2, c, :].rearrange("p a b -> p a b"),
                                         PS[0:CH, 3 if c else 0, :].rearrange("p (a b) -> p a b", a=2), ACT.Copy
                                         ).then_inc(q["qe"], 1)

        @block.vector
        def _(dve):
            link = chained(dve, q["d"])
            for b in range(B):
                for u in range(4):
                    dve.wait_ge(q["s"], 4 * b + u + 1)
                    nc.vector.tensor_tensor(sc[:, u, :, :], quad(PS[:, u, :]), R["masks"][:, 0:4, :], ALU.mult).then_inc(q["m"], 1)
                dve.wait_ge(q["m"], 4 * b + 4)
                M = sc[:, :, 0, :]
                link(nc.vector.tensor_tensor(Dt[:, :, :], M, R["masks"][:, 4, None, :].broadcast_to([P, 4, P]), ALU.mult))
                nc.vector.tensor_tensor(Dt[:, :, :], Dt[:, :, :], T["ident"][:, None, :].broadcast_to([P, 4, P]),
                                        ALU.add).then_inc(q["d0"], 1)
                dve.wait_ge(q["d0"], b + 1)
                dve.wait_ge(q["dtr"], b + 1)
                nc.vector.tensor_copy(Dm[:, :, :], quad(PD[:, :])).then_inc(q["dm"], 1)
                for l in range(LEVELS):
                    dve.wait_ge(q["dd"], LEVELS * b + l + 1)
                    if l < LEVELS - 1:
                        dve.wait_ge(q["dm"], 6 * b + l + 1)
                        nc.vector.tensor_tensor(Dm[:, :, :], quad(PD[:, :]), Dm[:, :, :], ALU.add)
                    nc.vector.tensor_tensor(Dt[:, :, :], quad(PE_[:, :]), Dt[:, :, :], ALU.add).then_inc(q["dm"], 1)
                    dve.wait_ge(q["dm"], 6 * b + l + 2)
                dve.wait_ge(q["y"], b + 1)
                nc.vector.tensor_copy(F["y"][:, 2 * b:2 * b + 2, :, :].rearrange("p a b c -> p (a b) c"),
                                      PS[:, 1, 0:4 * CH].rearrange("p (a b) -> p a b", b=CH)).then_inc(q["ye"], 1)

        @block.gpsimd
        def _(pool):
            for b in range(B):
                pool.wait_ge(q["m"], 4 * b + 4)
                if b:
                    pool.wait_ge(q["p"], LEVELS * b)
                for l in range(LEVELS):
                    nc.gpsimd.tensor_tensor(mt[:, l, :, :], sc[:, :, 0, :],
                                            R["masks"][:, 5 + l, None, :].broadcast_to([P, 4, P]), ALU.mult).then_inc(q["lm"], 1)


def state_phase(nc, T, R, F, p):
    with ExitStack() as ctx:
        sb = lambda n, s, dt=F32: ctx.enter_context(nc.sbuf_tensor(f"s{p}_{n}", s, dt))
        pb = lambda n, s: ctx.enter_context(nc.psum_tensor(f"s{p}_{n}", s, F32))
        ST = sb("ST", [CH, NCH + 1, 2, CH])
        tmp = sb("tmp", [P, NT, P])
        gs = sb("gs", [P, NT, P])
        bn = sb("bn", [P, NT, 2])
        mean = sb("mean", [P, NT, 2])
        var = sb("var", [P, NT, 2])
        PS = pb("PS", [P, 2, BANK])
        PY = pb("PY", [P, 2, BANK])
        PG = pb("PG", [P, 2, BANK])
        PB = pb("PB", [P, BANK])
        q = sems(nc, ctx, "st add g y d vs vq yd yt ge", f"s{p}_")
        block = ctx.enter_context(nc.Block())
        ch = slice(p * P, (p + 1) * P)

        @block.tensor
        def _(pe):
            def gates(i):
                nc.tensor.matmul(PG[:, i // 4, (i % 4) * P:(i % 4 + 1) * P], R["hg"][:, i * P:(i + 1) * P], R["g2"][:, ch],
                                 start=True, stop=True)
                last = nc.tensor.matmul(PB[:, 2 * i:2 * i + 2], F["bonus"][:, i * P:(i + 1) * P], R["blockones"][:, 0:P:CH],
                                        start=True, stop=True)
                if i == NT - 1:
                    last.then_inc(q["g"], 1)

            for c in range(NCH):
                pe.wait_ge(q["add"], c + 1)
                if c < NCH - 1:
                    for hh in range(2):
                        last = nc.tensor.matmul(PS[0:CH, c % 2, hh * CH:(hh + 1) * CH],
                                                F["gh"][:, c // 2, c % 2, 2 * hh * CH:(2 * hh + 1) * CH], ST[:, c, hh, :],
                                                start=True, stop=True)
                    last.then_inc(q["st"], 1)
                i, half = c // 2, c % 2
                for hh in range(2):
                    col = (i % 4) * P + hh * CH
                    last = nc.tensor.matmul(PY[half * CH:(half + 1) * CH, i // 4, col:col + CH],
                                            F["qt"][:, i, hh, half * CH:(half + 1) * CH], ST[:, c, hh, :], start=True, stop=True)
                if c % 8 == 7:
                    last.then_inc(q["y"], 1)
                if half:
                    gates(i)
            for g in range(2):
                pe.wait_ge(q["yd"], 1)
                for t in range(4):
                    i = 4 * g + t
                    last = nc.tensor.transpose(PY[:, g, t * P:(t + 1) * P], F["y"][:, i, :, :].rearrange("p a b -> p (a b)"),
                                               T["ident"][:, :])
                last.then_inc(q["yt"], 1)

        @block.vector
        def _(dve):
            link = chained(dve, q["d"])
            nc.vector.memset(ST[:, 0, :, :], 0.0).then_inc(q["add"], 1)
            for c in range(NCH - 1):
                dve.wait_ge(q["st"], c + 1)
                H = F["gh"][:, c // 2, c % 2, :].rearrange("p (a b c) -> p a b c", b=2, c=CH)[:, :, 1, :]
                nc.vector.tensor_tensor(ST[:, c + 1, :, :], PS[0:CH, c % 2, 0:P].rearrange("p (a b) -> p a b", b=CH), H,
                                        ALU.add).then_inc(q["add"], 1)
            Y = F["y"][:, :, :, :].rearrange("p a b c -> p (a b) c")
            flat = F["y"][:, :, :, :].rearrange("p a b c -> p a (b c)")
            G16 = lambda t: t.rearrange("p a b -> p (a b)")[:, :, None].broadcast_to([P, 2 * NT, CH])
            dve.wait_ge(q["y"], 2)
            link(nc.vector.tensor_tensor(Y, PY[:, :, :].rearrange("p a (b c) -> p (a b) c", c=CH), Y, ALU.add))
            link(nc.vector.tensor_reduce(mean[:, :, :].rearrange("p a b -> p (a b)"), Y, AX.X, ALU.add))
            link(nc.vector.tensor_scalar(mean[:, :, :], mean[:, :, :], 1.0 / CH, None, ALU.mult))
            link(nc.vector.tensor_tensor(Y, Y, G16(mean[:, :, :]), ALU.subtract))
            t16 = tmp[:, :, :].rearrange("p a (b c) -> p (a b) c", c=CH)
            link(nc.vector.tensor_tensor(t16, Y, Y, ALU.mult))
            link(nc.vector.tensor_reduce(var[:, :, :].rearrange("p a b -> p (a b)"), t16, AX.X, ALU.add))
            nc.vector.tensor_scalar(var[:, :, :], var[:, :, :], 1.0 / CH, LNX_EPS, ALU.mult, ALU.add).then_inc(q["vs"], 1)
            dve.wait_ge(q["g"], 1)
            link(nc.vector.tensor_copy(bn[:, :, :], PB[:, 0:2 * NT].rearrange("p (a b) -> p a b", b=2)))
            link(nc.vector.tensor_tensor(t16, F["vt"][:, :, :].rearrange("p a (b c) -> p (a b) c", c=CH), G16(bn[:, :, :]), ALU.mult))
            dve.wait_ge(q["vq"], 1)
            link(nc.vector.reciprocal(var[:, :, :], var[:, :, :]))
            link(nc.vector.tensor_tensor(Y, Y, G16(var[:, :, :]), ALU.mult))
            link(nc.vector.tensor_tensor(flat, flat, R["lng"][:, None, ch].broadcast_to([P, NT, P]), ALU.mult))
            link(nc.vector.tensor_tensor(flat, flat, R["lnb"][:, None, ch].broadcast_to([P, NT, P]), ALU.add))
            link(nc.vector.tensor_tensor(flat, flat, tmp[:, :, :], ALU.add))
            dve.wait_ge(q["ge"], 1)
            nc.vector.tensor_tensor(flat, flat, gs[:, :, :], ALU.mult).then_inc(q["yd"], 1)

        @block.scalar
        def _(act):
            act.wait_ge(q["g"], 1)
            nc.scalar.activation(gs[:, :, :].rearrange("p a b -> p (a b)"), PG[:, :, :].rearrange("p a b -> p (a b)"),
                                 ACT.Copy).then_inc(q["ge"], 1)
            act.wait_ge(q["vs"], 1)
            nc.scalar.activation(var[:, :, :], var[:, :, :], ACT.Sqrt).then_inc(q["vq"], 1)
            for g in range(2):
                act.wait_ge(q["yt"], g + 1)
                nc.scalar.activation(T["yT"][:, p, g * BANK:(g + 1) * BANK], PY[:, g, :], ACT.Copy)


def rwkv(nc, T):
    with ExitStack() as ctx:
        sb = lambda n, s, dt=F32: ctx.enter_context(nc.sbuf_tensor(n, s, dt))
        R = {}
        R["cols"] = sb("rw_cols_sb", [P, PAIRS, 8])
        R["omcols"] = sb("rw_omcols", [P, PAIRS, 8])
        R["w2a2"] = sb("rw_w2a2", [P, RW])
        R["g2"] = sb("rw_g2_sb", [P, RW])
        R["lng"] = sb("rw_lng", [P, RW])
        R["lnb"] = sb("rw_lnb", [P, RW])
        R["masks"] = sb("rw_masks", [P, 10, P])
        R["blockones"] = sb("rw_blockones", [P, P])
        R["ident2"] = sb("rw_ident2", [P, CH])
        R["hwa"] = sb("rw_hwa", [P, S])
        R["hg"] = sb("rw_hg", [P, S])
        lora_phase(nc, T, R)
        F = {}
        F["ar"] = sb("rw_ar", [P, 2, S])
        F["bt"] = sb("rw_bt", [P, S])
        F["kt"] = sb("rw_kt", [P, S])
        F["be"] = sb("rw_be", [P, S])
        F["ke"] = sb("rw_ke", [P, S])
        F["v"] = sb("rw_v", [P, S])
        F["bonus"] = sb("rw_bonus", [P, S])
        F["dc"] = sb("rw_dc", [P, NCH, CH])
        for p in range(PAIRS):
            features_phase(nc, T, R, F, p)
            with ExitStack() as c2:
                sb2 = lambda n, s: c2.enter_context(nc.sbuf_tensor(f"{n}{p}", s, F32))
                F["qt"] = sb2("rw_qt", [CH, NT, 2, P])
                F["gh"] = sb2("rw_gh", [CH, NT, 2, 2 * P])
                F["y"] = sb2("rw_y", [P, NT, 2, CH])
                F["vt"] = sb2("rw_vt", [P, NT, P])
                chunks_phase(nc, T, R, F, p)
                state_phase(nc, T, R, F, p)


_NAMES = ["x", "w_in", "rw_w1", "rw_w2", "rw_a1", "rw_a2", "rw_g1", "rw_g2", "rw_lnx_g", "rw_lnx_b", "nsa_qn_g", "nsa_kn_g",
          "nsa_pe", "nsa_cmp_w1", "nsa_cmp_w2", "w_out", "ln2_g", "moe_wr", "moe_br", "moe_w1", "moe_b1", "moe_w2", "moe_b2"]


def hybrid_layer_kernel(nc, arrays):
    T = dict(arrays)
    T["h_rows"] = nc.dram_tensor("h_rows", [S + PAD_ROWS, D], F32).ap()
    T["token_list"] = nc.dram_tensor("token_list", [P, N_SLOTS, 2], I32).ap()
    with ExitStack() as ctx:
        sb = lambda n, s, dt=F32: ctx.enter_context(nc.sbuf_tensor(n, s, dt))
        T["ident"] = sb("ident", [P, P])
        T["slots"] = sb("slots", [P, N_SLOTS, 2], I32)
        T["counts"] = sb("counts", [1, N_EXP], I32)
        with ExitStack() as mixers:
            T["yT"] = mixers.enter_context(nc.sbuf_tensor("yT", [P, DC, S], F32))
            with ExitStack() as normed:
                T["xnT"] = normed.enter_context(nc.sbuf_tensor("xnT", [P, DC, S + 1], F32))
                norm_phase(nc, T)
                with ExitStack() as attention:
                    sa = lambda n, s: attention.enter_context(nc.sbuf_tensor(n, s, F32))
                    N = dict(vs=sa("vs", [P, NT, P]), vw=sa("vw", [P, NT, P]), gates=sa("gates", [P, NT, 3 * QH]),
                              qT=sa("qT", [P, 4, S]), qrT=sa("qrT", [P, 4, S]), kT=sa("kT", [P, 4, S]),
                              vcmp=sa("vcmp", [N_CMP, 2, HD]), kcT=sa("kcT", [P, 2, N_CMP]))
                    with ExitStack() as blocks:
                        N["cT"] = blocks.enter_context(nc.sbuf_tensor("cT", [P, 4, S + 2], F32))
                        nsa_project_phase(nc, T, N)
                        compress_phase(nc, T, N)
                    attention_phase(nc, T, N)
                rwkv(nc, T)
            route_phase(nc, T)
        expert_phase(nc, T)


def _constants():
    f32 = np.float32
    c = {}
    c["c_ident"] = np.eye(P, dtype=f32)
    c["c_upper"] = np.triu(np.ones((P, P), f32), 1)
    c["c_lower"] = np.tril(np.ones((N_EXP, N_EXP), f32), -1).reshape(1, -1)
    pos = np.arange(S)
    inv = (10000.0 ** (-np.arange(HD // 2, dtype=f32) / f32(HD // 2))).astype(f32)
    ang = pos.astype(f32)[:, None] * inv[None, :]
    c["c_cos"] = np.cos(ang).astype(f32)
    c["c_sin"] = np.sin(ang).astype(f32)
    whole = (16 * np.arange(N_CMP) + 31)[None, :] <= pos[:, None]
    c["c_cmask"] = whole.astype(f32)
    c["c_cpen"] = np.where(whole, 0, NEG).astype(f32)
    row, col = np.arange(P)[:, None], np.arange(P)[None, :]
    c["c_wpen"] = np.concatenate([np.where(col > row, 0, NEG), np.zeros((P, P)), np.where(col <= row, 0, NEG)], 1).astype(f32)
    block, cur = np.arange(16)[None, :], (pos // 64)[:, None]
    forced = (block == 0) | (block == cur) | (block == cur - 1)
    future = block > cur
    c["c_free"] = (~(forced | future)).astype(f32)
    c["c_force"] = np.where(future, -1e6, np.where(forced, 1e6, 0)).astype(f32)
    c["c_lower16"] = np.tril(np.ones((16, 16), f32), -1).reshape(1, -1)
    same = lambda n: (row // n) == (col // n)
    masks = [same(CH) & (row < col), same(CH) & (row <= col)] * 2
    for n in (1, 2, 4, 8, 16, 32):
        masks.append(same(2 * n) & ((col // n) % 2 == 1) & ((row // n) % 2 == 0))
    c["c_masks"] = np.stack(masks, 1).astype(f32)
    c["c_blockones"] = same(CH).astype(f32)
    c["c_ident2"] = np.concatenate([np.eye(CH)] * 2, 0).astype(f32)
    return c


def _columns(inputs):
    cols = lambda v: np.asarray(v).reshape(-1, P).T
    mu = np.asarray(inputs["rw_mu_rkv"])[0]
    per_channel = [mu[0], mu[1], mu[2]] + [np.asarray(inputs[k])[0] for k in ("rw_w0", "rw_a0", "rw_k_k", "rw_k_a", "rw_r_k")]
    return {
        "ln1_cols": cols(inputs["ln1_g"]),
        "mu_wag_cols": np.asarray(inputs["rw_mu_wag"])[0].reshape(3, DC, P).transpose(2, 0, 1),
        "rw_cols": np.stack([cols(v) for v in per_channel], 2),
    }


def kernel(**inputs):
    import concourse.bacc as _bacc
    from concourse.bass_utils import run_bass_kernel_spmd as _run

    nc = _bacc.Bacc("TRN2", target_bir_lowering=False, num_devices=1)
    sent = {n: inputs[n] for n in _NAMES} | _columns(inputs) | _constants()
    arrays, aps = {}, {}
    for name, a in sent.items():
        a = np.ascontiguousarray(a)
        arrays[f"in_{name}"] = a
        aps[name] = nc.dram_tensor(f"in_{name}", a.shape, mybir.dt.from_np(a.dtype), kind="ExternalInput").ap()
    aps["out"] = nc.dram_tensor("out_rows", (S + PAD_ROWS, D), F32, kind="ExternalOutput").ap()
    hybrid_layer_kernel(nc, aps)
    r = _run(nc, [arrays], core_ids=[0])
    return r.results[0]["out_rows"][:S].reshape(1, S, D)
```

```python
import concourse.bass as bass
from concourse import mybir
from contextlib import ExitStack
import numpy as np

F32 = mybir.dt.float32
I32 = mybir.dt.int32
ALU = mybir.AluOpType
ACT = mybir.ActivationFunctionType
AX = mybir.AxisListType

P = 128
D = 1024
S = 1024
NT = S // P
DC = D // P
BANK = 512
EPS = 1e-6
N_EXP = 32
TOP_K = 4
D_FF = 1024
PAD_ROWS = P
LIST_K = S // P
N_SLOTS = N_EXP * LIST_K
LIMIT = 7.0
ALPHA = 1.702


def sem_list(nc, ctx, names):
    out = [nc.alloc_semaphore(n) for n in names]

    def over():
        nc.clear_and_free_semaphores(out)
        nc.all_engine_barrier(sem_only=True)
    ctx.callback(over)
    return out


def sems(nc, ctx, names, prefix=""):
    names = names.split()
    return dict(zip(names, sem_list(nc, ctx, [prefix + n for n in names])))


def chained(eng, sem):
    count = [0]

    def link(ins):
        count[0] += 1
        ins.then_inc(sem, 1)
        eng.wait_ge(sem, count[0])
    return link


def route_phase(nc, T):
    with ExitStack() as ctx:
        sb = lambda n, s, dt=F32: ctx.enter_context(nc.sbuf_tensor(n, s, dt))
        pb = lambda n, s: ctx.enter_context(nc.psum_tensor(n, s, F32))
        wout = sb("wout", [P, DC, D])
        x2 = sb("x2", [P, NT, D])
        hrow = sb("hrow", [P, 2, D])
        hT = sb("hT", [P, 2, DC, P])
        g2 = sb("g2", [P, D])
        wr = sb("wr", [P, DC, N_EXP])
        br = sb("br", [P, N_EXP])
        junk = sb("junk", [P, D])
        zero = sb("zero", [P, D])
        st = sb("st", [P, 3, NT])
        L = sb("L", [P, NT, N_EXP])
        cmp1 = sb("cmp1", [P, N_EXP, N_EXP])
        cmp2 = sb("cmp2", [P, N_EXP, N_EXP])
        lower = sb("lower", [P, N_EXP, N_EXP])
        rank = sb("rank", [P, NT, N_EXP])
        sel = sb("sel", [P, NT, N_EXP])
        G = sb("G", [P, NT, N_EXP])
        mx = sb("mx", [P, NT])
        den = sb("den", [P, NT])
        upper = sb("upper", [P, P])
        ones = sb("ones", [P, P])
        ecol = sb("ecol", [P, N_EXP])
        posi = sb("posi", [P, NT, N_EXP], I32)
        posk = sb("posk", [P, NT, N_EXP], I32)
        posf = sb("posf", [P, NT, N_EXP])
        poskf = sb("poskf", [P, NT, N_EXP])
        pick = sb("pick", [P, NT, N_EXP])
        dst = sb("dst", [P, TOP_K, NT])
        dsti = sb("dsti", [P, TOP_K, NT], I32)
        entry = sb("entry", [P, TOP_K, NT, 2], I32)
        gsel = sb("gsel", [P, TOP_K, NT])
        tok = sb("tok", [P, NT], I32)
        padlist = sb("padlist", [P, N_SLOTS, 2], I32)
        PO = pb("PO", [P, 2, D])
        PT = pb("PT", [P, 2, BANK])
        PL = pb("PL", [P, BANK])
        PC = pb("PC", [P, BANK])
        q = sems(nc, ctx, "r_ld_w r_ld_x r_ld_c r_po r_x2 r_ss r_ms r_sq r_h r_st_x r_st_ha r_st_hb r_st_x0 r_st_h0 r_tp r_hT r_lg "
                          "r_logit r_pool r_padst r_sel r_pos r_exp r_ent r_scat r_back r_dve r_mxn r_cnt")
        block = ctx.enter_context(nc.Block())
        h_stored = (q["r_st_ha"], q["r_st_hb"])
        x_rows = T["x"].rearrange("o (t p) d -> (o t) p d", p=P)

        @block.sync
        def _(sp):
            for k in range(DC):
                sp.dma_start(wout[:, k, :], T["w_out"][0, k * P:(k + 1) * P, :]).then_inc(q["r_ld_w"], 16)
            sp.dma_start(wr[:, :, :], T["moe_wr"][0].rearrange("(k p) e -> p k e", p=P)).then_inc(q["r_ld_c"], 16)
            sp.dma_start(upper[:, :], T["c_upper"]).then_inc(q["r_ld_c"], 16)
            sp.dma_start(lower[:, :, :].rearrange("p a b -> p (a b)"),
                         T["c_lower"].broadcast_to([P, N_EXP * N_EXP])).then_inc(q["r_ld_c"], 16)
            for i in range(NT):
                sp.wait_ge(q["r_x2"], i + 1)
                sp.dma_start(T["out"][i * P:(i + 1) * P, :], x2[:, i, :]).then_inc(q["r_st_x"], 16)
                sp.wait_ge(q["r_h"], i + 1)
                sp.dma_start(T["h_rows"][i * P:(i + 1) * P, :], hrow[:, i % 2, :]).then_inc(h_stored[i % 2], 16)
            sp.wait_ge(q["r_st_x"], 16 * NT)
            for s_h in h_stored:
                sp.wait_ge(s_h, 16 * NT // 2)

        @block.scalar
        def _(act):
            for i in range(NT):
                act.dma_start(x2[:, i, :], x_rows[i]).then_inc(q["r_ld_x"], 16)
            act.dma_start(g2[:, :], T["ln2_g"].broadcast_to([P, D])).then_inc(q["r_ld_c"], 16)
            act.dma_start(br[:, :], T["moe_br"].broadcast_to([P, N_EXP])).then_inc(q["r_ld_c"], 16)
            for i in range(NT):
                act.wait_ge(q["r_x2"], i + 1)
                if i:
                    act.wait_ge(q["r_ss"], i)
                nc.scalar.activation(junk[:, :], x2[:, i, :], ACT.Square,
                                     accum_out=st[:, 0, i:i + 1]).then_inc(q["r_ss"], 1)
                act.wait_ge(q["r_ms"], i + 1)
                nc.scalar.activation(st[:, 2, i:i + 1], st[:, 1, i:i + 1], ACT.Sqrt).then_inc(q["r_sq"], 1)
                for g in range(2):
                    act.wait_ge(q["r_tp"], 2 * i + g + 1)
                    if i >= 2:
                        act.wait_ge(q["r_lg"], i - 1)
                    nc.scalar.activation(hT[:, i % 2, 4 * g:4 * g + 4, :], PT[:, g, :].rearrange("p (a b) -> p a b", b=P),
                                         ACT.Copy).then_inc(q["r_hT"], 1)
            act.wait_ge(q["r_mxn"], 1)
            nc.scalar.activation(G[:, :, :], G[:, :, :], ACT.Exp).then_inc(q["r_exp"], 1)

        @block.tensor
        def _(pe):
            def project(i):
                if i == 0:
                    pe.wait_ge(q["r_ld_w"], 16 * DC)
                if i >= 2:
                    pe.wait_ge(q["r_x2"], i - 1)
                for n in range(2):
                    for k in range(DC):
                        last = nc.tensor.matmul(PO[:, i % 2, n * BANK:(n + 1) * BANK], T["yT"][:, k, i * P:(i + 1) * P],
                                                wout[:, k, n * BANK:(n + 1) * BANK], start=(k == 0), stop=(k == DC - 1))
                last.then_inc(q["r_po"], 1)

            def logits(i):
                pe.wait_ge(q["r_h"], i + 1)
                for g in range(2):
                    if i:
                        pe.wait_ge(q["r_hT"], 2 * (i - 1) + g + 1)
                    for c in range(4):
                        last = nc.tensor.transpose(PT[:, g, c * P:(c + 1) * P],
                                                   hrow[:, i % 2, (4 * g + c) * P:(4 * g + c + 1) * P], T["ident"][:, :])
                    last.then_inc(q["r_tp"], 1)
                pe.wait_ge(q["r_hT"], 2 * i + 2)
                if i == 0:
                    pe.wait_ge(q["r_ld_c"], 16 * 5)
                else:
                    pe.wait_ge(q["r_logit"], i)
                for k in range(DC):
                    last = nc.tensor.matmul(PL[:, 0:N_EXP], hT[:, i % 2, k, :], wr[:, k, :],
                                            start=(k == 0), stop=(k == DC - 1))
                last.then_inc(q["r_lg"], 1)

            project(0)
            for i in range(NT):
                if i + 1 < NT:
                    project(i + 1)
                logits(i)
            pe.wait_ge(q["r_pool"], 3)
            pe.wait_ge(q["r_sel"], 1)
            for i in range(NT):
                for j in range(i + 1):
                    last = nc.tensor.matmul(PC[:, i * N_EXP:(i + 1) * N_EXP], upper[:, :] if j == i else ones[:, :],
                                            sel[:, j, :], start=(j == 0), stop=(j == i))
            last.then_inc(q["r_pos"], 1)
            for j in range(NT):
                last = nc.tensor.matmul(PL[:, 0:N_EXP], ones[:, :], sel[:, j, :], start=(j == 0), stop=(j == NT - 1))
            last.then_inc(q["r_pos"], 1)

        @block.vector
        def _(dve):
            link = chained(dve, q["r_dve"])
            dve.wait_ge(q["r_ld_c"], 16 * 5)
            for i in range(NT):
                dve.wait_ge(q["r_po"], i + 1)
                if i == 0:
                    dve.wait_ge(q["r_ld_x"], 16 * NT)
                nc.vector.tensor_tensor(x2[:, i, :], PO[:, i % 2, :], x2[:, i, :], ALU.add).then_inc(q["r_x2"], 1)
                dve.wait_ge(q["r_ss"], i + 1)
                nc.vector.tensor_scalar(st[:, 1, i:i + 1], st[:, 0, i:i + 1], 1.0 / D, EPS,
                                        ALU.mult, ALU.add).then_inc(q["r_ms"], 1)
                dve.wait_ge(q["r_sq"], i + 1)
                link(nc.vector.reciprocal(st[:, 0, i:i + 1], st[:, 2, i:i + 1]))
                if i >= 2:
                    dve.wait_ge(h_stored[i % 2], 16 * (i // 2))
                    dve.wait_ge(q["r_tp"], 2 * (i - 1))
                nc.vector.scalar_tensor_tensor(out=hrow[:, i % 2, :], in0=x2[:, i, :], scalar=st[:, 0, i:i + 1],
                                               in1=g2[:, :], op0=ALU.mult, op1=ALU.mult).then_inc(q["r_h"], 1)
                if i:
                    dve.wait_ge(q["r_lg"], i)
                    nc.vector.tensor_tensor(L[:, i - 1, :], PL[:, 0:N_EXP], br[:, :], ALU.add).then_inc(q["r_logit"], 1)
            dve.wait_ge(q["r_lg"], NT)
            nc.vector.tensor_tensor(L[:, NT - 1, :], PL[:, 0:N_EXP], br[:, :], ALU.add).then_inc(q["r_logit"], 1)
            dve.wait_ge(q["r_logit"], NT)
            for i in range(NT):
                row = L[:, i, :]
                other = row[:, None, :].broadcast_to([P, N_EXP, N_EXP])
                own = row[:, :, None].broadcast_to([P, N_EXP, N_EXP])
                nc.vector.tensor_tensor(cmp1[:, :, :], other, own, ALU.is_gt)
                link(nc.vector.tensor_tensor(cmp2[:, :, :], other, own, ALU.is_equal))
                link(nc.vector.tensor_tensor(cmp2[:, :, :], cmp2[:, :, :], lower[:, :, :], ALU.mult))
                link(nc.vector.tensor_tensor(cmp1[:, :, :], cmp1[:, :, :], cmp2[:, :, :], ALU.add))
                link(nc.vector.tensor_reduce(rank[:, i, :], cmp1[:, :, :], AX.X, ALU.add))
            nc.vector.tensor_scalar(sel[:, :, :], rank[:, :, :], TOP_K - 0.5, None, ALU.is_lt).then_inc(q["r_sel"], 1)
            link(nc.vector.tensor_reduce(mx[:, :], L[:, :, :], AX.X, ALU.max))
            nc.vector.tensor_tensor(G[:, :, :], L[:, :, :], mx[:, :, None].broadcast_to([P, NT, N_EXP]),
                                    ALU.subtract).then_inc(q["r_mxn"], 1)
            dve.wait_ge(q["r_exp"], 1)
            dve.wait_ge(q["r_sel"], 1)
            link(nc.vector.tensor_tensor(G[:, :, :], G[:, :, :], sel[:, :, :], ALU.mult))
            link(nc.vector.tensor_reduce(den[:, :], G[:, :, :], AX.X, ALU.add))
            link(nc.vector.reciprocal(den[:, :], den[:, :]))
            link(nc.vector.tensor_tensor(G[:, :, :], G[:, :, :], den[:, :, None].broadcast_to([P, NT, N_EXP]), ALU.mult))
            dve.wait_ge(q["r_pos"], 1)
            dve.wait_ge(q["r_pool"], 4)
            link(nc.vector.tensor_copy(posi[:, :, :], PC[:, 0:NT * N_EXP].rearrange("p (t e) -> p t e", e=N_EXP)))
            link(nc.vector.tensor_scalar(posk[:, :, :], posi[:, :, :], 7, None, ALU.logical_shift_right))
            link(nc.vector.tensor_scalar(posi[:, :, :], posi[:, :, :], P - 1, None, ALU.bitwise_and))
            link(nc.vector.tensor_copy(poskf[:, :, :], posk[:, :, :]))
            link(nc.vector.tensor_copy(posf[:, :, :], posi[:, :, :]))
            link(nc.vector.scalar_tensor_tensor(out=posf[:, :, :], in0=posf[:, :, :], scalar=float(N_SLOTS),
                                                in1=poskf[:, :, :], op0=ALU.mult, op1=ALU.add))
            link(nc.vector.tensor_tensor(posf[:, :, :], posf[:, :, :], ecol[:, None, :].broadcast_to([P, NT, N_EXP]),
                                         ALU.add))
            for j in range(TOP_K):
                link(nc.vector.tensor_scalar(pick[:, :, :], rank[:, :, :], float(j), None, ALU.is_equal))
                link(nc.vector.tensor_tensor(poskf[:, :, :], pick[:, :, :], posf[:, :, :], ALU.mult))
                link(nc.vector.tensor_reduce(dst[:, j, :], poskf[:, :, :], AX.X, ALU.add))
                link(nc.vector.tensor_tensor(poskf[:, :, :], pick[:, :, :], G[:, :, :], ALU.mult))
                link(nc.vector.tensor_reduce(gsel[:, j, :], poskf[:, :, :], AX.X, ALU.add))
                link(nc.vector.tensor_copy(entry[:, j, :, 0], tok[:, :]))
                link(nc.vector.tensor_copy(entry[:, j, :, 1].bitcast(F32), gsel[:, j, :]))
            nc.vector.tensor_copy(dsti[:, :, :], dst[:, :, :]).then_inc(q["r_ent"], 1)
            dve.wait_ge(q["r_pos"], 2)
            nc.vector.tensor_copy(T["counts"][:, :], PL[0:1, 0:N_EXP]).then_inc(q["r_cnt"], 1)
            dve.wait_ge(q["r_cnt"], 1)

        @block.gpsimd
        def _(pool):
            nc.gpsimd.memset(zero[:, :], 0.0).then_inc(q["r_pool"], 1)
            nc.gpsimd.memset(ones[:, :], 1.0).then_inc(q["r_pool"], 1)
            nc.gpsimd.iota(tok[:, :], pattern=[[P, NT]], base=0, channel_multiplier=1).then_inc(q["r_pool"], 1)
            nc.gpsimd.iota(ecol[:, :], pattern=[[LIST_K, N_EXP]], base=0, channel_multiplier=0,
                           allow_small_or_imprecise_dtypes=True).then_inc(q["r_pool"], 1)
            nc.gpsimd.memset(padlist[:, :, 1].bitcast(F32), 0.0).then_inc(q["r_pool"], 1)
            nc.gpsimd.iota(padlist[:, :, 0], pattern=[[0, N_SLOTS]], base=S, channel_multiplier=1).then_inc(q["r_pool"], 1)
            pool.wait_ge(q["r_pool"], 6)
            nc.gpsimd.dma_start(T["token_list"], padlist[:, :, :]).then_inc(q["r_padst"], 16)
            nc.gpsimd.dma_start(T["out"][S:S + PAD_ROWS, :], zero[:, :]).then_inc(q["r_st_x0"], 16)
            nc.gpsimd.dma_start(T["h_rows"][S:S + PAD_ROWS, :], zero[:, :]).then_inc(q["r_st_h0"], 16)
            pool.wait_ge(q["r_padst"], 16)
            pool.wait_ge(q["r_ent"], 1)
            for j in range(TOP_K):
                for i in range(NT):
                    nc.gpsimd.indirect_dma_start(
                        out=T["token_list"].rearrange("p s c -> (p s) c"),
                        out_offset=bass.IndirectOffsetOnAxis(ap=dsti[:, j, i:i + 1], axis=0),
                        in_=entry[:, j, i, :], in_offset=None).then_inc(q["r_scat"], 16)
            pool.wait_ge(q["r_scat"], 16 * TOP_K * NT)
            nc.gpsimd.dma_start(T["slots"][:, :, :], T["token_list"]).then_inc(q["r_back"], 16)
            pool.wait_ge(q["r_back"], 16)
            pool.wait_ge(q["r_st_x0"], 16)
            pool.wait_ge(q["r_st_h0"], 16)


GROUP = 2 * P
WIDTHS = (128, 144, 160, 192, GROUP)
FC = D_FF // P


def expert_pass(nc, T, first):
    tag = "x1_" if first else "x2_"
    with ExitStack() as ctx:
        sb = lambda n, s, dt=F32: ctx.enter_context(nc.sbuf_tensor(tag + n, s, dt))
        pb = lambda n, s: ctx.enter_context(nc.psum_tensor(tag + n, s, F32))
        w1 = [sb(f"w1_{j}", [P, DC, 2, 2 * P]) for j in range(4)]
        w2 = [sb(f"w2_{j}", [P, FC, BANK]) for j in range(2)]
        bias_all = sb("bias_all", [P, N_EXP, 3 * FC])
        bias = sb("bias", [P, 3 * FC])
        gate = sb("gate", [P, 2])
        hg = sb("hg", [P, 2, D])
        hT = sb("hT", [P, DC, GROUP])
        glu = sb("glu", [P, 2, GROUP])
        lin = sb("lin", [P, 2, GROUP])
        sig = sb("sig", [P, 2, GROUP])
        act_T = sb("act_T", [P, FC, GROUP])
        yT = sb("yT", [P, DC, GROUP])
        ysb = sb("ysb", [P, 2, D])
        idx_in = sb("idx_in", [P, 2], I32)
        idx_out = sb("idx_out", [P, 2], I32)
        PU = pb("PU", [P, 4, 2, GROUP])
        PY = pb("PY", [P, 2, 2, GROUP])
        PT = pb("PT", [P, 2, BANK])
        q = sems(nc, ctx, "bias_in gathered0 gathered1 turned0 turned1 hT_copy hT_ready u_done u_used glu_ready sig_ready "
                          "act_ready y_done yT_ready back_done back_half back_used scat0 scat1 links pool_copy held init", tag)
        loaded = sem_list(nc, ctx, [f"{tag}loaded{j}" for j in range(6)])
        free = sem_list(nc, ctx, [f"{tag}free{j}" for j in range(6)])
        block = ctx.enter_context(nc.Block())

        def count_of(eng, e):
            return eng.value_load(T["counts"][0:1, bass.ds(e, 1)], min_val=0, max_val=S)

        def by_width(eng, count, body):
            if not first:
                body(GROUP)
                return
            low = 0
            for width in WIDTHS:
                if low == 0:
                    with eng.If(count < width + 1):
                        body(width)
                else:
                    with eng.If(count > low):
                        if width < GROUP:
                            with eng.If(count < width + 1):
                                body(width)
                        else:
                            body(width)
                        eng.nop()
                low = width

        def groups(eng, body, before=None):
            if first:
                if before is not None:
                    before()
                count, following = eng.alloc_register(tag + "count"), eng.alloc_register(tag + "following")
                eng.reg_load(following, T["counts"][0:1, 0:1])
                known = lambda r: eng.snap(r, min_val=0, max_val=S)
                with eng.Fori(0, N_EXP - 1) as e:
                    eng.reg_mov(count, following)
                    read_next = lambda: eng.reg_load(following, T["counts"][0:1, bass.ds(e + 1, 1)])
                    body(e, e, 0, known(count), (read_next, lambda: known(following)))
                eng.reg_mov(count, following)
                body(N_EXP - 1, N_EXP - 1, 0, known(count), None)
                return
            done = eng.alloc_register(f"{tag}{eng.engine}_groups".replace(".", "_"))
            eng.reg_mov(done, 0)
            with eng.Fori(0, N_EXP) as e:
                count = count_of(eng, e)
                with eng.If(count > GROUP):
                    with eng.Fori(1, S // GROUP) as j:
                        body(eng.snap(done), e, j, count, None)
                        eng.reg_add(done, done, 1)
                    eng.nop()
                eng.nop()

        @block.sync
        def _(sp):
            for j in range(6):
                sp.sem_inc(free[j], 1)
            sp.dma_start(bias_all[:, :, :], T["moe_bias_cols"]).then_inc(q["bias_in"], 16)

            def load(n, e, j, count, ahead):
                w1_e = T["moe_w1"][0][bass.ds(e, 1)].rearrange("o (k p) f -> p (o k) f", p=P)
                w2_e = T["moe_w2"][0][bass.ds(e, 1)].rearrange("o (k p) f -> p (o k) f", p=P)
                for s in range(4):
                    sp.wait_ge(free[s], n + 1)
                    for side in range(2):
                        lo = side * D_FF + 2 * s * P
                        sp.dma_start(w1[s][:, :, side, :], w1_e[:, :, lo:lo + 2 * P]).then_inc(loaded[s], 16)
                for s in range(2):
                    sp.wait_ge(free[4 + s], n + 1)
                    sp.dma_start(w2[s][:, :, :], w2_e[:, :, s * BANK:(s + 1) * BANK]).then_inc(loaded[4 + s], 16)

            groups(sp, load)
            sp.wait_ge(q["bias_in"], 16)

        @block.tensor
        def _(pe):
            seconds = pe.alloc_register(tag + "pe_seconds")
            pe.reg_mov(seconds, 0)

            def turn(n, count, wait_back):
                if wait_back:
                    pe.wait_ge(q["back_used"], n if first else n + 1)
                pe.wait_ge(q["gathered0"], 16 * n + 16)
                for c in range(DC):
                    last = nc.tensor.transpose(PT[:, c // 4, (c % 4) * P:(c % 4 + 1) * P], hg[:, 0, c * P:(c + 1) * P],
                                               T["ident"][:, :])
                last.then_inc(q["turned0"], 1)

                def second():
                    pe.wait_ge(q["gathered1"], 16 * pe.snap(seconds) + 16)
                    pe.wait_ge(q["hT_copy"], n + 1)
                    for c in range(DC):
                        last = nc.tensor.transpose(PT[:, c // 4, (c % 4) * P:(c % 4 + 1) * P], hg[:, 1, c * P:(c + 1) * P],
                                                   T["ident"][:, :])
                    last.then_inc(q["turned1"], 1)
                    pe.reg_add(seconds, seconds, 1)

                if first:
                    with pe.If(count > P):
                        second()
                    with pe.Else():
                        pe.sem_inc(q["turned1"], 1)
                else:
                    second()

            def up(n, N, ahead):
                for c in range(FC):
                    if c == 4 and ahead:
                        ahead[0]()
                    pe.wait_ge(loaded[c // 2], 32 * n + 32)
                    pe.wait_ge(q["u_used"], 8 * n + c + 1)
                    for side in range(2):
                        for k in range(DC):
                            last = nc.tensor.matmul(PU[:, c % 4, side, 0:N], w1[c // 2][:, k, side, (c % 2) * P:(c % 2 + 1) * P],
                                                    hT[:, k, 0:N], start=(k == 0), stop=(k == DC - 1))
                            if side == 0 and k == 0 and c and c % 2 == 0:
                                last.then_inc(free[c // 2 - 1], 1)
                    last.then_inc(q["u_done"], 1)

            def down(n, N, ahead):
                def back(pair):
                    pe.wait_ge(q["yT_ready"], 4 * n + pair + 3)
                    if pair == 0:
                        pe.wait_ge(q["hT_ready"], n + 2 if ahead else n + 1)
                    if pair == 2:
                        pe.wait_ge(q["back_half"], n + 1)
                    for c in (2 * pair, 2 * pair + 1):
                        for g in range(2 if N > P else 1):
                            last = nc.tensor.transpose(PT[:, g, (c % 4) * P:(c % 4 + 1) * P], yT[:, c, g * P:(g + 1) * P],
                                                       T["ident"][:, :])
                            if pair == 2 and c == 4 and g == 0:
                                last.then_inc(free[5], 1)
                    if pair % 2:
                        last.then_inc(q["back_done"], 1)

                pe.wait_ge(q["act_ready"], 8 * n + 8)
                for c in range(DC):
                    pair = c // 2
                    if c % 4 == 0:
                        pe.wait_ge(loaded[4 + c // 4], 16 * n + 16)
                    if c % 2 == 0:
                        pe.wait_ge(q["yT_ready"], 4 * n + pair + 1)
                    for k in range(FC):
                        last = nc.tensor.matmul(PY[:, pair % 2, c % 2, 0:N], w2[c // 4][:, k, (c % 4) * P:(c % 4 + 1) * P],
                                                act_T[:, k, 0:N], start=(k == 0), stop=(k == FC - 1))
                        if k == 0 and c % 4 == 0:
                            last.then_inc(free[4] if c else free[3], 1)
                    if c % 2:
                        last.then_inc(q["y_done"], 1)
                    if c % 2 and pair:
                        back(pair - 1)
                back(3)

            def group(n, e, j, count, ahead):
                if not first:
                    turn(n, count, True)
                pe.wait_ge(q["hT_ready"], n + 1)
                by_width(pe, count, lambda N: up(n, N, ahead))
                if ahead:
                    turn(n + 1, ahead[1](), True)
                by_width(pe, count, lambda N: down(n, N, ahead))

            groups(pe, group, lambda: turn(0, count_of(pe, 0), False))

        @block.scalar
        def _(act):
            def copy_turned(n, count):
                act.wait_ge(q["turned0"], n + 1)
                whole = PT[:, :, :].rearrange("p a (b c) -> p (a b) c", c=P)
                nc.scalar.activation(hT[:, :, 0:P], whole, ACT.Copy).then_inc(q["hT_copy"], 1)

                def second():
                    act.wait_ge(q["turned1"], n + 1)
                    nc.scalar.activation(hT[:, :, P:GROUP], whole, ACT.Copy).then_inc(q["hT_ready"], 1)

                if first:
                    with act.If(count > P):
                        second()
                    with act.Else():
                        act.wait_ge(q["hT_copy"], n + 1)
                        act.sem_inc(q["hT_ready"], 1)
                else:
                    second()

            def sigmoids(n, N):
                for c in range(FC):
                    act.wait_ge(q["glu_ready"], 8 * n + c + 1)
                    nc.scalar.activation(sig[:, c % 2, 0:N], glu[:, c % 2, 0:N], ACT.Sigmoid, scale=ALPHA).then_inc(q["sig_ready"], 1)

            def outputs(n, N):
                for pair in range(4):
                    act.wait_ge(q["y_done"], 4 * n + pair + 1)
                    for c in range(2):
                        f = 2 * pair + c
                        last = nc.scalar.activation(yT[:, f, 0:N], PY[:, pair % 2, c, 0:N], ACT.Identity,
                                                    bias=bias[:, 2 * FC + f:2 * FC + f + 1])
                    last.then_inc(q["yT_ready"], 1)

            def group(n, e, j, count, ahead):
                if not first:
                    copy_turned(n, count)
                by_width(act, count, lambda N: sigmoids(n, N))
                if ahead:
                    ahead[0]()
                    copy_turned(n + 1, ahead[1]())
                by_width(act, count, lambda N: outputs(n, N))

            groups(act, group, lambda: copy_turned(0, count_of(act, 0)))

        @block.vector
        def _(dve):
            seconds = dve.alloc_register(tag + "dve_seconds")
            dve.reg_mov(seconds, 0)
            dve.sem_inc(q["u_used"], 4)
            dve.sem_inc(q["back_used"], 1)
            dve.sem_inc(q["yT_ready"], 2)
            LINKS = 3 + 2 * FC
            nc.vector.memset(yT[:, :, :], 0.0).then_inc(q["init"], 1)
            dve.wait_ge(q["init"], 2)
            dve.wait_ge(q["bias_in"], 16)

            def gated(n, N):
                for c in range(FC):
                    b = c % 2
                    dve.wait_ge(q["u_done"], 8 * n + c + 1)
                    nc.vector.tensor_scalar(glu[:, b, 0:N], PU[:, c % 4, 0, 0:N], bias[:, c:c + 1], LIMIT,
                                            ALU.add, ALU.min).then_inc(q["glu_ready"], 1)
                    nc.vector.tensor_scalar(lin[:, b, 0:N], PU[:, c % 4, 1, 0:N], bias[:, FC + c:FC + c + 1], LIMIT,
                                            ALU.add, ALU.min).then_inc(q["u_used"], 1)
                    dve.wait_ge(q["u_used"], 8 * n + c + 5)
                    nc.vector.tensor_scalar(lin[:, b, 0:N], lin[:, b, 0:N], -LIMIT, 1.0, ALU.max, ALU.add).then_inc(q["links"], 1)
                    dve.wait_ge(q["links"], LINKS * n + 3 + 2 * c + 1)
                    nc.vector.tensor_tensor(lin[:, b, 0:N], lin[:, b, 0:N], glu[:, b, 0:N], ALU.mult).then_inc(q["links"], 1)
                    dve.wait_ge(q["links"], LINKS * n + 3 + 2 * c + 2)
                    dve.wait_ge(q["sig_ready"], 8 * n + c + 1)
                    nc.vector.tensor_tensor(act_T[:, c, 0:N], lin[:, b, 0:N], sig[:, b, 0:N], ALU.mult).then_inc(q["act_ready"], 1)

            def finish(n, N):
                for half in range(2):
                    cols = slice(half * BANK, (half + 1) * BANK)
                    dve.wait_ge(q["back_done"], 2 * n + half + 1)
                    if half == 0:
                        dve.wait_ge(q["scat0"], 16 * n + 16)
                        if N > P:
                            dve.wait_ge(q["scat1"], 16 * dve.snap(seconds) + 16)
                    for g in range(2 if N > P else 1):
                        last = nc.vector.tensor_scalar(ysb[:, g, cols], PT[:, g, :], gate[:, g:g + 1], None, ALU.mult)
                    last.then_inc(q["back_used"] if half else q["back_half"], 1)
                if N > P:
                    dve.reg_add(seconds, seconds, 1)

            def group(n, e, j, count, ahead):
                dve.wait_ge(q["back_used"], n + 1)
                nc.vector.tensor_copy(bias[:, :], bias_all[:, bass.ds(e, 1), :].rearrange("p a b -> p (a b)")).then_inc(q["links"], 1)
                for g in range(2):
                    slot = e * LIST_K + 2 * j + g
                    nc.vector.tensor_copy(gate[:, g:g + 1], T["slots"][:, bass.ds(slot, 1), 1].bitcast(F32)).then_inc(q["links"], 1)
                dve.wait_ge(q["links"], LINKS * n + 3)
                dve.sem_inc(q["held"], 1)
                if ahead:
                    ahead[0]()
                by_width(dve, count, lambda N: gated(n, N))
                by_width(dve, count, lambda N: finish(n, N))

            groups(dve, group)

        @block.gpsimd
        def _(pool):
            seconds_out = pool.alloc_register(tag + "pool_seconds_out")
            pool.reg_mov(seconds_out, 0)
            nc.gpsimd.memset(ysb[:, :, :], 0.0).then_inc(q["init"], 1)
            nc.gpsimd.iota(idx_out[:, :], pattern=[[0, 2]], base=S, channel_multiplier=1).then_inc(q["pool_copy"], 1)
            pool.wait_ge(q["init"], 2)
            pool.wait_ge(q["pool_copy"], 1)

            def hold(sem, value):
                pool.wait_ge(sem, value)
                pool.sem_inc(q["held"], 1)

            def add_rows(g):
                nc.gpsimd.indirect_dma_start(
                    out=T["out"], out_offset=bass.IndirectOffsetOnAxis(ap=idx_out[:, g:g + 1], axis=0),
                    in_=ysb[:, g, :], in_offset=None, compute_op=ALU.add).then_inc(q[f"scat{g}"], 16)

            def gather(g):
                nc.gpsimd.indirect_dma_start(
                    out=hg[:, g, :], out_offset=None, in_=T["h_rows"],
                    in_offset=bass.IndirectOffsetOnAxis(ap=idx_in[:, g:g + 1], axis=0)).then_inc(q[f"gathered{g}"], 16)

            add_rows(0)
            pool.wait_ge(q["scat0"], 16)
            add_rows(1)

            def fetch(n, e, j, count, copied):
                for g in range(2):
                    slot = e * LIST_K + 2 * j + g
                    nc.gpsimd.tensor_copy(idx_in[:, g:g + 1], T["slots"][:, bass.ds(slot, 1), 0]).then_inc(q["pool_copy"], 1)
                hold(q["pool_copy"], copied)
                gather(0)
                if first:
                    with pool.If(count > P):
                        gather(1)
                else:
                    gather(1)

            def scatter(n, e, j, count, copied):
                hold(q["scat0"], 16 * n + 16)
                hold(q["scat1"], 16 * pool.snap(seconds_out) + 16)
                for g in range(2):
                    slot = e * LIST_K + 2 * j + g
                    nc.gpsimd.tensor_copy(idx_out[:, g:g + 1], T["slots"][:, bass.ds(slot, 1), 0]).then_inc(q["pool_copy"], 1)
                hold(q["pool_copy"], copied)
                hold(q["back_used"], n + 2)
                add_rows(0)

                def second():
                    hold(q["scat0"], 16 * n + 32)
                    add_rows(1)
                    pool.reg_add(seconds_out, seconds_out, 1)

                if first:
                    with pool.If(count > P):
                        second()
                    pool.nop()
                else:
                    second()

            def group(n, e, j, count, ahead):
                if first:
                    hold(q["turned0"], n + 1)
                    hold(q["turned1"], n + 1)
                    if ahead:
                        ahead[0]()
                        fetch(n + 1, e + 1, 0, ahead[1](), 4 * n + 5)
                        scatter(n, e, j, count, 4 * n + 7)
                    else:
                        scatter(n, e, j, count, 4 * n + 5)
                else:
                    fetch(n, e, j, count, 4 * n + 3)
                    scatter(n, e, j, count, 4 * n + 5)

            groups(pool, group, lambda: fetch(0, 0, 0, count_of(pool, 0), 3))
            hold(q["scat0"], 16)
            hold(q["scat1"], 16 * pool.snap(seconds_out) + 16)


HD = 64
RW = 512
NSA_COLS = 1304
QH = 8
HEADS12 = 12
N_CMP = 63
CMP_H = 256
SCALE = HD ** -0.5
NEG = -1e30


def norm_phase(nc, T):
    with ExitStack() as ctx:
        sb = lambda n, s, dt=F32: ctx.enter_context(nc.sbuf_tensor(n, s, dt))
        xt = sb("xt", [P, NT, D])
        junk = sb("n_junk", [P, D])
        st = sb("n_st", [P, 2, NT])
        g1 = sb("n_g1", [P, DC])
        PT = ctx.enter_context(nc.psum_tensor("n_PT", [P, 4, BANK], F32))
        q = sems(nc, ctx, "n_c n_ss n_ms n_sq n_rs n_xn n_tp n_ev_a n_ev_d")
        loaded = sem_list(nc, ctx, [f"n_x{i}" for i in range(NT)])
        block = ctx.enter_context(nc.Block())

        @block.sync
        def _(sp):
            for i in range(NT):
                sp.dma_start(xt[:, i, :], T["x"][0, i * P:(i + 1) * P, :]).then_inc(loaded[i], 16)
            sp.dma_start(T["ident"][:, :], T["c_ident"]).then_inc(q["n_c"], 16)
            sp.dma_start(g1[:, :], T["ln1_cols"]).then_inc(q["n_c"], 16)

        @block.scalar
        def _(act):
            for i in range(NT):
                act.wait_ge(loaded[i], 16)
                if i:
                    act.wait_ge(q["n_ss"], i)
                nc.scalar.activation(junk[:, :], xt[:, i, :], ACT.Square, accum_out=st[:, 0, i:i + 1]).then_inc(q["n_ss"], 1)
            act.wait_ge(q["n_ms"], 1)
            nc.scalar.activation(st[:, 1, :], st[:, 1, :], ACT.Sqrt).then_inc(q["n_sq"], 1)
            act.wait_ge(q["n_c"], 32)
            for u in range(1, 2 * DC, 2):
                act.wait_ge(q["n_tp"], u + 1)
                c, half = u // 2, u % 2
                nc.scalar.activation(T["xnT"][:, c, 1 + half * BANK:1 + (half + 1) * BANK], PT[:, u % 4, :], ACT.Copy,
                                     scale=g1[:, c:c + 1]).then_inc(q["n_ev_a"], 1)

        @block.vector
        def _(dve):
            nc.vector.memset(T["xnT"][:, :, 0], 0.0)
            dve.wait_ge(q["n_ss"], NT)
            nc.vector.tensor_scalar(st[:, 1, :], st[:, 0, :], 1.0 / D, EPS, ALU.mult, ALU.add).then_inc(q["n_ms"], 1)
            dve.wait_ge(q["n_sq"], 1)
            nc.vector.reciprocal(st[:, 0, :], st[:, 1, :]).then_inc(q["n_rs"], 1)
            dve.wait_ge(q["n_rs"], 1)
            for i in range(NT):
                nc.vector.tensor_scalar(xt[:, i, :], xt[:, i, :], st[:, 0, i:i + 1], None, ALU.mult).then_inc(q["n_xn"], 1)
            dve.wait_ge(q["n_c"], 32)
            for u in range(0, 2 * DC, 2):
                dve.wait_ge(q["n_tp"], u + 1)
                c = u // 2
                nc.vector.tensor_scalar(T["xnT"][:, c, 1:1 + BANK], PT[:, u % 4, :], g1[:, c:c + 1], None,
                                        ALU.mult).then_inc(q["n_ev_d"], 1)

        @block.tensor
        def _(pe):
            pe.wait_ge(q["n_c"], 32)
            for u in range(2 * DC):
                c, half = u // 2, u % 2
                pe.wait_ge(q["n_xn"], 4 * half + 4 if u < 2 else NT)
                if u >= 4:
                    pe.wait_ge(q["n_ev_a"] if u % 2 else q["n_ev_d"], (u - 4) // 2 + 1)
                for t in range(4):
                    i = 4 * half + t
                    last = nc.tensor.transpose(PT[:, u % 4, t * P:(t + 1) * P], xt[:, i, c * P:(c + 1) * P], T["ident"][:, :])
                last.then_inc(q["n_tp"], 1)


def nsa_project_phase(nc, T, N):
    with ExitStack() as ctx:
        sb = lambda n, s, dt=F32: ctx.enter_context(nc.sbuf_tensor(n, s, dt))
        pb = lambda n, s: ctx.enter_context(nc.psum_tensor(n, s, F32))
        W = sb("p_W", [P, DC, NSA_COLS])
        heads = sb("p_heads", [P, 2, HEADS12, HD])
        rot = sb("p_rot", [P, 2, HEADS12, HD])
        tmp = sb("p_tmp", [P, HEADS12, HD])
        cmp_in = sb("p_cmpin", [P, 2, 4, 2, HD])
        rotk = sb("p_rotk", [P, 2, 4, 2, HD])
        rs = sb("p_rs", [P, 2, HEADS12])
        ms = sb("p_ms", [P, 2, HEADS12])
        gain = sb("p_gain", [P, 3, HD])
        cos = sb("p_cos", [P, NT, HD // 2])
        sin = sb("p_sin", [P, NT, HD // 2])
        PP = pb("p_PP", [P, 3, BANK])
        PT = pb("p_PT", [P, 4, BANK])
        q = sems(nc, ctx, "p_w p_c p_mm p_eva p_evd p_sum p_sq p_dve p_n p_r p_tp p_out p_gate p_gl")
        block = ctx.enter_context(nc.Block())
        c0 = 3 * RW
        bounds = ((0, 512), (512, 1024), (1024, NSA_COLS))

        @block.sync
        def _(sp):
            for k in range(DC):
                sp.dma_start(W[:, k, :], T["w_in"][0, k * P:(k + 1) * P, c0:c0 + NSA_COLS]).then_inc(q["p_w"], 16)
            sp.dma_start(gain[:, 0, :], T["nsa_qn_g"].broadcast_to([P, HD])).then_inc(q["p_c"], 16)
            for j in (1, 2):
                sp.dma_start(gain[:, j, :], T["nsa_kn_g"][0, j:j + 1, :].broadcast_to([P, HD])).then_inc(q["p_c"], 16)
            sp.dma_start(cos[:, :, :], T["c_cos"].rearrange("(t p) k -> p t k", p=P)).then_inc(q["p_c"], 16)
            sp.dma_start(sin[:, :, :], T["c_sin"].rearrange("(t p) k -> p t k", p=P)).then_inc(q["p_c"], 16)

        @block.tensor
        def _(pe):
            def project(i):
                if i == 0:
                    pe.wait_ge(q["p_w"], 16 * DC)
                else:
                    pe.wait_ge(q["p_eva"], i)
                    pe.wait_ge(q["p_evd"], i)
                for n, (a, b) in enumerate(bounds):
                    for k in range(DC):
                        last = nc.tensor.matmul(PP[:, n, 0:b - a], T["xnT"][:, k, 1 + i * P:1 + (i + 1) * P], W[:, k, a:b],
                                                start=(k == 0), stop=(k == DC - 1))
                last.then_inc(q["p_mm"], 1)

            def transposes(i):
                s = i % 2
                pe.wait_ge(q["p_n"], i + 1)
                pe.wait_ge(q["p_r"], i + 1)
                pe.wait_ge(q["p_eva"], i + 1)
                if i:
                    pe.wait_ge(q["p_out"], 5 * i)
                twice = lambda v: v.rearrange("p a b -> p (a b)")
                for p in range(4):
                    nc.tensor.transpose(PT[:, 0, p * P:(p + 1) * P],
                                        heads[:, s, 2 * p:2 * p + 2, :].rearrange("p a b -> p (a b)"), T["ident"][:, :])
                    nc.tensor.transpose(PT[:, 1, p * P:(p + 1) * P],
                                        rot[:, s, 2 * p:2 * p + 2, :].rearrange("p a b -> p (a b)"), T["ident"][:, :])
                    nc.tensor.transpose(PT[:, 2, p * P:(p + 1) * P], twice(rotk[:, s, p, :, :]), T["ident"][:, :])
                    last = nc.tensor.transpose(PT[:, 3, p * P:(p + 1) * P],
                                               twice(cmp_in[:, s, p, :, :]), T["ident"][:, :])
                last.then_inc(q["p_tp"], 1)

            project(0)
            for i in range(NT):
                if i + 1 < NT:
                    project(i + 1)
                transposes(i)

        @block.scalar
        def _(act):
            for i in range(NT):
                s = i % 2
                act.wait_ge(q["p_mm"], i + 1)
                if i >= 2:
                    act.wait_ge(q["p_tp"], i - 1)
                for c in range(2):
                    nc.scalar.activation(cmp_in[:, s, :, c, :], PP[:, 1, 0:256].rearrange("p (a b) -> p a b", b=HD), ACT.Copy)
                nc.scalar.activation(heads[:, s, 8:10, :].rearrange("p a b -> p (a b)"), PP[:, 1, 256:384], ACT.Copy)
                nc.scalar.activation(heads[:, s, 10:12, :].rearrange("p a b -> p (a b)"), PP[:, 2, 0:128], ACT.Copy)
                nc.scalar.activation(N["vs"][:, i, :], PP[:, 1, 384:512], ACT.Copy)
                nc.scalar.activation(N["vw"][:, i, :], PP[:, 2, 128:256], ACT.Copy)
                nc.scalar.activation(N["gates"][:, i, :], PP[:, 2, 256:280], ACT.Copy).then_inc(q["p_eva"], 1)
                act.wait_ge(q["p_sum"], i + 1)
                nc.scalar.activation(rs[:, s, :], ms[:, s, :], ACT.Sqrt).then_inc(q["p_sq"], 1)
                act.wait_ge(q["p_tp"], i + 1)
                tok = slice(i * P, (i + 1) * P)
                view = lambda g: PT[:, g, :].rearrange("p (a b) -> p a b", b=P)
                nc.scalar.activation(N["qT"][:, :, tok], view(0), ACT.Copy).then_inc(q["p_out"], 1)
                nc.scalar.activation(N["qrT"][:, :, tok], view(1), ACT.Copy).then_inc(q["p_out"], 1)
                nc.scalar.activation(N["kT"][:, :, tok], view(2), ACT.Copy).then_inc(q["p_out"], 1)
                nc.scalar.activation(N["cT"][0:HD, :, 1 + i * P:1 + (i + 1) * P], PT[0:HD, 3, :].rearrange("p (a b) -> p a b", b=P),
                                     ACT.Copy).then_inc(q["p_out"], 1)
                nc.scalar.activation(N["cT"][HD:P, :, i * P:(i + 1) * P], PT[HD:P, 3, :].rearrange("p (a b) -> p a b", b=P),
                                     ACT.Copy).then_inc(q["p_out"], 1)
            act.wait_ge(q["p_eva"], NT)
            nc.scalar.activation(N["gates"][:, :, :], N["gates"][:, :, :], ACT.Sigmoid)

        @block.vector
        def _(dve):
            link = chained(dve, q["p_dve"])
            dve.wait_ge(q["p_c"], 16 * 5)
            for i in range(NT):
                s = i % 2
                H = heads[:, s, :, :]
                dve.wait_ge(q["p_mm"], i + 1)
                if i >= 2:
                    dve.wait_ge(q["p_tp"], i - 1)
                nc.vector.tensor_copy(heads[:, s, 0:8, :].rearrange("p a b -> p (a b)"), PP[:, 0, :]).then_inc(q["p_evd"], 1)
                dve.wait_ge(q["p_evd"], i + 1)
                dve.wait_ge(q["p_eva"], i + 1)
                link(nc.vector.tensor_tensor(tmp[:, :, :], H, H, ALU.mult))
                link(nc.vector.tensor_reduce(ms[:, s, :], tmp[:, :, :], AX.X, ALU.add))
                nc.vector.tensor_scalar(ms[:, s, :], ms[:, s, :], 1.0 / HD, EPS, ALU.mult, ALU.add).then_inc(q["p_sum"], 1)
                dve.wait_ge(q["p_sq"], i + 1)
                link(nc.vector.reciprocal(rs[:, s, :], rs[:, s, :]))
                link(nc.vector.tensor_tensor(H, H, rs[:, s, :, None].broadcast_to([P, HEADS12, HD]), ALU.mult))
                for j, (a, b) in enumerate(((0, QH), (QH, QH + 2), (QH + 2, HEADS12))):
                    last = nc.vector.tensor_tensor(H[:, a:b, :], H[:, a:b, :], gain[:, j, None, :].broadcast_to([P, b - a, HD]),
                                                   ALU.mult)
                last.then_inc(q["p_n"], 1)
                dve.wait_ge(q["p_n"], i + 1)
                half = HD // 2
                lo, hi = H[:, :, 0:half], H[:, :, half:HD]
                cs = cos[:, i, None, :].broadcast_to([P, HEADS12, half])
                sn = sin[:, i, None, :].broadcast_to([P, HEADS12, half])
                R = rot[:, s, :, :]
                link(nc.vector.tensor_tensor(tmp[:, :, 0:half], hi, sn, ALU.mult))
                link(nc.vector.tensor_tensor(tmp[:, :, half:HD], lo, sn, ALU.mult))
                link(nc.vector.tensor_tensor(R[:, :, 0:half], lo, cs, ALU.mult))
                link(nc.vector.tensor_tensor(R[:, :, half:HD], hi, cs, ALU.mult))
                link(nc.vector.tensor_tensor(R[:, :, 0:half], R[:, :, 0:half], tmp[:, :, 0:half], ALU.subtract))
                link(nc.vector.tensor_tensor(R[:, :, half:HD], R[:, :, half:HD], tmp[:, :, half:HD], ALU.add))
                nc.vector.tensor_copy(rotk[:, s, :, 0, :], R[:, QH:HEADS12, :])
                nc.vector.tensor_copy(rotk[:, s, :, 1, :], R[:, QH:HEADS12, :]).then_inc(q["p_r"], 1)
                dve.wait_ge(q["p_r"], i + 1)


def compress_phase(nc, T, N):
    with ExitStack() as ctx:
        sb = lambda n, s, dt=F32: ctx.enter_context(nc.sbuf_tensor(n, s, dt))
        pb = lambda n, s: ctx.enter_context(nc.psum_tensor(n, s, F32))
        W1 = sb("c_W1", [P, 2, 16, CMP_H])
        W2 = sb("c_W2", [P, 2, 2, HD])
        pe_rows = sb("c_pe", [32, P])
        peT = sb("c_peT", [P, 32])
        bias = sb("c_bias", [P, 4])
        hid = sb("c_hid", [P, 4, 2 * N_CMP])
        kg = sb("c_kg", [N_CMP, HD])
        kc = sb("c_kc", [N_CMP, 2, HD])
        kc2 = sb("c_kc2", [N_CMP, 2, 2, HD])
        tmp = sb("c_tmp", [N_CMP, 2, HD])
        ms = sb("c_ms", [N_CMP, 2])
        PH = pb("c_PH", [P, 4, BANK])
        PB = pb("c_PB", [P, BANK])
        PO = pb("c_PO", [P, BANK])
        PT = pb("c_PT", [P, BANK])
        q = sems(nc, ctx, "c_w c_pet c_pete c_b c_be c_h c_g c_o c_v c_ms c_sq c_k c_kt c_dve")
        block = ctx.enter_context(nc.Block())

        @block.sync
        def _(sp):
            for i in range(2):
                sp.dma_start(W1[:, i, :, :], T["nsa_cmp_w1"][0, i].rearrange("(m two) d f -> (two d) m f", two=2)).then_inc(q["c_w"], 16)
                sp.dma_start(W2[:, i, :, :], T["nsa_cmp_w2"][0, i].rearrange("(c p) d -> p c d", p=P)).then_inc(q["c_w"], 16)
            sp.dma_start(pe_rows[:, :], T["nsa_pe"][0].rearrange("i (m two) d -> (i m) (two d)", two=2)).then_inc(q["c_w"], 16)
            sp.dma_start(kg[:, :], T["nsa_kn_g"][0, 0:1, :].broadcast_to([N_CMP, HD])).then_inc(q["c_w"], 16)

        @block.tensor
        def _(pe):
            pe.wait_ge(q["c_w"], 16 * 6)
            nc.tensor.transpose(PT[:, 0:32], pe_rows[:, :], T["ident"][0:32, 0:32]).then_inc(q["c_pet"], 1)
            pe.wait_ge(q["c_pete"], 1)
            for i in range(2):
                for f in range(2):
                    u = 2 * i + f
                    for m in range(16):
                        w = W1[:, i, m, f * P:(f + 1) * P]
                        last = nc.tensor.matmul(PB[:, u:u + 1], w, peT[:, 16 * i + m:16 * i + m + 1],
                                                start=(m == 0), stop=(m == 15))
            last.then_inc(q["c_b"], 1)
            for i in range(2):
                for f in range(2):
                    u = 2 * i + f
                    for m in range(16):
                        last = nc.tensor.matmul(PH[:, u, 0:2 * N_CMP], W1[:, i, m, f * P:(f + 1) * P],
                                                N["cT"][:, 2 * i:2 * i + 2, 1 + 2 * m:1 + 2 * m + 16 * (N_CMP - 1) + 1:16],
                                                start=(m == 0), stop=(m == 15))
                    last.then_inc(q["c_h"], 1)
            pe.wait_ge(q["c_g"], 4)
            for i in range(2):
                for h in range(2):
                    u = 2 * i + h
                    for f in range(2):
                        last = nc.tensor.matmul(PO[0:N_CMP, u * HD:(u + 1) * HD],
                                                hid[:, 2 * i + f, h * N_CMP:(h + 1) * N_CMP], W2[:, i, f, :],
                                                start=(f == 0), stop=(f == 1))
            last.then_inc(q["c_o"], 1)
            pe.wait_ge(q["c_k"], 1)
            for h in range(2):
                last = nc.tensor.transpose(PT[:, BANK // 2 + h * N_CMP:BANK // 2 + (h + 1) * N_CMP],
                                           kc2[:, h, :, :].rearrange("p a b -> p (a b)"), T["ident"][0:N_CMP, 0:N_CMP])
            last.then_inc(q["c_kt"], 1)

        @block.scalar
        def _(act):
            act.wait_ge(q["c_be"], 1)
            for u in range(4):
                act.wait_ge(q["c_h"], u + 1)
                nc.scalar.activation(hid[:, u, :], PH[:, u, 0:2 * N_CMP], ACT.Gelu_apprx_tanh,
                                     bias=bias[:, u:u + 1]).then_inc(q["c_g"], 1)
            act.wait_ge(q["c_ms"], 1)
            nc.scalar.activation(ms[:, :], ms[:, :], ACT.Sqrt).then_inc(q["c_sq"], 1)

        @block.vector
        def _(dve):
            link = chained(dve, q["c_dve"])
            dve.wait_ge(q["c_pet"], 1)
            nc.vector.tensor_copy(peT[:, :], PT[:, 0:32]).then_inc(q["c_pete"], 1)
            dve.wait_ge(q["c_b"], 1)
            nc.vector.tensor_copy(bias[:, :], PB[:, 0:4]).then_inc(q["c_be"], 1)
            dve.wait_ge(q["c_o"], 1)
            link(nc.vector.tensor_copy(kc[:, :, :], PO[0:N_CMP, 0:2 * HD].rearrange("p (a b) -> p a b", b=HD)))
            nc.vector.tensor_copy(N["vcmp"][:, :, :], PO[0:N_CMP, 2 * HD:4 * HD].rearrange("p (a b) -> p a b", b=HD))
            link(nc.vector.tensor_tensor(tmp[:, :, :], kc[:, :, :], kc[:, :, :], ALU.mult))
            link(nc.vector.tensor_reduce(ms[:, :], tmp[:, :, :], AX.X, ALU.add))
            nc.vector.tensor_scalar(ms[:, :], ms[:, :], 1.0 / HD, EPS, ALU.mult, ALU.add).then_inc(q["c_ms"], 1)
            dve.wait_ge(q["c_sq"], 1)
            link(nc.vector.reciprocal(ms[:, :], ms[:, :]))
            link(nc.vector.tensor_tensor(kc[:, :, :], kc[:, :, :], ms[:, :, None].broadcast_to([N_CMP, 2, HD]), ALU.mult))
            for c in range(2):
                last = nc.vector.tensor_tensor(kc2[:, :, c, :], kc[:, :, :], kg[:, None, :].broadcast_to([N_CMP, 2, HD]),
                                               ALU.mult)
            last.then_inc(q["c_k"], 1)
            dve.wait_ge(q["c_kt"], 1)
            nc.vector.tensor_copy(N["kcT"][:, :, :], PT[:, BANK // 2:BANK // 2 + 2 * N_CMP].rearrange("p (a b) -> p a b", b=N_CMP))


def attention_phase(nc, T, N):
    KW = S + 3 * P
    with ExitStack() as ctx:
        sb = lambda n, s, dt=F32: ctx.enter_context(nc.sbuf_tensor(n, s, dt))
        pb = lambda n, s: ctx.enter_context(nc.psum_tensor(n, s, F32))
        cmask = sb("a_cmask", [P, NT, N_CMP])
        cpen = sb("a_cpen", [P, NT, N_CMP])
        wpen = sb("a_wpen", [P, 3 * P])
        free16 = sb("a_free", [P, NT, 16])
        force16 = sb("a_force", [P, NT, 16])
        lower16 = sb("a_lower", [P, 16, 16])
        sc = sb("a_sc", [P, 4, N_CMP])
        pc = sb("a_pc", [P, 4, N_CMP])
        pcT = sb("a_pcT", [N_CMP, 4, P])
        small = sb("a_small", [P, 4, 4])
        ps = sb("a_ps", [P, 65])
        imp = sb("a_imp", [P, 16])
        c1 = sb("a_c1", [P, 16, 16])
        c2 = sb("a_c2", [P, 16, 16])
        bpen = sb("a_bpen", [P, 16])
        pen = sb("a_pen", [P, S])
        Sc = sb("a_S", [P, 3, KW])
        pT = sb("a_pT", [P, 2, 11, P])
        mm = sb("a_mm", [P, 3, 2])
        nm = sb("a_nm", [P, 3, 2])
        dn = sb("a_dn", [P, 3, 2])
        rd = sb("a_rd", [P, 3, 2])
        oN = sb("a_oN", [P, 2, QH, HD])
        gsc = sb("a_gsc", [P, 3, 2])
        PSel = pb("a_PSel", [P, 3, BANK])
        PC = pb("a_PC", [P, BANK])
        PT = pb("a_PT", [P, 2, BANK])
        POc = pb("a_POc", [P, BANK])
        PO = pb("a_PO", [P, BANK])
        q = sems(nc, ctx, "a_c a_cs a_csd a_cm a_ce a_cp a_ct a_cte a_co a_cod a_sp a_sd a_m a_e a_tp a_te a_po "
                          "a_pod a_od a_oT a_oTe a_dve a_half")
        block = ctx.enter_context(nc.Block())
        steps = [(i, kv) for i in range(NT) for kv in range(2)]

        def banks_of(i):
            tiles = [(j, S * 0 + j) for j in range(i + 1)]
            wins = [j for j in range(max(0, i - 2), i + 1)]
            cols = [("s", j, j * P) for j, _ in tiles] + [("w", j, S + (j - i + 2) * P) for j in wins]
            return [cols[a:a + 4] for a in range(0, len(cols), 4)]

        heads = [(i, kv, g) for i, kv in steps for g in range(4)]
        group_base = {}
        n = 0
        for u, (i, kv, g) in enumerate(heads):
            group_base[u] = n
            n += len(banks_of(i))

        @block.sync
        def _(sp):
            for dst, src in ((cmask, T["c_cmask"]), (cpen, T["c_cpen"]), (free16, T["c_free"]), (force16, T["c_force"])):
                sp.dma_start(dst[:, :, :], src.rearrange("(t p) n -> p t n", p=P)).then_inc(q["a_c"], 16)
            sp.dma_start(wpen[:, :], T["c_wpen"]).then_inc(q["a_c"], 16)
            sp.dma_start(lower16[:, :, :].rearrange("p a b -> p (a b)"), T["c_lower16"].broadcast_to([P, 256])).then_inc(q["a_c"], 16)

        @block.tensor
        def _(pe):
            def cmp_scores(s):
                i, kv = steps[s]
                if s:
                    pe.wait_ge(q["a_csd"], s)
                    pe.wait_ge(q["a_cod"], s)
                for g in (0, 2, 1, 3):
                    h = 4 * kv + g
                    r = slice(HD * (h % 2), HD * (h % 2) + HD)
                    if g == 1:
                        last.then_inc(q["a_half"], 1)
                        pe.wait_ge(q["a_half"], s + 1)
                    last = nc.tensor.matmul(PC[:, g * HD:g * HD + N_CMP], N["qT"][r, h // 2, i * P:(i + 1) * P],
                                            N["kcT"][r, kv, :], start=True, stop=True)
                last.then_inc(q["a_cs"], 1)

            def cmp_turn(s):
                i, kv = steps[s]
                pe.wait_ge(q["a_cp"], s + 1)
                turned = i - 1 if kv == 0 else i
                if turned > 0:
                    pe.wait_ge(q["a_oTe"], turned)
                for g in range(4):
                    last = nc.tensor.transpose(POc[0:N_CMP, g * P:(g + 1) * P], pc[:, g, :], T["ident"][:, :])
                last.then_inc(q["a_ct"], 1)

            def cmp_out(s):
                i, kv = steps[s]
                pe.wait_ge(q["a_cte"], s + 1)
                for g in range(4):
                    last = nc.tensor.matmul(PC[:, 256 + g * HD:256 + (g + 1) * HD], pcT[:, g, :], N["vcmp"][:, kv, :],
                                            start=True, stop=True)
                last.then_inc(q["a_co"], 1)

            def scores(u):
                i, kv, g = heads[u]
                h = 4 * kv + g
                r = slice(HD * (h % 2), HD * (h % 2) + HD)
                if u:
                    pe.wait_ge(q["a_sd"], u)
                lhs = N["qrT"][r, h // 2, i * P:(i + 1) * P]
                for b in range(0, (i + 1) * P, BANK):
                    n = min(BANK, (i + 1) * P - b)
                    nc.tensor.matmul(PSel[:, b // BANK, 0:n], lhs, N["kT"][r, kv, b:b + n], start=True, stop=True)
                lo = max(0, i - 2)
                last = nc.tensor.matmul(PSel[:, 2, (lo - i + 2) * P:3 * P], lhs, N["kT"][r, 2 + kv, lo * P:(i + 1) * P],
                                        start=True, stop=True)
                last.then_inc(q["a_sp"], 1)

            def turn(u, n):
                i, kv, g = heads[u]
                at = group_base[u] + n
                if n == 0:
                    pe.wait_ge(q["a_e"], 2 * u + 2)
                if at >= 2:
                    pe.wait_ge(q["a_te"], at - 1)
                for c, (_, _, col) in enumerate(banks_of(i)[n]):
                    last = nc.tensor.transpose(PT[:, at % 2, c * P:(c + 1) * P], Sc[:, u % 3, col:col + P], T["ident"][:, :])
                last.then_inc(q["a_tp"], 1)

            def values(u, kind):
                i, kv, g = heads[u]
                if kind == "s":
                    if u:
                        pe.wait_ge(q["a_pod"], u)
                    pe.wait_ge(q["a_te"], group_base[u] + len(banks_of(i)))
                flat = [x for grp in banks_of(i) for x in grp]
                V, dst = (N["vs"], 0) if kind == "s" else (N["vw"], HD)
                mine = [(c, j) for c, (k, j, _) in enumerate(flat) if k == kind]
                for m, (c, j) in enumerate(mine):
                    last = nc.tensor.matmul(PO[:, dst:dst + HD], pT[:, u % 2, c, :], V[:, j, kv * HD:(kv + 1) * HD],
                                            start=(m == 0), stop=(m == len(mine) - 1))
                if kind == "w":
                    last.then_inc(q["a_po"], 1)

            def turn_out(i):
                pe.wait_ge(q["a_od"], i + 1)
                pe.wait_ge(q["a_cte"], min(2 * i + 3, len(steps)) - 1)
                for p in range(4):
                    last = nc.tensor.transpose(POc[:, p * P:(p + 1) * P],
                                               oN[:, i % 2, 2 * p:2 * p + 2, :].rearrange("p a b -> p (a b)"), T["ident"][:, :])
                last.then_inc(q["a_oT"], 1)

            cmp_scores(0)
            cmp_turn(0)
            cmp_out(0)
            for u in range(-2, len(heads)):
                if u + 2 < len(heads):
                    scores(u + 2)
                groups = len(banks_of(heads[u + 1][0])) if -1 <= u + 1 < len(heads) and u + 1 >= 0 else 0
                for n in range(min(2, groups)):
                    turn(u + 1, n)
                if u >= 0:
                    i, kv, g = heads[u]
                    s = u // 4
                    more = s + 1 < len(steps)
                    if g == 0 and more:
                        cmp_scores(s + 1)
                    if g == 2 and more:
                        cmp_turn(s + 1)
                    values(u, "s")
                for n in range(2, groups):
                    turn(u + 1, n)
                if u >= 0:
                    if g == 3 and more:
                        cmp_out(s + 1)
                    values(u, "w")
                    if g == 0 and kv == 0 and i:
                        turn_out(i - 1)
            turn_out(NT - 1)

        @block.scalar
        def _(act):
            def cmp_exp(s):
                act.wait_ge(q["a_cm"], s + 1)
                for g in range(4):
                    last = nc.scalar.activation(sc[:, g, :], sc[:, g, :], ACT.Exp, bias=small[:, 1, g:g + 1])
                last.then_inc(q["a_ce"], 1)

            def cmp_evac(s):
                act.wait_ge(q["a_ct"], s + 1)
                if s:
                    act.wait_ge(q["a_co"], s)
                nc.scalar.activation(pcT[:, :, :], POc[0:N_CMP, :].rearrange("p (a b) -> p a b", b=P),
                                     ACT.Copy).then_inc(q["a_cte"], 1)

            def exps(u):
                i, kv, g = heads[u]
                b = u % 3
                act.wait_ge(q["a_m"], u + 1)
                nc.scalar.activation(Sc[:, b, 0:(i + 1) * P], Sc[:, b, 0:(i + 1) * P], ACT.Exp, bias=nm[:, b, 0:1],
                                     accum_out=dn[:, b, 0:1]).then_inc(q["a_e"], 1)
                lo = S + (max(0, i - 2) - i + 2) * P
                nc.scalar.activation(Sc[:, b, lo:KW], Sc[:, b, lo:KW], ACT.Exp, bias=nm[:, b, 1:2],
                                     accum_out=dn[:, b, 1:2]).then_inc(q["a_e"], 1)

            def evacs(u):
                i, kv, g = heads[u]
                if u >= 2:
                    act.wait_ge(q["a_po"], u - 1)
                for n, grp in enumerate(banks_of(i)):
                    at = group_base[u] + n
                    act.wait_ge(q["a_tp"], at + 1)
                    nc.scalar.activation(pT[:, u % 2, 4 * n:4 * n + len(grp), :],
                                         PT[:, at % 2, 0:len(grp) * P].rearrange("p (a b) -> p a b", b=P),
                                         ACT.Copy).then_inc(q["a_te"], 1)

            def out_evac(i):
                act.wait_ge(q["a_oT"], i + 1)
                nc.scalar.activation(T["yT"][:, 4:8, i * P:(i + 1) * P], POc[:, :].rearrange("p (a b) -> p a b", b=P),
                                     ACT.Copy).then_inc(q["a_oTe"], 1)

            cmp_exp(0)
            cmp_evac(0)
            for u in range(-2, len(heads)):
                if 0 <= u + 1 < len(heads):
                    evacs(u + 1)
                if u >= 0:
                    i, kv, g = heads[u]
                    s = u // 4
                    if g == 2 and s + 1 < len(steps):
                        cmp_evac(s + 1)
                if u + 2 < len(heads):
                    exps(u + 2)
                if u >= 0:
                    if g == 1 and s + 1 < len(steps):
                        cmp_exp(s + 1)
                    if g == 0 and kv == 0 and i:
                        out_evac(i - 1)
            out_evac(NT - 1)

        @block.vector
        def _(dve):
            link = chained(dve, q["a_dve"])
            dve.wait_ge(q["a_c"], 16 * 6)
            link(nc.vector.memset(ps[:, :], 0.0))

            def cmp_masked(s):
                i, kv = steps[s]
                dve.wait_ge(q["a_cs"], s + 1)
                view = PC[:, 0:4 * HD].rearrange("p (a b) -> p a b", b=HD)[:, :, 0:N_CMP]
                nc.vector.scalar_tensor_tensor(out=sc[:, :, :], in0=view, scalar=SCALE,
                                               in1=cpen[:, i, None, :].broadcast_to([P, 4, N_CMP]),
                                               op0=ALU.mult, op1=ALU.add).then_inc(q["a_csd"], 1)
                dve.wait_ge(q["a_csd"], s + 1)
                link(nc.vector.tensor_reduce(small[:, 0, :], sc[:, :, :], AX.X, ALU.max))
                nc.vector.tensor_scalar(small[:, 1, :], small[:, 0, :], -1.0, None, ALU.mult).then_inc(q["a_cm"], 1)

            def cmp_norm(s):
                i, kv = steps[s]
                dve.wait_ge(q["a_ce"], s + 1)
                if s:
                    dve.wait_ge(q["a_ct"], s)
                link(nc.vector.tensor_tensor(sc[:, :, :], sc[:, :, :], cmask[:, i, None, :].broadcast_to([P, 4, N_CMP]),
                                             ALU.mult))
                link(nc.vector.tensor_reduce(small[:, 2, :], sc[:, :, :], AX.X, ALU.add))
                link(nc.vector.tensor_scalar(small[:, 2, :], small[:, 2, :], 1e-30, None, ALU.max))
                link(nc.vector.reciprocal(small[:, 3, :], small[:, 2, :]))
                nc.vector.tensor_tensor(pc[:, :, :], sc[:, :, :], small[:, 3, :, None].broadcast_to([P, 4, N_CMP]),
                                        ALU.mult).then_inc(q["a_cp"], 1)
                dve.wait_ge(q["a_cp"], s + 1)

            def select(s):
                i, kv = steps[s]
                keys = (i + 1) * P
                causal = wpen[:, 2 * P:3 * P]
                if i < 4:
                    link(nc.vector.memset(bpen[:, :], 0.0))
                else:
                    link(nc.vector.tensor_reduce(ps[:, 1:64], pc[:, :, :].rearrange("p a b -> p b a"), AX.X, ALU.add))
                    link(nc.vector.tensor_reduce(imp[:, :], ps[:, 0:64].rearrange("p (a b) -> p a b", b=4), AX.X, ALU.add))
                    link(nc.vector.tensor_tensor(imp[:, :], imp[:, :], ps[:, 4:65:4], ALU.add))
                    link(nc.vector.tensor_tensor(imp[:, :], imp[:, :], free16[:, i, :], ALU.mult))
                    link(nc.vector.tensor_tensor(imp[:, :], imp[:, :], force16[:, i, :], ALU.add))
                    other = imp[:, None, :].broadcast_to([P, 16, 16])
                    own = imp[:, :, None].broadcast_to([P, 16, 16])
                    link(nc.vector.tensor_tensor(c1[:, :, :], other, own, ALU.is_gt))
                    link(nc.vector.tensor_tensor(c2[:, :, :], other, own, ALU.is_equal))
                    link(nc.vector.tensor_tensor(c2[:, :, :], c2[:, :, :], lower16[:, :, :], ALU.mult))
                    link(nc.vector.tensor_tensor(c1[:, :, :], c1[:, :, :], c2[:, :, :], ALU.add))
                    link(nc.vector.tensor_reduce(bpen[:, :], c1[:, :, :], AX.X, ALU.add))
                    link(nc.vector.tensor_scalar(bpen[:, :], bpen[:, :], 7.5, NEG, ALU.is_gt, ALU.mult))
                nb = keys // HD
                link(nc.vector.tensor_copy(pen[:, 0:keys].rearrange("p (a b) -> p a b", b=HD),
                                           bpen[:, 0:nb, None].broadcast_to([P, nb, HD])))
                link(nc.vector.tensor_tensor(pen[:, i * P:keys], pen[:, i * P:keys], causal, ALU.add))

            def masked(u):
                i, kv, g = heads[u]
                b = u % 3
                keys = (i + 1) * P
                lo = (max(0, i - 2) - i + 2) * P
                dve.wait_ge(q["a_sp"], u + 1)
                nc.vector.scalar_tensor_tensor(
                    out=Sc[:, b, 0:keys], in0=PSel[:, 0:2, :].rearrange("p a b -> p (a b)")[:, 0:keys], scalar=SCALE,
                    in1=pen[:, 0:keys], op0=ALU.mult, op1=ALU.add)
                nc.vector.scalar_tensor_tensor(out=Sc[:, b, S + lo:KW], in0=PSel[:, 2, lo:3 * P], scalar=SCALE,
                                               in1=wpen[:, lo:3 * P], op0=ALU.mult, op1=ALU.add).then_inc(q["a_sd"], 1)
                dve.wait_ge(q["a_sd"], u + 1)
                nc.vector.tensor_reduce(mm[:, b, 0:1], Sc[:, b, 0:keys], AX.X, ALU.max)
                link(nc.vector.tensor_reduce(mm[:, b, 1:2], Sc[:, b, S + lo:KW], AX.X, ALU.max))
                nc.vector.tensor_scalar(nm[:, b, :], mm[:, b, :], -1.0, None, ALU.mult).then_inc(q["a_m"], 1)

            def combine(u):
                i, kv, g = heads[u]
                h = 4 * kv + g
                b = u % 3
                o = oN[:, i % 2, h, :]
                dve.wait_ge(q["a_e"], 2 * u + 2)
                link(nc.vector.reciprocal(rd[:, b, :], dn[:, b, :]))
                link(nc.vector.tensor_tensor(gsc[:, b, :], rd[:, b, :], N["gates"][:, i, 3 * h + 1:3 * h + 3], ALU.mult))
                dve.wait_ge(q["a_po"], u + 1)
                link(nc.vector.scalar_tensor_tensor(out=o, in0=PO[:, 0:HD], scalar=gsc[:, b, 0:1], in1=o,
                                                    op0=ALU.mult, op1=ALU.add))
                nc.vector.scalar_tensor_tensor(out=o, in0=PO[:, HD:2 * HD], scalar=gsc[:, b, 1:2], in1=o,
                                               op0=ALU.mult, op1=ALU.add).then_inc(q["a_pod"], 1)
                dve.wait_ge(q["a_pod"], u + 1)

            def cmp_combine(s):
                i, kv = steps[s]
                dve.wait_ge(q["a_co"], s + 1)
                if i >= 2 and kv == 0:
                    dve.wait_ge(q["a_oT"], i - 1)
                for g in range(4):
                    h = 4 * kv + g
                    last = nc.vector.tensor_scalar(oN[:, i % 2, h, :], PC[:, 256 + g * HD:256 + (g + 1) * HD],
                                                   N["gates"][:, i, 3 * h:3 * h + 1], None, ALU.mult)
                last.then_inc(q["a_cod"], 1)
                dve.wait_ge(q["a_cod"], s + 1)

            cmp_masked(0)
            cmp_norm(0)
            select(0)
            cmp_combine(0)
            for u in range(-2, len(heads)):
                if u + 2 < len(heads):
                    masked(u + 2)
                if u >= 0:
                    i, kv, g = heads[u]
                    s = u // 4
                    more = s + 1 < len(steps)
                    combine(u)
                    if g == 0 and more:
                        cmp_masked(s + 1)
                    if g == 1 and more:
                        cmp_norm(s + 1)
                        select(s + 1)
                    if g == 3 and more:
                        cmp_combine(s + 1)
                    if g == 3 and kv == 1:
                        dve.sem_inc(q["a_od"], 1)


HD = 64
RW = 512
PAIRS = 4
CH = 64
NCH = S // CH
LEVELS = 5
LAG = 4
LNX_EPS = 64e-5
E_HALF = float(np.exp(-0.5))
(MU_R, MU_K, MU_V, W0, A0, K_K, K_A, R_K) = range(8)


def lora_phase(nc, T, R):
    with ExitStack() as ctx:
        sb = lambda n, s, dt=F32: ctx.enter_context(nc.sbuf_tensor(n, s, dt))
        wl = sb("l_w", [P, DC, 256])
        wb = sb("l_wb", [P, DC, 256])
        mu = sb("l_mu", [P, 3, DC])
        PH = ctx.enter_context(nc.psum_tensor("l_PH", [P, 4, BANK], F32))
        q = sems(nc, ctx, "l_ld l_d l_m")
        block = ctx.enter_context(nc.Block())
        parts = ((0, 0, 64), (1, 64, 128), (2, 128, 256))

        @block.sync
        def _(sp):
            for (_, a, b), src in zip(parts, (T["rw_w1"], T["rw_a1"], T["rw_g1"])):
                sp.dma_start(wl[:, :, a:b], src[0].rearrange("(k p) f -> p k f", p=P)).then_inc(q["l_ld"], 16)
            sp.dma_start(mu[:, :, :], T["mu_wag_cols"]).then_inc(q["l_ld"], 16)
            sp.dma_start(R["cols"][:, :, :], T["rw_cols"]).then_inc(q["l_ld"], 16)
            sp.dma_start(R["w2a2"][0:64, :], T["rw_w2"][0]).then_inc(q["l_ld"], 16)
            sp.dma_start(R["w2a2"][64:P, :], T["rw_a2"][0]).then_inc(q["l_ld"], 16)
            sp.dma_start(R["g2"][:, :], T["rw_g2"][0]).then_inc(q["l_ld"], 16)
            sp.dma_start(R["lng"][:, :], T["rw_lnx_g"].broadcast_to([P, RW])).then_inc(q["l_ld"], 16)
            sp.dma_start(R["lnb"][:, :], T["rw_lnx_b"].broadcast_to([P, RW])).then_inc(q["l_ld"], 16)
            sp.dma_start(R["masks"][:, :, :], T["c_masks"]).then_inc(q["l_ld"], 16)
            sp.dma_start(R["blockones"][:, :], T["c_blockones"]).then_inc(q["l_ld"], 16)
            sp.dma_start(R["ident2"][:, :], T["c_ident2"]).then_inc(q["l_ld"], 16)

        @block.vector
        def _(dve):
            dve.wait_ge(q["l_ld"], 16 * 13)
            for j, a, b in parts:
                last = nc.vector.tensor_tensor(wb[:, :, a:b], wl[:, :, a:b], mu[:, j, :, None].broadcast_to([P, DC, b - a]),
                                               ALU.mult)
            last.then_inc(q["l_d"], 1)
            dve.wait_ge(q["l_d"], 1)
            nc.vector.tensor_tensor(wl[:, :, :], wl[:, :, :], wb[:, :, :], ALU.subtract).then_inc(q["l_d"], 1)
            nc.vector.tensor_scalar(R["omcols"][:, :, :], R["cols"][:, :, :], -1.0, 1.0, ALU.mult, ALU.add)

        @block.tensor
        def _(pe):
            pe.wait_ge(q["l_d"], 2)
            for m in range(2):
                for n in range(2):
                    for k in range(DC):
                        nc.tensor.matmul(PH[:, 2 * m + n, :], wl[:, k, m * P:(m + 1) * P],
                                         T["xnT"][:, k, 1 + n * BANK:1 + (n + 1) * BANK], start=(k == 0), stop=False)
                        last = nc.tensor.matmul(PH[:, 2 * m + n, :], wb[:, k, m * P:(m + 1) * P],
                                                T["xnT"][:, k, n * BANK:(n + 1) * BANK], start=False, stop=(k == DC - 1))
                last.then_inc(q["l_m"], 1)

        @block.scalar
        def _(act):
            act.wait_ge(q["l_m"], 1)
            hid = PH[:, 0:2, :].rearrange("p a b -> p (a b)")
            nc.scalar.activation(R["hwa"][0:64, :], hid[0:64, :], ACT.Tanh)
            nc.scalar.activation(R["hwa"][64:P, :], hid[64:P, :], ACT.Copy)
            act.wait_ge(q["l_m"], 2)
            nc.scalar.activation(R["hg"][:, :], PH[:, 2:4, :].rearrange("p a b -> p (a b)"), ACT.Sigmoid)


def features_phase(nc, T, R, F, p):
    with ExitStack() as ctx:
        sb = lambda n, s, dt=F32: ctx.enter_context(nc.sbuf_tensor(f"f{p}_{n}", s, dt))
        W = sb("W", [P, DC, 3, P])
        raw = sb("raw", [P, 3, S + 1])
        mix = sb("mix", [P, 3, S])
        tmp = sb("tmp", [P, S])
        kk = sb("kk", [P, S])
        a = sb("a", [P, S])
        dec = sb("dec", [P, S])
        cum = sb("cum", [P, NCH, CH + 1])
        inv = sb("inv", [P, S])
        icum = sb("icum", [P, S])
        gain = sb("gain", [P, S])
        zero = sb("zero", [P, CH])
        PX = ctx.enter_context(nc.psum_tensor(f"f{p}_PX", [P, 4, 2, BANK], F32))
        q = sems(nc, ctx, "ld mm ev km sq ss nrm za sga dec d z", f"f{p}_")
        block = ctx.enter_context(nc.Block())
        col = lambda j: R["cols"][:, p, j:j + 1]
        om = lambda j: R["omcols"][:, p, j:j + 1]
        ch = slice(p * P, (p + 1) * P)
        wide = lambda n: PX[:, n, :, :].rearrange("p a b -> p (a b)")

        @block.sync
        def _(sp):
            for j in range(3):
                sp.dma_start(W[:, :, j, :], T["w_in"][0, :, j * RW + p * P:j * RW + (p + 1) * P]
                             .rearrange("(k p) f -> p k f", p=P)).then_inc(q["ld"], 16)

        @block.tensor
        def _(pe):
            for n in range(2):
                nc.tensor.matmul(PX[:, 0, n, :], R["w2a2"][0:64, ch], R["hwa"][0:64, n * BANK:(n + 1) * BANK], start=True, stop=True)
            for n in range(2):
                last = nc.tensor.matmul(PX[:, 1, n, :], R["w2a2"][64:P, ch], R["hwa"][64:P, n * BANK:(n + 1) * BANK],
                                        start=True, stop=True)
            last.then_inc(q["za"], 1)
            pe.wait_ge(q["ld"], 48)
            for j, bank in ((1, 2), (0, 3), (2, 0)):
                if bank == 0:
                    pe.wait_ge(q["sga"], 1)
                for n in range(2):
                    for k in range(DC):
                        last = nc.tensor.matmul(PX[:, bank, n, :], W[:, k, j, :], T["xnT"][:, k, 1 + n * BANK:1 + (n + 1) * BANK],
                                                start=(k == 0), stop=(k == DC - 1))
                    if bank == 3 and n == 0:
                        pe.wait_ge(q["sga"], 2)
                        pe.wait_ge(q["sq"], 1)
                        for m in range(2):
                            sums = nc.tensor.matmul(PX[:, 1, m, :], R["blockones"][:, :], tmp[:, m * BANK:(m + 1) * BANK],
                                                    start=True, stop=True)
                        sums.then_inc(q["ss"], 1)
                last.then_inc(q["mm"], 1)

        @block.scalar
        def _(act):
            act.wait_ge(q["za"], 1)
            nc.scalar.activation(dec[:, :], wide(0), ACT.Sigmoid, bias=col(W0)).then_inc(q["sga"], 1)
            nc.scalar.activation(a[:, :], wide(1), ACT.Sigmoid, bias=col(A0)).then_inc(q["sga"], 1)
            act.wait_ge(q["sga"], 2)
            nc.scalar.activation(dec[:, :], dec[:, :], ACT.Exp, scale=-E_HALF).then_inc(q["dec"], 1)
            nc.scalar.activation(gain[:, :], a[:, :], ACT.Identity, bias=om(K_A), scale=col(K_A)).then_inc(q["sga"], 1)

            def evac(m, j, bank):
                act.wait_ge(q["mm"], m + 1)
                nc.scalar.activation(raw[:, j, 1:S + 1], wide(bank), ACT.Copy)
                nc.scalar.activation(mix[:, j, :], wide(bank), ACT.Copy, scale=om(j)).then_inc(q["ev"], 1)

            act.wait_ge(q["z"], 1)
            evac(0, 1, 2)
            act.wait_ge(q["km"], 1)
            nc.scalar.activation(tmp[:, :], mix[:, 1, :], ACT.Square, scale=col(K_K)).then_inc(q["sq"], 1)
            act.wait_ge(q["ss"], 1)
            nc.scalar.activation(inv[:, :], wide(1), ACT.Sqrt).then_inc(q["nrm"], 1)
            evac(1, 0, 3)
            evac(2, 2, 0)

        @block.vector
        def _(dve):
            link = chained(dve, q["d"])
            nc.vector.memset(raw[:, :, 0], 0.0)
            nc.vector.memset(cum[:, :, 0], 1.0)
            nc.vector.memset(zero[:, :], 0.0).then_inc(q["z"], 1)
            dve.wait_ge(q["z"], 1)
            r, k, v = mix[:, 0, :], mix[:, 1, :], mix[:, 2, :]
            cs = cum[:, :, 1:CH + 1]
            prev = cum[:, :, 0:CH]
            last_c = cum[:, :, CH:CH + 1].broadcast_to([P, NCH, CH])
            by = lambda t: t.rearrange("p (c t) -> p c t", t=CH)
            dve.wait_ge(q["dec"], 1)
            for c in range(NCH):
                last = nc.vector.tensor_tensor_scan(cum[:, c, 1:CH + 1], dec[:, c * CH:(c + 1) * CH], zero[:, :], 1.0,
                                                    ALU.mult, ALU.add)
            link(last)
            link(nc.vector.reciprocal(by(icum[:, :]), cs))
            link(nc.vector.tensor_tensor(F["dc"][:, :, :], R["ident2"][:, None, :].broadcast_to([P, NCH, CH]), last_c, ALU.mult))

            def mixed(j, m, out):
                dve.wait_ge(q["ev"], m)
                return nc.vector.scalar_tensor_tensor(out=out, in0=raw[:, j, 0:S], scalar=col(j), in1=mix[:, j, :],
                                                      op0=ALU.mult, op1=ALU.add)

            mixed(1, 1, k).then_inc(q["km"], 1)
            dve.wait_ge(q["km"], 1)
            link(nc.vector.tensor_scalar(kk[:, :], k, col(K_K), None, ALU.mult))
            dve.wait_ge(q["sga"], 3)
            dve.wait_ge(q["sq"], 1)
            link(nc.vector.tensor_tensor(k, k, gain[:, :], ALU.mult))
            link(nc.vector.tensor_tensor(F["kt"][:, :], k, icum[:, :], ALU.mult))
            link(nc.vector.tensor_tensor(by(F["ke"][:, :]), by(F["kt"][:, :]), last_c, ALU.mult))
            dve.wait_ge(q["nrm"], 1)
            link(nc.vector.tensor_scalar(inv[:, :], inv[:, :], 1e-12, None, ALU.max))
            link(nc.vector.reciprocal(inv[:, :], inv[:, :]))
            link(nc.vector.tensor_tensor(kk[:, :], kk[:, :], inv[:, :], ALU.mult))
            link(nc.vector.scalar_tensor_tensor(out=by(F["ar"][:, 0, :]), in0=by(kk[:, :]), scalar=-1.0, in1=prev,
                                                op0=ALU.mult, op1=ALU.mult))
            link(nc.vector.tensor_tensor(kk[:, :], kk[:, :], a[:, :], ALU.mult))
            link(nc.vector.tensor_tensor(F["bt"][:, :], kk[:, :], icum[:, :], ALU.mult))
            link(nc.vector.tensor_tensor(by(F["be"][:, :]), by(F["bt"][:, :]), last_c, ALU.mult))
            link(mixed(0, 2, r))
            link(nc.vector.scalar_tensor_tensor(out=F["bonus"][:, :], in0=r, scalar=col(R_K), in1=k, op0=ALU.mult, op1=ALU.mult))
            link(nc.vector.tensor_tensor(by(F["ar"][:, 1, :]), by(r), cs, ALU.mult))
            link(mixed(2, 3, F["v"][:, :]))


def chunks_phase(nc, T, R, F, p):
    with ExitStack() as ctx:
        streams = []
        for x in "ab":
            sb = lambda n, s, dt=F32: ctx.enter_context(nc.sbuf_tensor(f"k{p}{x}_{n}", s, dt))
            pb = lambda n: ctx.enter_context(nc.psum_tensor(f"k{p}{x}_{n}", [P, BANK], F32))
            streams.append({
                "tk": sb("tk", [P, 4, P]), "sc": sb("sc", [P, 2, 4, P]), "mt": sb("mt", [P, LEVELS, 2, P]),
                "D": sb("D", [P, 2, P]), "Dt": sb("Dt", [P, 2, P]), "Ps": sb("Ps", [P, 2, P]),
                "LV": sb("LV", [P, 2, CH]), "WZ": sb("WZ", [P, 2, 2, CH]),
                "S": [pb("S0"), pb("S1")], "X": pb("X"), "DD": pb("DD"),
                "q": sems(nc, ctx, "turned turned_out scored masked levels d_first d_turned p_done p_out dd_done d_added "
                                   "lv_done lv_out w_done w_out q_done q_out y_done y_out link", f"k{p}{x}_")})
        block = ctx.enter_context(nc.Block())
        rows = lambda hh: slice(CH * hh, CH * hh + CH)
        quad = lambda bank: bank.rearrange("p (a b) -> p a b", b=P)
        STAGES = 3 + 2 * LEVELS + 3
        PER = NT // 2

        def schedule(stage_of):
            for step in range(PER * STAGES + LAG):
                for x in range(2):
                    at = step - LAG * x
                    if 0 <= at < PER * STAGES:
                        n, k = at // STAGES, at % STAGES
                        stage_of(streams[x], streams[x]["q"], n, 2 * n + x, k)

        @block.tensor
        def _(pe):
            def stage(B, q, n, t, k):
                tok = slice(t * P, (t + 1) * P)
                tk, sc, WZ, Dt = B["tk"], B["sc"], B["WZ"], B["Dt"]
                if k == 0:
                    if n:
                        pe.wait_ge(q["q_out"], 3 * n)
                    for j, src in enumerate((F["ar"][:, 0, tok], F["be"][:, tok], F["ke"][:, tok], F["v"][:, tok])):
                        last = nc.tensor.transpose(B["X"][:, j * P:(j + 1) * P], src, T["ident"][:, :])
                    last.then_inc(q["turned"], 1)
                elif k == 1:
                    for hh in range(2):
                        nc.tensor.matmul(B["S"][hh][:, 0:2 * P], F["bt"][rows(hh), tok], F["ar"][rows(hh), :, tok],
                                         start=True, stop=True)
                        last = nc.tensor.matmul(B["S"][hh][:, 2 * P:4 * P], F["kt"][rows(hh), tok], F["ar"][rows(hh), :, tok],
                                                start=True, stop=True)
                        last.then_inc(q["scored"], 1)
                elif k == 2:
                    if n:
                        pe.wait_ge(q["y_out"], n)
                    pe.wait_ge(q["d_first"], n + 1)
                    for hh in range(2):
                        last = nc.tensor.transpose(B["DD"][:, hh * P:(hh + 1) * P], Dt[:, hh, :], T["ident"][:, :])
                    last.then_inc(q["d_turned"], 1)
                elif k < 3 + 2 * LEVELS:
                    l, second = (k - 3) // 2, (k - 3) % 2
                    if not second:
                        pe.wait_ge(q["d_added"], (LEVELS + 1) * n + l + 1)
                        pe.wait_ge(q["levels"], LEVELS * n + l + 1)
                        if l == 0:
                            pe.wait_ge(q["turned_out"], n + 1)
                        for hh in range(2):
                            last = nc.tensor.matmul(B["X"][:, hh * P:(hh + 1) * P], B["mt"][:, l, hh, :], B["D"][:, hh, :],
                                                    start=True, stop=True)
                        last.then_inc(q["p_done"], 1)
                    else:
                        pe.wait_ge(q["p_out"], LEVELS * n + l + 1)
                        for hh in range(2):
                            last = nc.tensor.matmul(B["DD"][:, (2 + hh) * P:(3 + hh) * P], B["Ps"][:, hh, :], Dt[:, hh, :],
                                                    start=True, stop=True)
                            if l < LEVELS - 1:
                                last = nc.tensor.matmul(B["DD"][:, hh * P:(hh + 1) * P], Dt[:, hh, :], B["Ps"][:, hh, :],
                                                        start=True, stop=True)
                        last.then_inc(q["dd_done"], 1)
                elif k == STAGES - 3:
                    for hh in range(2):
                        last = nc.tensor.matmul(B["S"][0][:, hh * CH:(hh + 1) * CH], sc[:, hh, 2, :], tk[:, 3, rows(hh)],
                                                start=True, stop=True)
                    last.then_inc(q["lv_done"], 1)
                elif k == STAGES - 2:
                    pe.wait_ge(q["d_added"], (LEVELS + 1) * (n + 1))
                    pe.wait_ge(q["lv_out"], n + 1)
                    for hh in range(2):
                        nc.tensor.matmul(B["S"][1][:, 2 * hh * CH:(2 * hh + 1) * CH], Dt[:, hh, :], tk[:, 0, rows(hh)],
                                         start=True, stop=True)
                        last = nc.tensor.matmul(B["S"][1][:, (2 * hh + 1) * CH:(2 * hh + 2) * CH], Dt[:, hh, :],
                                                B["LV"][:, hh, :], start=True, stop=True)
                    last.then_inc(q["w_done"], 1)
                else:
                    pe.wait_ge(q["w_out"], n + 1)
                    for hh in range(2):
                        o = B["S"][0][0:CH, hh * P:(hh + 1) * P]
                        nc.tensor.matmul(o, WZ[:, hh, 0, :], sc[:, hh, 1, :], start=True, stop=False)
                        last = nc.tensor.matmul(o, T["ident"][:, rows(hh)], F["ar"][:, 1, tok], start=False, stop=True)
                    last.then_inc(q["q_done"], 1)
                    for c in range(2):
                        half = rows(c)
                        bank = B["X"] if c else B["S"][1]
                        for hh in range(2):
                            g = bank[0:CH, 2 * hh * CH:(2 * hh + 1) * CH]
                            nc.tensor.matmul(g, WZ[half, hh, 0, :], tk[half, 1, rows(hh)], start=True, stop=False)
                            nc.tensor.matmul(g, T["ident"][:, rows(hh)], F["dc"][:, 2 * t + c, :], start=False, stop=True)
                            h = bank[0:CH, (2 * hh + 1) * CH:(2 * hh + 2) * CH]
                            nc.tensor.matmul(h, tk[half, 1, rows(hh)], WZ[half, hh, 1, :], start=True, stop=False)
                            last = nc.tensor.matmul(h, tk[half, 2, rows(hh)], tk[half, 3, rows(hh)], start=False, stop=True)
                        last.then_inc(q["q_done"], 1)
                    for hh in range(2):
                        o = B["DD"][:, hh * CH:(hh + 1) * CH]
                        nc.tensor.matmul(o, sc[:, hh, 1, :], WZ[:, hh, 1, :], start=True, stop=False)
                        last = nc.tensor.matmul(o, sc[:, hh, 3, :], tk[:, 3, rows(hh)], start=False, stop=True)
                    last.then_inc(q["y_done"], 1)

            schedule(stage)

        @block.scalar
        def _(act):
            def stage(B, q, n, t, k):
                if k == 0:
                    act.wait_ge(q["turned"], n + 1)
                    if n:
                        act.wait_ge(q["y_done"], n)
                    nc.scalar.activation(F["vt"][:, t, :], B["X"][:, 3 * P:4 * P], ACT.Copy)
                    nc.scalar.activation(B["tk"][:, :, :], quad(B["X"][:, :]), ACT.Copy).then_inc(q["turned_out"], 1)
                elif 3 <= k < 3 + 2 * LEVELS and (k - 3) % 2 == 0:
                    l = (k - 3) // 2
                    act.wait_ge(q["p_done"], LEVELS * n + l + 1)
                    nc.scalar.activation(B["Ps"][:, :, :], quad(B["X"][:, 0:2 * P]), ACT.Copy).then_inc(q["p_out"], 1)
                elif k == STAGES - 3:
                    act.wait_ge(q["lv_done"], n + 1)
                    nc.scalar.activation(B["LV"][:, :, :].rearrange("p a b -> p (a b)"), B["S"][0][:, 0:2 * CH], ACT.Copy
                                         ).then_inc(q["lv_out"], 1)
                elif k == STAGES - 2:
                    act.wait_ge(q["w_done"], n + 1)
                    nc.scalar.activation(B["WZ"][:, :, :, :].rearrange("p a b c -> p (a b c)"), B["S"][1][:, 0:4 * CH], ACT.Copy
                                         ).then_inc(q["w_out"], 1)
                elif k == STAGES - 1:
                    act.wait_ge(q["q_done"], 3 * n + 1)
                    nc.scalar.activation(F["qt"][:, t, :, :], quad(B["S"][0][0:CH, 0:2 * P]), ACT.Copy).then_inc(q["q_out"], 1)
                    for c in range(2):
                        act.wait_ge(q["q_done"], 3 * n + 2 + c)
                        nc.scalar.activation(F["gh"][:, t, c, :], (B["X"] if c else B["S"][1])[0:CH, 0:4 * CH], ACT.Copy
                                             ).then_inc(q["q_out"], 1)

            schedule(stage)

        @block.vector
        def _(dve):
            links = [chained(dve, B["q"]["link"]) for B in streams]

            def stage(B, q, n, t, k):
                link = links[t % 2]
                D, Dt, DD = B["D"], B["Dt"], B["DD"]
                if k == 1:
                    if n:
                        dve.wait_ge(q["y_done"], n)
                    for hh in range(2):
                        dve.wait_ge(q["scored"], 2 * n + hh + 1)
                        nc.vector.tensor_tensor(B["sc"][:, hh, :, :], quad(B["S"][hh][:, :]), R["masks"][:, 0:4, :],
                                                ALU.mult).then_inc(q["masked"], 1)
                    dve.wait_ge(q["masked"], 2 * n + 2)
                    link(nc.vector.tensor_tensor(Dt[:, :, :], B["sc"][:, :, 0, :],
                                                 R["masks"][:, 4, None, :].broadcast_to([P, 2, P]), ALU.mult))
                    nc.vector.tensor_tensor(Dt[:, :, :], Dt[:, :, :], T["ident"][:, None, :].broadcast_to([P, 2, P]),
                                            ALU.add).then_inc(q["d_first"], 1)
                    dve.wait_ge(q["d_first"], n + 1)
                elif k == 2:
                    dve.wait_ge(q["d_turned"], n + 1)
                    nc.vector.tensor_copy(D[:, :, :], quad(DD[:, 0:2 * P])).then_inc(q["d_added"], 1)
                    dve.wait_ge(q["d_added"], (LEVELS + 1) * n + 1)
                elif 3 <= k < 3 + 2 * LEVELS and (k - 3) % 2:
                    l = (k - 3) // 2
                    dve.wait_ge(q["dd_done"], LEVELS * n + l + 1)
                    if l < LEVELS - 1:
                        nc.vector.tensor_tensor(D[:, :, :], quad(DD[:, 0:2 * P]), D[:, :, :], ALU.add)
                    nc.vector.tensor_tensor(Dt[:, :, :], quad(DD[:, 2 * P:4 * P]), Dt[:, :, :], ALU.add
                                            ).then_inc(q["d_added"], 1)
                    dve.wait_ge(q["d_added"], (LEVELS + 1) * n + l + 2)
                elif k == STAGES - 1:
                    dve.wait_ge(q["y_done"], n + 1)
                    nc.vector.tensor_copy(F["y"][:, t, :, :], B["DD"][:, 0:2 * CH].rearrange("p (a b) -> p a b", b=CH)
                                          ).then_inc(q["y_out"], 1)

            schedule(stage)

        @block.gpsimd
        def _(pool):
            def stage(B, q, n, t, k):
                if k == 1:
                    pool.wait_ge(q["masked"], 2 * n + 2)
                    if n:
                        pool.wait_ge(q["p_done"], LEVELS * n)
                    for l in range(LEVELS):
                        nc.gpsimd.tensor_tensor(B["mt"][:, l, :, :], B["sc"][:, :, 0, :],
                                                R["masks"][:, 5 + l, None, :].broadcast_to([P, 2, P]), ALU.mult
                                                ).then_inc(q["levels"], 1)

            schedule(stage)


def state_phase(nc, T, R, F, p):
    with ExitStack() as ctx:
        sb = lambda n, s, dt=F32: ctx.enter_context(nc.sbuf_tensor(f"s{p}_{n}", s, dt))
        pb = lambda n, s: ctx.enter_context(nc.psum_tensor(f"s{p}_{n}", s, F32))
        ST = sb("ST", [CH, NCH + 1, 2, CH])
        tmp = sb("tmp", [P, NT, P])
        gs = sb("gs", [P, NT, P])
        bn = sb("bn", [P, NT, 2])
        mean = sb("mean", [P, NT, 2])
        var = sb("var", [P, NT, 2])
        PS = pb("PS", [P, 2, BANK])
        PY = pb("PY", [P, 2, BANK])
        PG = pb("PG", [P, 2, BANK])
        PB = pb("PB", [P, BANK])
        q = sems(nc, ctx, "st add g y d vs vq yd yt ge", f"s{p}_")
        block = ctx.enter_context(nc.Block())
        ch = slice(p * P, (p + 1) * P)

        @block.tensor
        def _(pe):
            def gates(i):
                nc.tensor.matmul(PG[:, i // 4, (i % 4) * P:(i % 4 + 1) * P], R["hg"][:, i * P:(i + 1) * P], R["g2"][:, ch],
                                 start=True, stop=True)
                last = nc.tensor.matmul(PB[:, 2 * i:2 * i + 2], F["bonus"][:, i * P:(i + 1) * P], R["blockones"][:, 0:P:CH],
                                        start=True, stop=True)
                if i == NT - 1:
                    last.then_inc(q["g"], 1)

            for c in range(NCH):
                pe.wait_ge(q["add"], c + 1)
                if c < NCH - 1:
                    for hh in range(2):
                        last = nc.tensor.matmul(PS[0:CH, c % 2, hh * CH:(hh + 1) * CH],
                                                F["gh"][:, c // 2, c % 2, 2 * hh * CH:(2 * hh + 1) * CH], ST[:, c, hh, :],
                                                start=True, stop=True)
                    last.then_inc(q["st"], 1)
                i, half = c // 2, c % 2
                for hh in range(2):
                    col = (i % 4) * P + hh * CH
                    last = nc.tensor.matmul(PY[half * CH:(half + 1) * CH, i // 4, col:col + CH],
                                            F["qt"][:, i, hh, half * CH:(half + 1) * CH], ST[:, c, hh, :], start=True, stop=True)
                if c % 8 == 7:
                    last.then_inc(q["y"], 1)
                if half:
                    gates(i)
            for g in range(2):
                pe.wait_ge(q["yd"], 1)
                for t in range(4):
                    i = 4 * g + t
                    last = nc.tensor.transpose(PY[:, g, t * P:(t + 1) * P], F["y"][:, i, :, :].rearrange("p a b -> p (a b)"),
                                               T["ident"][:, :])
                last.then_inc(q["yt"], 1)

        @block.vector
        def _(dve):
            link = chained(dve, q["d"])
            nc.vector.memset(ST[:, 0, :, :], 0.0).then_inc(q["add"], 1)
            for c in range(NCH - 1):
                dve.wait_ge(q["st"], c + 1)
                H = F["gh"][:, c // 2, c % 2, :].rearrange("p (a b c) -> p a b c", b=2, c=CH)[:, :, 1, :]
                nc.vector.tensor_tensor(ST[:, c + 1, :, :], PS[0:CH, c % 2, 0:P].rearrange("p (a b) -> p a b", b=CH), H,
                                        ALU.add).then_inc(q["add"], 1)
            Y = F["y"][:, :, :, :].rearrange("p a b c -> p (a b) c")
            flat = F["y"][:, :, :, :].rearrange("p a b c -> p a (b c)")
            G16 = lambda t: t.rearrange("p a b -> p (a b)")[:, :, None].broadcast_to([P, 2 * NT, CH])
            dve.wait_ge(q["y"], 2)
            link(nc.vector.tensor_tensor(Y, PY[:, :, :].rearrange("p a (b c) -> p (a b) c", c=CH), Y, ALU.add))
            link(nc.vector.tensor_reduce(mean[:, :, :].rearrange("p a b -> p (a b)"), Y, AX.X, ALU.add))
            link(nc.vector.tensor_scalar(mean[:, :, :], mean[:, :, :], 1.0 / CH, None, ALU.mult))
            link(nc.vector.tensor_tensor(Y, Y, G16(mean[:, :, :]), ALU.subtract))
            t16 = tmp[:, :, :].rearrange("p a (b c) -> p (a b) c", c=CH)
            link(nc.vector.tensor_tensor(t16, Y, Y, ALU.mult))
            link(nc.vector.tensor_reduce(var[:, :, :].rearrange("p a b -> p (a b)"), t16, AX.X, ALU.add))
            nc.vector.tensor_scalar(var[:, :, :], var[:, :, :], 1.0 / CH, LNX_EPS, ALU.mult, ALU.add).then_inc(q["vs"], 1)
            dve.wait_ge(q["g"], 1)
            link(nc.vector.tensor_copy(bn[:, :, :], PB[:, 0:2 * NT].rearrange("p (a b) -> p a b", b=2)))
            link(nc.vector.tensor_tensor(t16, F["vt"][:, :, :].rearrange("p a (b c) -> p (a b) c", c=CH), G16(bn[:, :, :]), ALU.mult))
            dve.wait_ge(q["vq"], 1)
            link(nc.vector.reciprocal(var[:, :, :], var[:, :, :]))
            link(nc.vector.tensor_tensor(Y, Y, G16(var[:, :, :]), ALU.mult))
            link(nc.vector.tensor_tensor(flat, flat, R["lng"][:, None, ch].broadcast_to([P, NT, P]), ALU.mult))
            link(nc.vector.tensor_tensor(flat, flat, R["lnb"][:, None, ch].broadcast_to([P, NT, P]), ALU.add))
            link(nc.vector.tensor_tensor(flat, flat, tmp[:, :, :], ALU.add))
            dve.wait_ge(q["ge"], 1)
            nc.vector.tensor_tensor(flat, flat, gs[:, :, :], ALU.mult).then_inc(q["yd"], 1)

        @block.scalar
        def _(act):
            act.wait_ge(q["g"], 1)
            nc.scalar.activation(gs[:, :, :].rearrange("p a b -> p (a b)"), PG[:, :, :].rearrange("p a b -> p (a b)"),
                                 ACT.Copy).then_inc(q["ge"], 1)
            act.wait_ge(q["vs"], 1)
            nc.scalar.activation(var[:, :, :], var[:, :, :], ACT.Sqrt).then_inc(q["vq"], 1)
            for g in range(2):
                act.wait_ge(q["yt"], g + 1)
                nc.scalar.activation(T["yT"][:, p, g * BANK:(g + 1) * BANK], PY[:, g, :], ACT.Copy)


def rwkv(nc, T):
    with ExitStack() as ctx:
        sb = lambda n, s, dt=F32: ctx.enter_context(nc.sbuf_tensor(n, s, dt))
        R = {}
        R["cols"] = sb("rw_cols_sb", [P, PAIRS, 8])
        R["omcols"] = sb("rw_omcols", [P, PAIRS, 8])
        R["w2a2"] = sb("rw_w2a2", [P, RW])
        R["g2"] = sb("rw_g2_sb", [P, RW])
        R["lng"] = sb("rw_lng", [P, RW])
        R["lnb"] = sb("rw_lnb", [P, RW])
        R["masks"] = sb("rw_masks", [P, 10, P])
        R["blockones"] = sb("rw_blockones", [P, P])
        R["ident2"] = sb("rw_ident2", [P, CH])
        R["hwa"] = sb("rw_hwa", [P, S])
        R["hg"] = sb("rw_hg", [P, S])
        lora_phase(nc, T, R)
        F = {}
        F["ar"] = sb("rw_ar", [P, 2, S])
        F["bt"] = sb("rw_bt", [P, S])
        F["kt"] = sb("rw_kt", [P, S])
        F["be"] = sb("rw_be", [P, S])
        F["ke"] = sb("rw_ke", [P, S])
        F["v"] = sb("rw_v", [P, S])
        F["bonus"] = sb("rw_bonus", [P, S])
        F["dc"] = sb("rw_dc", [P, NCH, CH])
        for p in range(PAIRS):
            features_phase(nc, T, R, F, p)
            with ExitStack() as c2:
                sb2 = lambda n, s: c2.enter_context(nc.sbuf_tensor(f"{n}{p}", s, F32))
                F["qt"] = sb2("rw_qt", [CH, NT, 2, P])
                F["gh"] = sb2("rw_gh", [CH, NT, 2, 2 * P])
                F["y"] = sb2("rw_y", [P, NT, 2, CH])
                F["vt"] = sb2("rw_vt", [P, NT, P])
                chunks_phase(nc, T, R, F, p)
                state_phase(nc, T, R, F, p)


_NAMES = ["x", "w_in", "rw_w1", "rw_w2", "rw_a1", "rw_a2", "rw_g1", "rw_g2", "rw_lnx_g", "rw_lnx_b", "nsa_qn_g", "nsa_kn_g",
          "nsa_pe", "nsa_cmp_w1", "nsa_cmp_w2", "w_out", "ln2_g", "moe_wr", "moe_br", "moe_w1", "moe_w2"]


def hybrid_layer_kernel(nc, arrays):
    T = dict(arrays)
    T["h_rows"] = nc.dram_tensor("h_rows", [S + PAD_ROWS, D], F32).ap()
    T["token_list"] = nc.dram_tensor("token_list", [P, N_SLOTS, 2], I32).ap()
    with ExitStack() as ctx:
        sb = lambda n, s, dt=F32: ctx.enter_context(nc.sbuf_tensor(n, s, dt))
        T["ident"] = sb("ident", [P, P])
        T["slots"] = sb("slots", [P, N_SLOTS, 2], I32)
        T["counts"] = sb("counts", [1, N_EXP], I32)
        with ExitStack() as mixers:
            T["yT"] = mixers.enter_context(nc.sbuf_tensor("yT", [P, DC, S], F32))
            with ExitStack() as normed:
                T["xnT"] = normed.enter_context(nc.sbuf_tensor("xnT", [P, DC, S + 1], F32))
                norm_phase(nc, T)
                with ExitStack() as attention:
                    sa = lambda n, s: attention.enter_context(nc.sbuf_tensor(n, s, F32))
                    N = dict(vs=sa("vs", [P, NT, P]), vw=sa("vw", [P, NT, P]), gates=sa("gates", [P, NT, 3 * QH]),
                              qT=sa("qT", [P, 4, S]), qrT=sa("qrT", [P, 4, S]), kT=sa("kT", [P, 4, S]),
                              vcmp=sa("vcmp", [N_CMP, 2, HD]), kcT=sa("kcT", [P, 2, N_CMP]))
                    with ExitStack() as blocks:
                        N["cT"] = blocks.enter_context(nc.sbuf_tensor("cT", [P, 4, S + 2], F32))
                        nsa_project_phase(nc, T, N)
                        compress_phase(nc, T, N)
                    attention_phase(nc, T, N)
                rwkv(nc, T)
            route_phase(nc, T)
        expert_pass(nc, T, True)
        expert_pass(nc, T, False)


def _constants():
    f32 = np.float32
    c = {}
    c["c_ident"] = np.eye(P, dtype=f32)
    c["c_upper"] = np.triu(np.ones((P, P), f32), 1)
    c["c_lower"] = np.tril(np.ones((N_EXP, N_EXP), f32), -1).reshape(1, -1)
    pos = np.arange(S)
    inv = (10000.0 ** (-np.arange(HD // 2, dtype=f32) / f32(HD // 2))).astype(f32)
    ang = pos.astype(f32)[:, None] * inv[None, :]
    c["c_cos"] = np.cos(ang).astype(f32)
    c["c_sin"] = np.sin(ang).astype(f32)
    whole = (16 * np.arange(N_CMP) + 31)[None, :] <= pos[:, None]
    c["c_cmask"] = whole.astype(f32)
    c["c_cpen"] = np.where(whole, 0, NEG).astype(f32)
    row, col = np.arange(P)[:, None], np.arange(P)[None, :]
    c["c_wpen"] = np.concatenate([np.where(col > row, 0, NEG), np.zeros((P, P)), np.where(col <= row, 0, NEG)], 1).astype(f32)
    block, cur = np.arange(16)[None, :], (pos // 64)[:, None]
    forced = (block == 0) | (block == cur) | (block == cur - 1)
    future = block > cur
    c["c_free"] = (~(forced | future)).astype(f32)
    c["c_force"] = np.where(future, -1e6, np.where(forced, 1e6, 0)).astype(f32)
    c["c_lower16"] = np.tril(np.ones((16, 16), f32), -1).reshape(1, -1)
    same = lambda n: (row // n) == (col // n)
    masks = [same(CH) & (row < col), same(CH) & (row <= col)] * 2
    for n in (1, 2, 4, 8, 16, 32):
        masks.append(same(2 * n) & ((col // n) % 2 == 1) & ((row // n) % 2 == 0))
    c["c_masks"] = np.stack(masks, 1).astype(f32)
    c["c_blockones"] = same(CH).astype(f32)
    c["c_ident2"] = np.concatenate([np.eye(CH)] * 2, 0).astype(f32)
    return c


def _columns(inputs):
    cols = lambda v: np.asarray(v).reshape(-1, P).T
    mu = np.asarray(inputs["rw_mu_rkv"])[0]
    per_channel = [mu[0], mu[1], mu[2]] + [np.asarray(inputs[k])[0] for k in ("rw_w0", "rw_a0", "rw_k_k", "rw_k_a", "rw_r_k")]
    return {
        "ln1_cols": cols(inputs["ln1_g"]),
        "mu_wag_cols": np.asarray(inputs["rw_mu_wag"])[0].reshape(3, DC, P).transpose(2, 0, 1),
        "moe_bias_cols": np.concatenate([np.asarray(inputs["moe_b1"])[0].reshape(N_EXP, 2 * FC, P),
                                         np.asarray(inputs["moe_b2"])[0].reshape(N_EXP, DC, P)], 1).transpose(2, 0, 1),
        "rw_cols": np.stack([cols(v) for v in per_channel], 2),
    }


def kernel(**inputs):
    import concourse.bacc as _bacc
    from concourse.bass_utils import run_bass_kernel_spmd as _run

    nc = _bacc.Bacc("TRN2", target_bir_lowering=False, num_devices=1)
    sent = {n: inputs[n] for n in _NAMES} | _columns(inputs) | _constants()
    arrays, aps = {}, {}
    for name, a in sent.items():
        a = np.ascontiguousarray(a)
        arrays[f"in_{name}"] = a
        aps[name] = nc.dram_tensor(f"in_{name}", a.shape, mybir.dt.from_np(a.dtype), kind="ExternalInput").ap()
    aps["out"] = nc.dram_tensor("out_rows", (S + PAD_ROWS, D), F32, kind="ExternalOutput").ap()
    hybrid_layer_kernel(nc, aps)
    r = _run(nc, [arrays], core_ids=[0])
    return r.results[0]["out_rows"][:S].reshape(1, S, D)
```

```python
import concourse.bass as bass
from concourse import mybir
from contextlib import ExitStack
import numpy as np

F32 = mybir.dt.float32
I32 = mybir.dt.int32
ALU = mybir.AluOpType
ACT = mybir.ActivationFunctionType
AX = mybir.AxisListType

P = 128
D = 1024
S = 1024
NT = S // P
DC = D // P
BANK = 512
EPS = 1e-6
N_EXP = 32
TOP_K = 4
D_FF = 1024
PAD_ROWS = P
LIST_K = S // P
N_SLOTS = N_EXP * LIST_K
LIMIT = 7.0
ALPHA = 1.702


def sem_list(nc, ctx, names):
    out = [nc.alloc_semaphore(n) for n in names]

    def over():
        nc.clear_and_free_semaphores(out)
        nc.all_engine_barrier(sem_only=True)
    ctx.callback(over)
    return out


def sems(nc, ctx, names, prefix=""):
    names = names.split()
    return dict(zip(names, sem_list(nc, ctx, [prefix + n for n in names])))


def chained(eng, sem):
    count = [0]

    def link(ins):
        count[0] += 1
        ins.then_inc(sem, 1)
        eng.wait_ge(sem, count[0])
    return link


def route_phase(nc, T):
    with ExitStack() as ctx:
        sb = lambda n, s, dt=F32: ctx.enter_context(nc.sbuf_tensor(n, s, dt))
        pb = lambda n, s: ctx.enter_context(nc.psum_tensor(n, s, F32))
        wout = sb("wout", [P, DC, D])
        x2 = sb("x2", [P, NT, D])
        hrow = sb("hrow", [P, 2, D])
        hT = sb("hT", [P, 2, DC, P])
        g2 = sb("g2", [P, D])
        wr = sb("wr", [P, DC, N_EXP])
        br = sb("br", [P, N_EXP])
        junk = sb("junk", [P, D])
        zero = sb("zero", [P, D // 2])
        st = sb("st", [P, 3, NT])
        L = sb("L", [P, N_EXP])
        cmp1 = sb("cmp1", [P, N_EXP, N_EXP])
        cmp2 = sb("cmp2", [P, N_EXP, N_EXP])
        lower = sb("lower", [P, N_EXP, N_EXP])
        rank = sb("rank", [P, N_EXP])
        sel = sb("sel", [P, N_EXP])
        before = sb("before", [P, NT + 1, N_EXP])
        G = sb("G", [P, N_EXP])
        mx = sb("mx", [P, 1])
        den = sb("den", [P, 1])
        upper = sb("upper", [P, P])
        ones = sb("ones", [P, P])
        ecol = sb("ecol", [P, N_EXP])
        places = sb("places", [P, TOP_K, N_EXP])
        posi = sb("posi", [P, N_EXP], I32)
        posk = sb("posk", [P, N_EXP], I32)
        posf = sb("posf", [P, N_EXP])
        poskf = sb("poskf", [P, N_EXP])
        pick = sb("pick", [P, TOP_K, N_EXP])
        chosen = sb("chosen", [P, 2, TOP_K, N_EXP])
        dst = sb("dst", [P, NT, TOP_K])
        dsti = sb("dsti", [P, NT, TOP_K], I32)
        entry = sb("entry", [P, NT, TOP_K, 2], I32)
        tok = sb("tok", [P, NT], I32)
        padlist = T["slots"]
        PO = pb("PO", [P, 2, D])
        PT = pb("PT", [P, 2, BANK])
        PL = pb("PL", [P, BANK])
        PC = pb("PC", [P, BANK])
        q = sems(nc, ctx, "r_ld_x r_ld_c r_po r_x2 r_ss r_ms r_sq r_h r_st_x r_st_ha r_st_hb r_st_x0 r_st_h0 r_tp r_hT r_lg "
                          "r_logit r_pool r_padst r_sel r_pos r_exp r_ent r_scat r_back r_dve r_mxn r_cnt r_pos_out r_ld_up "
                          "r_total " + " ".join(f"r_ld_w{k}" for k in range(DC)))
        block = ctx.enter_context(nc.Block())
        h_stored = (q["r_st_ha"], q["r_st_hb"])
        x_rows = T["x"].rearrange("o (t p) d -> (o t) p d", p=P)

        @block.sync
        def _(sp):
            for k in range(DC):
                sp.dma_start(wout[:, k, :], T["w_out"][0, k * P:(k + 1) * P, :]).then_inc(q[f"r_ld_w{k}"], 16)
            sp.dma_start(wr[:, :, :], T["moe_wr"][0].rearrange("(k p) e -> p k e", p=P)).then_inc(q["r_ld_c"], 16)
            sp.dma_start(upper[:, :], T["c_upper"]).then_inc(q["r_ld_c"], 16)
            sp.dma_start(lower[:, :, :].rearrange("p a b -> p (a b)"),
                         T["c_lower"].broadcast_to([P, N_EXP * N_EXP])).then_inc(q["r_ld_c"], 16)
            sp.wait_ge(q["r_ld_x"], 16 * NT)
            for s in range(4):
                for side in range(2):
                    lo = side * D_FF + 2 * s * P
                    sp.dma_start(T["w1"][s][:, :, side, :], T["moe_w1"][0, 0, :, lo:lo + 2 * P]
                                 .rearrange("(k p) f -> p k f", p=P)).then_inc(q["r_ld_up"], 16)
            for i in range(NT):
                sp.wait_ge(q["r_x2"], i + 1)
                sp.dma_start(T["out"][i * P:(i + 1) * P, :], x2[:, i, :]).then_inc(q["r_st_x"], 16)
                sp.wait_ge(q["r_h"], i + 1)
                sp.dma_start(T["h_rows"][i * P:(i + 1) * P, :], hrow[:, i % 2, :]).then_inc(h_stored[i % 2], 16)
            sp.wait_ge(q["r_st_x"], 16 * NT)
            for s_h in h_stored:
                sp.wait_ge(s_h, 16 * NT // 2)
            sp.wait_ge(q["r_ld_up"], 16 * 8)

        @block.scalar
        def _(act):
            act.dma_start(g2[:, :], T["ln2_g"].broadcast_to([P, D])).then_inc(q["r_ld_c"], 16)
            act.dma_start(br[:, :], T["moe_br"].broadcast_to([P, N_EXP])).then_inc(q["r_ld_c"], 16)

            act.wait_ge(q[f"r_ld_w{DC - 1}"], 16)
            for i in range(NT):
                act.dma_start(x2[:, i, :], x_rows[i]).then_inc(q["r_ld_x"], 16)

            def exp_logits(i):
                act.wait_ge(q["r_mxn"], i + 1)
                nc.scalar.activation(G[:, :], G[:, :], ACT.Exp).then_inc(q["r_exp"], 1)

            for i in range(NT):
                act.wait_ge(q["r_x2"], i + 1)
                if i:
                    act.wait_ge(q["r_ss"], i)
                nc.scalar.activation(junk[:, :], x2[:, i, :], ACT.Square,
                                     accum_out=st[:, 0, i:i + 1]).then_inc(q["r_ss"], 1)
                act.wait_ge(q["r_ms"], i + 1)
                nc.scalar.activation(st[:, 2, i:i + 1], st[:, 1, i:i + 1], ACT.Sqrt).then_inc(q["r_sq"], 1)
                if i:
                    exp_logits(i - 1)
                for g in range(2):
                    act.wait_ge(q["r_tp"], 2 * i + g + 1)
                    if i >= 2:
                        act.wait_ge(q["r_lg"], i - 1)
                    nc.scalar.activation(hT[:, i % 2, 4 * g:4 * g + 4, :], PT[:, g, :].rearrange("p (a b) -> p a b", b=P),
                                         ACT.Copy).then_inc(q["r_hT"], 1)
            exp_logits(NT - 1)

        @block.tensor
        def _(pe):
            def project(i):
                if i >= 2:
                    pe.wait_ge(q["r_x2"], i - 1)
                for k in range(DC):
                    if i == 0:
                        pe.wait_ge(q[f"r_ld_w{k}"], 16)
                    for n in range(2):
                        last = nc.tensor.matmul(PO[:, i % 2, n * BANK:(n + 1) * BANK], T["yT"][:, k, i * P:(i + 1) * P],
                                                wout[:, k, n * BANK:(n + 1) * BANK], start=(k == 0), stop=(k == DC - 1))
                last.then_inc(q["r_po"], 1)

            def logits(i):
                pe.wait_ge(q["r_h"], i + 1)
                for g in range(2):
                    if i:
                        pe.wait_ge(q["r_hT"], 2 * (i - 1) + g + 1)
                    for c in range(4):
                        last = nc.tensor.transpose(PT[:, g, c * P:(c + 1) * P],
                                                   hrow[:, i % 2, (4 * g + c) * P:(4 * g + c + 1) * P], T["ident"][:, :])
                    last.then_inc(q["r_tp"], 1)
                pe.wait_ge(q["r_hT"], 2 * i + 2)
                if i == 0:
                    pe.wait_ge(q["r_ld_c"], 16 * 5)
                else:
                    pe.wait_ge(q["r_logit"], i)
                for k in range(DC):
                    last = nc.tensor.matmul(PL[:, 0:N_EXP], hT[:, i % 2, k, :], wr[:, k, :],
                                            start=(k == 0), stop=(k == DC - 1))
                last.then_inc(q["r_lg"], 1)

            def positions(i):
                pe.wait_ge(q["r_sel"], i + 1)
                if i:
                    pe.wait_ge(q["r_pos_out"], i)
                nc.tensor.matmul(PC[:, 0:N_EXP], upper[:, :], sel[:, :], start=True, stop=False)
                nc.tensor.matmul(PC[:, 0:N_EXP], ones[:, :], before[:, i, :], start=False, stop=True).then_inc(q["r_pos"], 1)

            project(0)
            for i in range(NT):
                if i + 1 < NT:
                    project(i + 1)
                if i == 1:
                    pe.wait_ge(q["r_pool"], 3)
                if i:
                    positions(i - 1)
                logits(i)
            positions(NT - 1)
            pe.wait_ge(q["r_logit"], NT)
            nc.tensor.matmul(PL[:, 0:N_EXP], ones[:, :], before[:, NT, :], start=True, stop=True).then_inc(q["r_total"], 1)

        @block.vector
        def _(dve):
            link = chained(dve, q["r_dve"])
            dve.wait_ge(q["r_ld_c"], 16 * 5)
            dve.wait_ge(q["r_pool"], 4)
            nc.vector.memset(before[:, 0, :], 0.0)
            for j in range(TOP_K):
                nc.vector.memset(places[:, j, :], float(j))
                last = nc.vector.tensor_copy(entry[:, :, j, 0], tok[:, :])
            link(last)

            def choose(i):
                dve.wait_ge(q["r_lg"], i + 1)
                nc.vector.tensor_tensor(L[:, :], PL[:, 0:N_EXP], br[:, :], ALU.add).then_inc(q["r_logit"], 1)
                dve.wait_ge(q["r_logit"], i + 1)
                link(nc.vector.tensor_reduce(mx[:, :], L[:, :], AX.X, ALU.max))
                nc.vector.tensor_scalar(G[:, :], L[:, :], mx[:, 0:1], None, ALU.subtract).then_inc(q["r_mxn"], 1)
                other = L[:, None, :].broadcast_to([P, N_EXP, N_EXP])
                own = L[:, :, None].broadcast_to([P, N_EXP, N_EXP])
                nc.vector.tensor_tensor(cmp1[:, :, :], other, own, ALU.is_gt)
                link(nc.vector.tensor_tensor(cmp2[:, :, :], other, own, ALU.is_equal))
                link(nc.vector.tensor_tensor(cmp2[:, :, :], cmp2[:, :, :], lower[:, :, :], ALU.mult))
                link(nc.vector.tensor_tensor(cmp1[:, :, :], cmp1[:, :, :], cmp2[:, :, :], ALU.add))
                link(nc.vector.tensor_reduce(rank[:, :], cmp1[:, :, :], AX.X, ALU.add))
                link(nc.vector.tensor_scalar(sel[:, :], rank[:, :], TOP_K - 0.5, None, ALU.is_lt))
                nc.vector.tensor_tensor(before[:, i + 1, :], before[:, i, :], sel[:, :], ALU.add).then_inc(q["r_sel"], 1)
                link(nc.vector.tensor_tensor(pick[:, :, :], rank[:, None, :].broadcast_to([P, TOP_K, N_EXP]), places[:, :, :],
                                             ALU.is_equal))
                dve.wait_ge(q["r_exp"], i + 1)
                link(nc.vector.tensor_tensor(G[:, :], G[:, :], sel[:, :], ALU.mult))
                link(nc.vector.tensor_reduce(den[:, :], G[:, :], AX.X, ALU.add))
                link(nc.vector.reciprocal(den[:, :], den[:, :]))
                link(nc.vector.tensor_scalar(G[:, :], G[:, :], den[:, 0:1], None, ALU.mult))

            def address(i):
                dve.wait_ge(q["r_pos"], i + 1)
                nc.vector.tensor_copy(posi[:, :], PC[:, 0:N_EXP]).then_inc(q["r_pos_out"], 1)
                dve.wait_ge(q["r_pos_out"], i + 1)
                link(nc.vector.tensor_scalar(posk[:, :], posi[:, :], P.bit_length() - 1, None, ALU.logical_shift_right))
                link(nc.vector.tensor_scalar(posi[:, :], posi[:, :], P - 1, None, ALU.bitwise_and))
                nc.vector.tensor_copy(poskf[:, :], posk[:, :])
                link(nc.vector.tensor_copy(posf[:, :], posi[:, :]))
                link(nc.vector.scalar_tensor_tensor(out=posf[:, :], in0=posf[:, :], scalar=float(N_SLOTS),
                                                    in1=poskf[:, :], op0=ALU.mult, op1=ALU.add))
                link(nc.vector.tensor_tensor(posf[:, :], posf[:, :], ecol[:, :], ALU.add))
                for n, what in enumerate((posf, G)):
                    last = nc.vector.tensor_tensor(chosen[:, n, :, :], pick[:, :, :],
                                                   what[:, None, :].broadcast_to([P, TOP_K, N_EXP]), ALU.mult)
                link(last)
                nc.vector.tensor_reduce(entry[:, i, :, 1].bitcast(F32), chosen[:, 1, :, :], AX.X, ALU.add)
                link(nc.vector.tensor_reduce(dst[:, i, :], chosen[:, 0, :, :], AX.X, ALU.add))
                nc.vector.tensor_copy(dsti[:, i, :], dst[:, i, :]).then_inc(q["r_ent"], 1)

            for i in range(NT):
                dve.wait_ge(q["r_po"], i + 1)
                if i == 0:
                    dve.wait_ge(q["r_ld_x"], 16 * NT)
                nc.vector.tensor_tensor(x2[:, i, :], PO[:, i % 2, :], x2[:, i, :], ALU.add).then_inc(q["r_x2"], 1)
                dve.wait_ge(q["r_ss"], i + 1)
                nc.vector.tensor_scalar(st[:, 1, i:i + 1], st[:, 0, i:i + 1], 1.0 / D, EPS,
                                        ALU.mult, ALU.add).then_inc(q["r_ms"], 1)
                dve.wait_ge(q["r_sq"], i + 1)
                link(nc.vector.reciprocal(st[:, 0, i:i + 1], st[:, 2, i:i + 1]))
                if i >= 2:
                    dve.wait_ge(h_stored[i % 2], 16 * (i // 2))
                    dve.wait_ge(q["r_tp"], 2 * (i - 1))
                nc.vector.scalar_tensor_tensor(out=hrow[:, i % 2, :], in0=x2[:, i, :], scalar=st[:, 0, i:i + 1],
                                               in1=g2[:, :], op0=ALU.mult, op1=ALU.mult).then_inc(q["r_h"], 1)
                if i:
                    choose(i - 1)
                    address(i - 1)
            choose(NT - 1)
            address(NT - 1)
            dve.wait_ge(q["r_total"], 1)
            nc.vector.tensor_copy(T["counts"][:, 0:N_EXP], PL[0:1, 0:N_EXP]).then_inc(q["r_cnt"], 1)
            link(nc.vector.tensor_reduce(den[0:1, :], PL[0:1, 0:N_EXP], AX.X, ALU.max))
            nc.vector.tensor_copy(T["counts"][:, N_EXP:N_EXP + 1], den[0:1, :]).then_inc(q["r_cnt"], 1)
            dve.wait_ge(q["r_cnt"], 2)

        @block.gpsimd
        def _(pool):
            nc.gpsimd.memset(zero[:, :], 0.0).then_inc(q["r_pool"], 1)
            nc.gpsimd.memset(ones[:, :], 1.0).then_inc(q["r_pool"], 1)
            nc.gpsimd.iota(tok[:, :], pattern=[[P, NT]], base=0, channel_multiplier=1).then_inc(q["r_pool"], 1)
            nc.gpsimd.iota(ecol[:, :], pattern=[[LIST_K, N_EXP]], base=0, channel_multiplier=0,
                           allow_small_or_imprecise_dtypes=True).then_inc(q["r_pool"], 1)
            nc.gpsimd.memset(padlist[:, :, 1].bitcast(F32), 0.0).then_inc(q["r_pool"], 1)
            nc.gpsimd.iota(padlist[:, :, 0], pattern=[[0, N_SLOTS]], base=S, channel_multiplier=1).then_inc(q["r_pool"], 1)
            pool.wait_ge(q["r_pool"], 6)
            nc.gpsimd.dma_start(T["token_list"], padlist[:, :, :]).then_inc(q["r_padst"], 16)
            for half in (slice(0, D // 2), slice(D // 2, D)):
                nc.gpsimd.dma_start(T["out"][S:S + PAD_ROWS, half], zero[:, :]).then_inc(q["r_st_x0"], 16)
                nc.gpsimd.dma_start(T["h_rows"][S:S + PAD_ROWS, half], zero[:, :]).then_inc(q["r_st_h0"], 16)
            pool.wait_ge(q["r_padst"], 16)
            for i in range(NT):
                pool.wait_ge(q["r_ent"], i + 1)
                for j in range(TOP_K):
                    nc.gpsimd.indirect_dma_start(
                        out=T["token_list"].rearrange("p s c -> (p s) c"),
                        out_offset=bass.IndirectOffsetOnAxis(ap=dsti[:, i, j:j + 1], axis=0),
                        in_=entry[:, i, j, :], in_offset=None).then_inc(q["r_scat"], 16)
            pool.wait_ge(q["r_scat"], 16 * TOP_K * NT)
            nc.gpsimd.dma_start(T["slots"][:, :, :], T["token_list"]).then_inc(q["r_back"], 16)
            pool.wait_ge(q["r_back"], 16)
            pool.wait_ge(q["r_st_x0"], 32)
            pool.wait_ge(q["r_st_h0"], 32)


GROUP = 2 * P
WIDTHS = (128, 136, 144, 160, 192, GROUP)
FC = D_FF // P


def expert_pass(nc, T, first):
    tag = "x1_" if first else "x2_"
    with ExitStack() as ctx:
        sb = lambda n, s, dt=F32: ctx.enter_context(nc.sbuf_tensor(tag + n, s, dt))
        pb = lambda n, s: ctx.enter_context(nc.psum_tensor(tag + n, s, F32))
        w1 = T["w1"]
        w2 = [sb(f"w2_{j}", [P, FC, BANK]) for j in range(2)]
        bias_all = sb("bias_all", [P, N_EXP, 3 * FC])
        bias = sb("bias", [P, 3 * FC])
        gate = sb("gate", [P, 2])
        hg = sb("hg", [P, 2, D])
        hT = sb("hT", [P, DC, GROUP])
        glu = sb("glu", [P, 2, GROUP])
        lin = sb("lin", [P, 2, GROUP])
        sig = sb("sig", [P, 2, GROUP])
        act_T = sb("act_T", [P, FC, GROUP])
        yT = sb("yT", [P, DC, GROUP])
        ysb = sb("ysb", [P, 2, D])
        idx_in = sb("idx_in", [P, 2], I32)
        idx_out = sb("idx_out", [P, 2], I32)
        PU = pb("PU", [P, 4, 2, GROUP])
        PY = pb("PY", [P, 2, 2, GROUP])
        PT = pb("PT", [P, 2, BANK])
        q = sems(nc, ctx, "bias_in gathered0 gathered1 turned0 turned1 hT_copy hT_ready u_done u_used glu_ready sig_ready "
                          "act_ready y_done yT_ready back_done back_half back_used scat0 scat1 links pool_copy held init "
                          + " ".join(f"loaded{j} free{j}" for j in range(6)), tag)
        loaded = [q[f"loaded{j}"] for j in range(6)]
        free = [q[f"free{j}"] for j in range(6)]
        block = ctx.enter_context(nc.Block())

        def count_of(eng, e):
            return eng.value_load(T["counts"][0:1, bass.ds(e, 1)], min_val=0, max_val=S)

        def by_width(eng, count, body):
            if not first:
                body(GROUP)
                return
            def least(widths):
                if len(widths) == 1:
                    body(widths[0])
                    return
                with eng.If(count < widths[0] + 1):
                    body(widths[0])
                    eng.nop()
                with eng.Else():
                    least(widths[1:])
                    eng.nop()
            least(WIDTHS)

        def groups(eng, body, before=None):
            if first:
                if before is not None:
                    before()
                count, following = eng.alloc_register(tag + "count"), eng.alloc_register(tag + "following")
                eng.reg_load(following, T["counts"][0:1, 0:1])
                known = lambda r: eng.snap(r, min_val=0, max_val=S)
                with eng.Fori(0, N_EXP - 1) as e:
                    eng.reg_mov(count, following)
                    read_next = lambda: eng.reg_load(following, T["counts"][0:1, bass.ds(e + 1, 1)])
                    body(e, e, 0, known(count), (read_next, lambda: known(following)))
                eng.reg_mov(count, following)
                body(N_EXP - 1, N_EXP - 1, 0, known(count), None)
                return
            done = eng.alloc_register(f"{tag}{eng.engine}_groups".replace(".", "_"))
            eng.reg_mov(done, 0)
            greatest = eng.value_load(T["counts"][0:1, N_EXP:N_EXP + 1], min_val=0, max_val=S)
            with eng.If(greatest > GROUP):
                with eng.Fori(0, N_EXP) as e:
                    count = count_of(eng, e)
                    with eng.If(count > GROUP):
                        with eng.Fori(1, S // GROUP) as j:
                            body(eng.snap(done), e, j, count, None)
                            eng.reg_add(done, done, 1)
                        eng.nop()
                    eng.nop()
                eng.nop()

        @block.sync
        def _(sp):
            sp.dma_start(bias_all[:, :, :], T["moe_bias_cols"]).then_inc(q["bias_in"], 16)
            sp.sem_inc(free[4], 1)
            sp.sem_inc(free[5], 1)

            def load_up(n, e):
                w1_e = T["moe_w1"][0][bass.ds(e, 1)].rearrange("o (k p) f -> p (o k) f", p=P)
                for s in range(4):
                    sp.wait_ge(free[s], n)
                    for side in range(2):
                        lo = side * D_FF + 2 * s * P
                        sp.dma_start(w1[s][:, :, side, :], w1_e[:, :, lo:lo + 2 * P]).then_inc(loaded[s], 16)

            def load_down(n, e):
                w2_e = T["moe_w2"][0][bass.ds(e, 1)].rearrange("o (k p) f -> p (o k) f", p=P)
                for s in range(2):
                    sp.wait_ge(free[4 + s], n + 1)
                    sp.dma_start(w2[s][:, :, :], w2_e[:, :, s * BANK:(s + 1) * BANK]).then_inc(loaded[4 + s], 16)

            if first:
                for s in range(4):
                    sp.sem_inc(loaded[s], 32)
                with sp.Fori(0, N_EXP - 1) as e:
                    load_down(e, e)
                    load_up(e + 1, e + 1)
                load_down(N_EXP - 1, N_EXP - 1)
            else:
                for s in range(4):
                    sp.sem_inc(free[s], 1)

                def load(n, e, j, count, ahead):
                    load_up(n + 1, e)
                    load_down(n, e)
                groups(sp, load)
            sp.wait_ge(q["bias_in"], 16)

        @block.tensor
        def _(pe):
            def turn(n, half, after):
                if half:
                    pe.wait_ge(q["hT_copy"], n + 1)
                elif after:
                    pe.wait_ge(q["back_used"], n if first else n + 1)
                pe.wait_ge(q[f"gathered{half}"], 16 * n + 16)
                for c in range(DC):
                    last = nc.tensor.transpose(PT[:, c // 4, (c % 4) * P:(c % 4 + 1) * P], hg[:, half, c * P:(c + 1) * P],
                                               T["ident"][:, :])
                last.then_inc(q[f"turned{half}"], 1)

            def up(n, N, ahead):
                for c in range(FC):
                    if c == 4 and ahead:
                        ahead[0]()
                    pe.wait_ge(loaded[c // 2], 32 * n + 32)
                    pe.wait_ge(q["u_used"], 8 * n + c + 1)
                    for side in range(2):
                        for k in range(DC):
                            last = nc.tensor.matmul(PU[:, c % 4, side, 0:N], w1[c // 2][:, k, side, (c % 2) * P:(c % 2 + 1) * P],
                                                    hT[:, k, 0:N], start=(k == 0), stop=(k == DC - 1))
                            if side == 0 and k == 0 and c and c % 2 == 0:
                                last.then_inc(free[c // 2 - 1], 1)
                    last.then_inc(q["u_done"], 1)

            def down(n, N, ahead):
                def back(pair):
                    pe.wait_ge(q["yT_ready"], 4 * n + pair + 3)
                    if pair == 0:
                        pe.wait_ge(q["hT_ready"], n + 2 if ahead else n + 1)
                    if pair == 2:
                        pe.wait_ge(q["back_half"], n + 1)
                    for c in (2 * pair, 2 * pair + 1):
                        for g in range(2 if N > P else 1):
                            last = nc.tensor.transpose(PT[:, g, (c % 4) * P:(c % 4 + 1) * P], yT[:, c, g * P:(g + 1) * P],
                                                       T["ident"][:, :])
                            if pair == 2 and c == 4 and g == 0:
                                last.then_inc(free[5], 1)
                    if pair % 2:
                        last.then_inc(q["back_done"], 1)

                pe.wait_ge(q["act_ready"], 8 * n + 7)
                for c in range(DC):
                    pair = c // 2
                    if c % 4 == 0:
                        pe.wait_ge(loaded[4 + c // 4], 16 * n + 16)
                    if c % 2 == 0:
                        pe.wait_ge(q["yT_ready"], 4 * n + pair + 1)
                    for k in range(FC):
                        if c == 0 and k == FC - 1:
                            pe.wait_ge(q["act_ready"], 8 * n + 8)
                        last = nc.tensor.matmul(PY[:, pair % 2, c % 2, 0:N], w2[c // 4][:, k, (c % 4) * P:(c % 4 + 1) * P],
                                                act_T[:, k, 0:N], start=(k == 0), stop=(k == FC - 1))
                        if k == 0 and c % 4 == 0:
                            last.then_inc(free[4] if c else free[3], 1)
                    if c % 2:
                        last.then_inc(q["y_done"], 1)
                    if c == 1 and ahead:
                        turn(n + 1, 1, True)
                    if c % 2 and pair:
                        back(pair - 1)
                back(3)

            def group(n, e, j, count, ahead):
                def wide(N):
                    up(n, N, ahead)
                    if ahead:
                        turn(n + 1, 0, True)
                    down(n, N, ahead)

                if not first:
                    turn(n, 0, True)
                    turn(n, 1, True)
                pe.wait_ge(q["hT_ready"], n + 1)
                by_width(pe, count, wide)

            def start():
                turn(0, 0, False)
                turn(0, 1, False)

            groups(pe, group, start)

        @block.scalar
        def _(act):
            def copy_turned(n):
                whole = PT[:, :, :].rearrange("p a (b c) -> p (a b) c", c=P)
                act.wait_ge(q["turned0"], n + 1)
                nc.scalar.activation(hT[:, :, 0:P], whole, ACT.Copy).then_inc(q["hT_copy"], 1)
                act.wait_ge(q["turned1"], n + 1)
                nc.scalar.activation(hT[:, :, P:GROUP], whole, ACT.Copy).then_inc(q["hT_ready"], 1)

            def sigmoids(n, N):
                for c in range(FC):
                    act.wait_ge(q["glu_ready"], 8 * n + c + 1)
                    nc.scalar.activation(sig[:, c % 2, 0:N], glu[:, c % 2, 0:N], ACT.Sigmoid, scale=ALPHA).then_inc(q["sig_ready"], 1)

            def group(n, e, j, count, ahead):
                if not first:
                    copy_turned(n)
                by_width(act, count, lambda N: sigmoids(n, N))
                if ahead:
                    ahead[0]()
                    copy_turned(n + 1)

            groups(act, group, lambda: copy_turned(0))

        @block.vector
        def _(dve):
            seconds = dve.alloc_register(tag + "dve_seconds")
            dve.reg_mov(seconds, 0)
            dve.sem_inc(q["u_used"], 4)
            dve.sem_inc(q["back_used"], 1)
            dve.sem_inc(q["yT_ready"], 2)
            LINKS = 3 + 2 * FC
            nc.vector.memset(yT[:, :, :], 0.0).then_inc(q["init"], 1)
            dve.wait_ge(q["init"], 2)
            dve.wait_ge(q["bias_in"], 16)

            def gated(n, N):
                for c in range(FC):
                    b = c % 2
                    dve.wait_ge(q["u_done"], 8 * n + c + 1)
                    nc.vector.tensor_scalar(glu[:, b, 0:N], PU[:, c % 4, 0, 0:N], bias[:, c:c + 1], LIMIT,
                                            ALU.add, ALU.min).then_inc(q["glu_ready"], 1)
                    nc.vector.tensor_scalar(lin[:, b, 0:N], PU[:, c % 4, 1, 0:N], bias[:, FC + c:FC + c + 1], LIMIT,
                                            ALU.add, ALU.min).then_inc(q["u_used"], 1)
                    dve.wait_ge(q["u_used"], 8 * n + c + 5)
                    nc.vector.tensor_scalar(lin[:, b, 0:N], lin[:, b, 0:N], -LIMIT, 1.0, ALU.max, ALU.add).then_inc(q["links"], 1)
                    dve.wait_ge(q["links"], LINKS * n + 3 + 2 * c + 1)
                    nc.vector.tensor_tensor(lin[:, b, 0:N], lin[:, b, 0:N], glu[:, b, 0:N], ALU.mult).then_inc(q["links"], 1)
                    dve.wait_ge(q["links"], LINKS * n + 3 + 2 * c + 2)
                    dve.wait_ge(q["sig_ready"], 8 * n + c + 1)
                    nc.vector.tensor_tensor(act_T[:, c, 0:N], lin[:, b, 0:N], sig[:, b, 0:N], ALU.mult).then_inc(q["act_ready"], 1)

            def outputs(n, N, pair):
                dve.wait_ge(q["y_done"], 4 * n + pair + 1)
                for c in range(2):
                    f = 2 * pair + c
                    last = nc.vector.tensor_scalar(yT[:, f, 0:N], PY[:, pair % 2, c, 0:N], bias[:, 2 * FC + f:2 * FC + f + 1],
                                                   None, ALU.add)
                last.then_inc(q["yT_ready"], 1)

            def finish(n, N, half):
                cols = slice(half * BANK, (half + 1) * BANK)
                dve.wait_ge(q["back_done"], 2 * n + half + 1)
                if half == 0:
                    dve.wait_ge(q["scat0"], 16 * n + 16)
                    if N > P:
                        dve.wait_ge(q["scat1"], 16 * dve.snap(seconds) + 16)
                for g in range(2 if N > P else 1):
                    last = nc.vector.tensor_scalar(ysb[:, g, cols], PT[:, g, :], gate[:, g:g + 1], None, ALU.mult)
                last.then_inc(q["back_used"] if half else q["back_half"], 1)

            def wide(n, N):
                gated(n, N)
                for pair in range(3):
                    outputs(n, N, pair)
                finish(n, N, 0)
                outputs(n, N, 3)
                finish(n, N, 1)
                if N > P:
                    dve.reg_add(seconds, seconds, 1)

            def group(n, e, j, count, ahead):
                dve.wait_ge(q["back_used"], n + 1)
                nc.vector.tensor_copy(bias[:, :], bias_all[:, bass.ds(e, 1), :].rearrange("p a b -> p (a b)")).then_inc(q["links"], 1)
                for g in range(2):
                    slot = e * LIST_K + 2 * j + g
                    nc.vector.tensor_copy(gate[:, g:g + 1], T["slots"][:, bass.ds(slot, 1), 1].bitcast(F32)).then_inc(q["links"], 1)
                dve.wait_ge(q["links"], LINKS * n + 3)
                dve.sem_inc(q["held"], 1)
                if ahead:
                    ahead[0]()
                by_width(dve, count, lambda N: wide(n, N))

            groups(dve, group)

        @block.gpsimd
        def _(pool):
            seconds_out = pool.alloc_register(tag + "pool_seconds_out")
            pool.reg_mov(seconds_out, 0)
            nc.gpsimd.memset(ysb[:, :, :], 0.0).then_inc(q["init"], 1)
            nc.gpsimd.iota(idx_out[:, :], pattern=[[0, 2]], base=S, channel_multiplier=1).then_inc(q["pool_copy"], 1)
            pool.wait_ge(q["init"], 2)
            pool.wait_ge(q["pool_copy"], 1)

            def hold(sem, value):
                pool.wait_ge(sem, value)
                pool.sem_inc(q["held"], 1)

            def add_rows(g):
                nc.gpsimd.indirect_dma_start(
                    out=T["out"], out_offset=bass.IndirectOffsetOnAxis(ap=idx_out[:, g:g + 1], axis=0),
                    in_=ysb[:, g, :], in_offset=None, compute_op=ALU.add).then_inc(q[f"scat{g}"], 16)

            def gather(g):
                nc.gpsimd.indirect_dma_start(
                    out=hg[:, g, :], out_offset=None, in_=T["h_rows"],
                    in_offset=bass.IndirectOffsetOnAxis(ap=idx_in[:, g:g + 1], axis=0)).then_inc(q[f"gathered{g}"], 16)

            def zeros():
                add_rows(0)
                pool.wait_ge(q["scat0"], 16)
                add_rows(1)

            def fetch(n, e, j, count, copied):
                for g in range(2):
                    slot = e * LIST_K + 2 * j + g
                    nc.gpsimd.tensor_copy(idx_in[:, g:g + 1], T["slots"][:, bass.ds(slot, 1), 0]).then_inc(q["pool_copy"], 1)
                hold(q["pool_copy"], copied)
                gather(0)
                gather(1)

            def scatter(n, e, j, count, copied):
                hold(q["scat0"], 16 * n + 16)
                hold(q["scat1"], 16 * pool.snap(seconds_out) + 16)
                for g in range(2):
                    slot = e * LIST_K + 2 * j + g
                    nc.gpsimd.tensor_copy(idx_out[:, g:g + 1], T["slots"][:, bass.ds(slot, 1), 0]).then_inc(q["pool_copy"], 1)
                hold(q["pool_copy"], copied)
                hold(q["back_used"], n + 2)
                add_rows(0)

                def second():
                    hold(q["scat0"], 16 * n + 32)
                    add_rows(1)
                    pool.reg_add(seconds_out, seconds_out, 1)

                if first:
                    with pool.If(count > P):
                        second()
                    pool.nop()
                else:
                    second()

            def group(n, e, j, count, ahead):
                if first:
                    hold(q["turned0"], n + 1)
                    hold(q["turned1"], n + 1)
                    if ahead:
                        ahead[0]()
                        fetch(n + 1, e + 1, 0, ahead[1](), 4 * n + 5)
                        scatter(n, e, j, count, 4 * n + 7)
                    else:
                        scatter(n, e, j, count, 4 * n + 5)
                else:
                    fetch(n, e, j, count, 4 * n + 3)
                    scatter(n, e, j, count, 4 * n + 5)

            def start():
                fetch(0, 0, 0, count_of(pool, 0), 3)
                zeros()

            if not first:
                zeros()
            groups(pool, group, start)
            hold(q["scat0"], 16)
            hold(q["scat1"], 16 * pool.snap(seconds_out) + 16)


HD = 64
RW = 512
NSA_COLS = 1304
QH = 8
HEADS12 = 12
N_CMP = 63
CMP_H = 256
SCALE = HD ** -0.5
NEG = -1e30


def norm_phase(nc, T):
    with ExitStack() as ctx:
        sb = lambda n, s, dt=F32: ctx.enter_context(nc.sbuf_tensor(n, s, dt))
        xt = T["yT"]
        junk = sb("n_junk", [P, D])
        st = sb("n_st", [P, 2, NT])
        g1 = sb("n_g1", [P, DC])
        PT = ctx.enter_context(nc.psum_tensor("n_PT", [P, 4, BANK], F32))
        q = sems(nc, ctx, "n_c n_ss n_ms n_sq n_rs n_xn n_tp n_ev_a n_ev_d n_w " + " ".join(f"n_x{i}" for i in range(NT)))
        loaded = [q[f"n_x{i}"] for i in range(NT)]
        block = ctx.enter_context(nc.Block())

        @block.sync
        def _(sp):
            for i in range(NT):
                sp.dma_start(xt[:, i, :], T["x"][0, i * P:(i + 1) * P, :]).then_inc(loaded[i], 16)
            sp.dma_start(T["ident"][:, :], T["c_ident"]).then_inc(q["n_c"], 16)
            sp.dma_start(g1[:, :], T["ln1_cols"]).then_inc(q["n_c"], 16)
            for k in range(DC):
                sp.dma_start(T["w_nsa"][:, k, :], T["w_in"][0, k * P:(k + 1) * P, 3 * RW:3 * RW + NSA_COLS]).then_inc(q["n_w"], 16)
            sp.wait_ge(q["n_w"], 16 * DC)

        @block.scalar
        def _(act):
            for i in range(NT):
                act.wait_ge(loaded[i], 16)
                if i:
                    act.wait_ge(q["n_ss"], i)
                nc.scalar.activation(junk[:, :], xt[:, i, :], ACT.Square, accum_out=st[:, 0, i:i + 1]).then_inc(q["n_ss"], 1)
            act.wait_ge(q["n_ms"], 1)
            nc.scalar.activation(st[:, 1, :], st[:, 1, :], ACT.Sqrt).then_inc(q["n_sq"], 1)
            act.wait_ge(q["n_c"], 32)
            for u in range(1, 2 * DC, 2):
                act.wait_ge(q["n_tp"], u + 1)
                c, half = u // 2, u % 2
                nc.scalar.activation(T["xnT"][:, c, 1 + half * BANK:1 + (half + 1) * BANK], PT[:, u % 4, :], ACT.Copy,
                                     scale=g1[:, c:c + 1]).then_inc(q["n_ev_a"], 1)

        @block.vector
        def _(dve):
            nc.vector.memset(T["xnT"][:, :, 0], 0.0)
            dve.wait_ge(q["n_ss"], NT)
            nc.vector.tensor_scalar(st[:, 1, :], st[:, 0, :], 1.0 / D, EPS, ALU.mult, ALU.add).then_inc(q["n_ms"], 1)
            dve.wait_ge(q["n_sq"], 1)
            nc.vector.reciprocal(st[:, 0, :], st[:, 1, :]).then_inc(q["n_rs"], 1)
            dve.wait_ge(q["n_rs"], 1)
            for i in range(NT):
                nc.vector.tensor_scalar(xt[:, i, :], xt[:, i, :], st[:, 0, i:i + 1], None, ALU.mult).then_inc(q["n_xn"], 1)
            dve.wait_ge(q["n_c"], 32)
            for u in range(0, 2 * DC, 2):
                dve.wait_ge(q["n_tp"], u + 1)
                c = u // 2
                nc.vector.tensor_scalar(T["xnT"][:, c, 1:1 + BANK], PT[:, u % 4, :], g1[:, c:c + 1], None,
                                        ALU.mult).then_inc(q["n_ev_d"], 1)

        @block.tensor
        def _(pe):
            pe.wait_ge(q["n_c"], 32)
            for u in range(2 * DC):
                c, half = u // 2, u % 2
                pe.wait_ge(q["n_xn"], 4 * half + 4 if u < 2 else NT)
                if u >= 4:
                    pe.wait_ge(q["n_ev_a"] if u % 2 else q["n_ev_d"], (u - 4) // 2 + 1)
                for t in range(4):
                    i = 4 * half + t
                    last = nc.tensor.transpose(PT[:, u % 4, t * P:(t + 1) * P], xt[:, i, c * P:(c + 1) * P], T["ident"][:, :])
                last.then_inc(q["n_tp"], 1)


def nsa_project_phase(nc, T, N):
    with ExitStack() as ctx:
        sb = lambda n, s, dt=F32: ctx.enter_context(nc.sbuf_tensor(n, s, dt))
        pb = lambda n, s: ctx.enter_context(nc.psum_tensor(n, s, F32))
        W = T["w_nsa"]
        heads = sb("p_heads", [P, 2, HEADS12, HD])
        rot = sb("p_rot", [P, 2, HEADS12, HD])
        tmp = sb("p_tmp", [P, HEADS12, HD])
        cmp_in = sb("p_cmpin", [P, 2, 4, 2, HD])
        rotk = sb("p_rotk", [P, 2, 4, 2, HD])
        rs = sb("p_rs", [P, 2, HEADS12])
        ms = sb("p_ms", [P, 2, HEADS12])
        gain = sb("p_gain", [P, 3, HD])
        cos = sb("p_cos", [P, NT, HD // 2])
        sin = sb("p_sin", [P, NT, HD // 2])
        PP = pb("p_PP", [P, 3, BANK])
        PT = pb("p_PT", [P, 4, BANK])
        q = sems(nc, ctx, "p_c p_mm p_eva p_evd p_sum p_sq p_dve p_n p_r p_tp p_out p_gate p_gl")
        block = ctx.enter_context(nc.Block())
        bounds = ((0, 512), (512, 1024), (1024, NSA_COLS))

        @block.sync
        def _(sp):
            sp.dma_start(gain[:, 0, :], T["nsa_qn_g"].broadcast_to([P, HD])).then_inc(q["p_c"], 16)
            for j in (1, 2):
                sp.dma_start(gain[:, j, :], T["nsa_kn_g"][0, j:j + 1, :].broadcast_to([P, HD])).then_inc(q["p_c"], 16)
            sp.dma_start(cos[:, :, :], T["c_cos"].rearrange("(t p) k -> p t k", p=P)).then_inc(q["p_c"], 16)
            sp.dma_start(sin[:, :, :], T["c_sin"].rearrange("(t p) k -> p t k", p=P)).then_inc(q["p_c"], 16)

        @block.tensor
        def _(pe):
            def project(i):
                if i:
                    pe.wait_ge(q["p_eva"], i)
                    pe.wait_ge(q["p_evd"], i)
                for n, (a, b) in enumerate(bounds):
                    for k in range(DC):
                        last = nc.tensor.matmul(PP[:, n, 0:b - a], T["xnT"][:, k, 1 + i * P:1 + (i + 1) * P], W[:, k, a:b],
                                                start=(k == 0), stop=(k == DC - 1))
                last.then_inc(q["p_mm"], 1)

            def transposes(i):
                s = i % 2
                pe.wait_ge(q["p_n"], i + 1)
                pe.wait_ge(q["p_r"], i + 1)
                pe.wait_ge(q["p_eva"], i + 1)
                if i:
                    pe.wait_ge(q["p_out"], 5 * i)
                twice = lambda v: v.rearrange("p a b -> p (a b)")
                for p in range(4):
                    nc.tensor.transpose(PT[:, 0, p * P:(p + 1) * P],
                                        heads[:, s, 2 * p:2 * p + 2, :].rearrange("p a b -> p (a b)"), T["ident"][:, :])
                    nc.tensor.transpose(PT[:, 1, p * P:(p + 1) * P],
                                        rot[:, s, 2 * p:2 * p + 2, :].rearrange("p a b -> p (a b)"), T["ident"][:, :])
                    nc.tensor.transpose(PT[:, 2, p * P:(p + 1) * P], twice(rotk[:, s, p, :, :]), T["ident"][:, :])
                    last = nc.tensor.transpose(PT[:, 3, p * P:(p + 1) * P],
                                               twice(cmp_in[:, s, p, :, :]), T["ident"][:, :])
                last.then_inc(q["p_tp"], 1)

            project(0)
            for i in range(NT):
                if i + 1 < NT:
                    project(i + 1)
                transposes(i)

        @block.scalar
        def _(act):
            def evac(i):
                s = i % 2
                act.wait_ge(q["p_mm"], i + 1)
                if i >= 2:
                    act.wait_ge(q["p_tp"], i - 1)
                for c in range(2):
                    nc.scalar.activation(cmp_in[:, s, :, c, :], PP[:, 1, 0:256].rearrange("p (a b) -> p a b", b=HD), ACT.Copy)
                nc.scalar.activation(heads[:, s, 8:10, :].rearrange("p a b -> p (a b)"), PP[:, 1, 256:384], ACT.Copy)
                nc.scalar.activation(heads[:, s, 10:12, :].rearrange("p a b -> p (a b)"), PP[:, 2, 0:128], ACT.Copy)
                nc.scalar.activation(N["vs"][:, i, :], PP[:, 1, 384:512], ACT.Copy)
                nc.scalar.activation(N["vw"][:, i, :], PP[:, 2, 128:256], ACT.Copy)
                nc.scalar.activation(N["gates"][:, i, :], PP[:, 2, 256:280], ACT.Copy).then_inc(q["p_eva"], 1)

            def outs(i):
                tok = slice(i * P, (i + 1) * P)
                view = lambda g: PT[:, g, :].rearrange("p (a b) -> p a b", b=P)
                act.wait_ge(q["p_tp"], i + 1)
                nc.scalar.activation(N["qT"][:, :, tok], view(0), ACT.Copy).then_inc(q["p_out"], 1)
                nc.scalar.activation(N["qrT"][:, :, tok], view(1), ACT.Copy).then_inc(q["p_out"], 1)
                nc.scalar.activation(N["kT"][:, :, tok], view(2), ACT.Copy).then_inc(q["p_out"], 1)
                nc.scalar.activation(N["cT"][0:HD, :, 1 + i * P:1 + (i + 1) * P], PT[0:HD, 3, :].rearrange("p (a b) -> p a b", b=P),
                                     ACT.Copy).then_inc(q["p_out"], 1)
                nc.scalar.activation(N["cT"][HD:P, :, i * P:(i + 1) * P], PT[HD:P, 3, :].rearrange("p (a b) -> p a b", b=P),
                                     ACT.Copy).then_inc(q["p_out"], 1)

            evac(0)
            for i in range(NT):
                act.wait_ge(q["p_sum"], i + 1)
                nc.scalar.activation(rs[:, i % 2, :], ms[:, i % 2, :], ACT.Sqrt).then_inc(q["p_sq"], 1)
                if i + 1 < NT:
                    evac(i + 1)
                outs(i)
            act.wait_ge(q["p_eva"], NT)
            nc.scalar.activation(N["gates"][:, :, :], N["gates"][:, :, :], ACT.Sigmoid)

        @block.vector
        def _(dve):
            link = chained(dve, q["p_dve"])
            dve.wait_ge(q["p_c"], 16 * 5)
            for i in range(NT):
                s = i % 2
                H = heads[:, s, :, :]
                dve.wait_ge(q["p_mm"], i + 1)
                if i >= 2:
                    dve.wait_ge(q["p_tp"], i - 1)
                nc.vector.tensor_copy(heads[:, s, 0:8, :].rearrange("p a b -> p (a b)"), PP[:, 0, :]).then_inc(q["p_evd"], 1)
                dve.wait_ge(q["p_evd"], i + 1)
                dve.wait_ge(q["p_eva"], i + 1)
                link(nc.vector.tensor_tensor(tmp[:, :, :], H, H, ALU.mult))
                link(nc.vector.tensor_reduce(ms[:, s, :], tmp[:, :, :], AX.X, ALU.add))
                nc.vector.tensor_scalar(ms[:, s, :], ms[:, s, :], 1.0 / HD, EPS, ALU.mult, ALU.add).then_inc(q["p_sum"], 1)
                dve.wait_ge(q["p_sq"], i + 1)
                link(nc.vector.reciprocal(rs[:, s, :], rs[:, s, :]))
                link(nc.vector.tensor_tensor(H, H, rs[:, s, :, None].broadcast_to([P, HEADS12, HD]), ALU.mult))
                for j, (a, b) in enumerate(((0, QH), (QH, QH + 2), (QH + 2, HEADS12))):
                    last = nc.vector.tensor_tensor(H[:, a:b, :], H[:, a:b, :], gain[:, j, None, :].broadcast_to([P, b - a, HD]),
                                                   ALU.mult)
                last.then_inc(q["p_n"], 1)
                dve.wait_ge(q["p_n"], i + 1)
                half = HD // 2
                lo, hi = H[:, :, 0:half], H[:, :, half:HD]
                cs = cos[:, i, None, :].broadcast_to([P, HEADS12, half])
                sn = sin[:, i, None, :].broadcast_to([P, HEADS12, half])
                R = rot[:, s, :, :]
                link(nc.vector.tensor_tensor(tmp[:, :, 0:half], hi, sn, ALU.mult))
                link(nc.vector.tensor_tensor(tmp[:, :, half:HD], lo, sn, ALU.mult))
                link(nc.vector.tensor_tensor(R[:, :, 0:half], lo, cs, ALU.mult))
                link(nc.vector.tensor_tensor(R[:, :, half:HD], hi, cs, ALU.mult))
                link(nc.vector.tensor_tensor(R[:, :, 0:half], R[:, :, 0:half], tmp[:, :, 0:half], ALU.subtract))
                link(nc.vector.tensor_tensor(R[:, :, half:HD], R[:, :, half:HD], tmp[:, :, half:HD], ALU.add))
                nc.vector.tensor_copy(rotk[:, s, :, 0, :], R[:, QH:HEADS12, :])
                nc.vector.tensor_copy(rotk[:, s, :, 1, :], R[:, QH:HEADS12, :]).then_inc(q["p_r"], 1)
                dve.wait_ge(q["p_r"], i + 1)


def compress_phase(nc, T, N):
    with ExitStack() as ctx:
        sb = lambda n, s, dt=F32: ctx.enter_context(nc.sbuf_tensor(n, s, dt))
        pb = lambda n, s: ctx.enter_context(nc.psum_tensor(n, s, F32))
        W1 = sb("c_W1", [P, 2, 16, CMP_H])
        W2 = sb("c_W2", [P, 2, 2, HD])
        pe_rows = sb("c_pe", [32, P])
        peT = sb("c_peT", [P, 32])
        bias_row = sb("c_bias_row", [1, 4 * P])
        bias = sb("c_bias", [P, 4])
        hid = sb("c_hid", [P, 4, 2 * N_CMP])
        kg = sb("c_kg", [N_CMP, HD])
        kc = sb("c_kc", [N_CMP, 2, HD])
        kc2 = sb("c_kc2", [N_CMP, 2, 2, HD])
        tmp = sb("c_tmp", [N_CMP, 2, HD])
        ms = sb("c_ms", [N_CMP, 2])
        PH = pb("c_PH", [P, 4, BANK])
        PB = pb("c_PB", [P, BANK])
        PO = pb("c_PO", [P, BANK])
        PT = pb("c_PT", [P, BANK])
        q = sems(nc, ctx, "c_w c_pet c_pete c_b c_row c_col c_be c_h c_g c_o c_v c_ms c_sq c_k c_kt c_dve")
        block = ctx.enter_context(nc.Block())

        @block.sync
        def _(sp):
            for i in range(2):
                sp.dma_start(W1[:, i, :, :], T["nsa_cmp_w1"][0, i].rearrange("(m two) d f -> (two d) m f", two=2)).then_inc(q["c_w"], 16)
                sp.dma_start(W2[:, i, :, :], T["nsa_cmp_w2"][0, i].rearrange("(c p) d -> p c d", p=P)).then_inc(q["c_w"], 16)
            sp.dma_start(pe_rows[:, :], T["nsa_pe"][0].rearrange("i (m two) d -> (i m) (two d)", two=2)).then_inc(q["c_w"], 16)
            sp.dma_start(kg[:, :], T["nsa_kn_g"][0, 0:1, :].broadcast_to([N_CMP, HD])).then_inc(q["c_w"], 16)

        @block.tensor
        def _(pe):
            pe.wait_ge(q["c_w"], 16 * 6)
            nc.tensor.transpose(PT[:, 0:32], pe_rows[:, :], T["ident"][0:32, 0:32]).then_inc(q["c_pet"], 1)
            pe.wait_ge(q["c_pete"], 1)
            for i in range(2):
                for m in range(16):
                    last = nc.tensor.matmul(PB[0:1, i * CMP_H:(i + 1) * CMP_H], peT[:, 16 * i + m:16 * i + m + 1],
                                            W1[:, i, m, :], start=(m == 0), stop=(m == 15))
            last.then_inc(q["c_b"], 1)
            for i in range(2):
                for f in range(2):
                    u = 2 * i + f
                    for m in range(16):
                        last = nc.tensor.matmul(PH[:, u, 0:2 * N_CMP], W1[:, i, m, f * P:(f + 1) * P],
                                                N["cT"][:, 2 * i:2 * i + 2, 1 + 2 * m:1 + 2 * m + 16 * (N_CMP - 1) + 1:16],
                                                start=(m == 0), stop=(m == 15))
                    last.then_inc(q["c_h"], 1)
                    if u == 0:
                        pe.wait_ge(q["c_row"], 1)
                        for j in range(4):
                            last = nc.tensor.transpose(PT[:, BANK // 4 + j:BANK // 4 + j + 1], bias_row[:, j * P:(j + 1) * P],
                                                       T["ident"][0:1, 0:1])
                        last.then_inc(q["c_col"], 1)
            pe.wait_ge(q["c_g"], 4)
            for i in range(2):
                for h in range(2):
                    u = 2 * i + h
                    for f in range(2):
                        last = nc.tensor.matmul(PO[0:N_CMP, u * HD:(u + 1) * HD],
                                                hid[:, 2 * i + f, h * N_CMP:(h + 1) * N_CMP], W2[:, i, f, :],
                                                start=(f == 0), stop=(f == 1))
            last.then_inc(q["c_o"], 1)
            pe.wait_ge(q["c_k"], 1)
            for h in range(2):
                last = nc.tensor.transpose(PT[:, BANK // 2 + h * N_CMP:BANK // 2 + (h + 1) * N_CMP],
                                           kc2[:, h, :, :].rearrange("p a b -> p (a b)"), T["ident"][0:N_CMP, 0:N_CMP])
            last.then_inc(q["c_kt"], 1)

        @block.scalar
        def _(act):
            act.wait_ge(q["c_be"], 1)
            for u in range(4):
                act.wait_ge(q["c_h"], u + 1)
                nc.scalar.activation(hid[:, u, :], PH[:, u, 0:2 * N_CMP], ACT.Gelu_apprx_tanh,
                                     bias=bias[:, u:u + 1]).then_inc(q["c_g"], 1)
            act.wait_ge(q["c_ms"], 1)
            nc.scalar.activation(ms[:, :], ms[:, :], ACT.Sqrt).then_inc(q["c_sq"], 1)

        @block.vector
        def _(dve):
            link = chained(dve, q["c_dve"])
            dve.wait_ge(q["c_pet"], 1)
            nc.vector.tensor_copy(peT[:, :], PT[:, 0:32]).then_inc(q["c_pete"], 1)
            dve.wait_ge(q["c_b"], 1)
            nc.vector.tensor_copy(bias_row[:, :], PB[0:1, :]).then_inc(q["c_row"], 1)
            dve.wait_ge(q["c_col"], 1)
            nc.vector.tensor_copy(bias[:, :], PT[:, BANK // 4:BANK // 4 + 4]).then_inc(q["c_be"], 1)
            dve.wait_ge(q["c_o"], 1)
            link(nc.vector.tensor_copy(kc[:, :, :], PO[0:N_CMP, 0:2 * HD].rearrange("p (a b) -> p a b", b=HD)))
            nc.vector.tensor_copy(N["vcmp"][:, :, :], PO[0:N_CMP, 2 * HD:4 * HD].rearrange("p (a b) -> p a b", b=HD))
            link(nc.vector.tensor_tensor(tmp[:, :, :], kc[:, :, :], kc[:, :, :], ALU.mult))
            link(nc.vector.tensor_reduce(ms[:, :], tmp[:, :, :], AX.X, ALU.add))
            nc.vector.tensor_scalar(ms[:, :], ms[:, :], 1.0 / HD, EPS, ALU.mult, ALU.add).then_inc(q["c_ms"], 1)
            dve.wait_ge(q["c_sq"], 1)
            link(nc.vector.reciprocal(ms[:, :], ms[:, :]))
            link(nc.vector.tensor_tensor(kc[:, :, :], kc[:, :, :], ms[:, :, None].broadcast_to([N_CMP, 2, HD]), ALU.mult))
            for c in range(2):
                last = nc.vector.tensor_tensor(kc2[:, :, c, :], kc[:, :, :], kg[:, None, :].broadcast_to([N_CMP, 2, HD]),
                                               ALU.mult)
            last.then_inc(q["c_k"], 1)
            dve.wait_ge(q["c_kt"], 1)
            nc.vector.tensor_copy(N["kcT"][:, :, :], PT[:, BANK // 2:BANK // 2 + 2 * N_CMP].rearrange("p (a b) -> p a b", b=N_CMP))


def attention_phase(nc, T, N):
    KW = S + 3 * P
    with ExitStack() as ctx:
        sb = lambda n, s, dt=F32: ctx.enter_context(nc.sbuf_tensor(n, s, dt))
        pb = lambda n, s: ctx.enter_context(nc.psum_tensor(n, s, F32))
        cmask = sb("a_cmask", [P, NT, N_CMP])
        cpen = sb("a_cpen", [P, NT, N_CMP])
        wpen = sb("a_wpen", [P, 3 * P])
        free16 = sb("a_free", [P, NT, 16])
        force16 = sb("a_force", [P, NT, 16])
        lower16 = sb("a_lower", [P, 16, 16])
        sc = sb("a_sc", [P, 4, N_CMP])
        pc = sb("a_pc", [P, 4, N_CMP])
        pcT = sb("a_pcT", [N_CMP, 4, P])
        small = sb("a_small", [P, 4, 4])
        ps = sb("a_ps", [P, 65])
        imp = sb("a_imp", [P, 16])
        c1 = sb("a_c1", [P, 16, 16])
        c2 = sb("a_c2", [P, 16, 16])
        bpen = sb("a_bpen", [P, 16])
        pen = sb("a_pen", [P, S])
        Sc = sb("a_S", [P, 3, KW])
        pT = sb("a_pT", [P, 2, 11, P])
        mm = sb("a_mm", [P, 3, 2])
        nm = sb("a_nm", [P, 3, 2])
        dn = sb("a_dn", [P, 3, 2])
        rd = sb("a_rd", [P, 3, 2])
        oN = sb("a_oN", [P, 2, QH, HD])
        gsc = sb("a_gsc", [P, 3, 2])
        PSel = pb("a_PSel", [P, 3, BANK])
        PC = pb("a_PC", [P, BANK])
        PT = pb("a_PT", [P, 2, BANK])
        POc = pb("a_POc", [P, BANK])
        PO = pb("a_PO", [P, BANK])
        q = sems(nc, ctx, "a_c a_cs a_csd a_cm a_ce a_cp a_ct a_cte a_co a_cod a_sp a_sd a_m a_e a_tp a_te a_po "
                          "a_pod a_od a_oT a_oTe a_dve a_half")
        block = ctx.enter_context(nc.Block())
        steps = [(i, kv) for i in range(NT) for kv in range(2)]

        def banks_of(i):
            tiles = [(j, S * 0 + j) for j in range(i + 1)]
            wins = [j for j in range(max(0, i - 2), i + 1)]
            cols = [("s", j, j * P) for j, _ in tiles] + [("w", j, S + (j - i + 2) * P) for j in wins]
            return [cols[a:a + 4] for a in range(0, len(cols), 4)]

        heads = [(i, kv, g) for i, kv in steps for g in range(4)]
        group_base = {}
        n = 0
        for u, (i, kv, g) in enumerate(heads):
            group_base[u] = n
            n += len(banks_of(i))

        @block.sync
        def _(sp):
            for dst, src in ((cmask, T["c_cmask"]), (cpen, T["c_cpen"]), (free16, T["c_free"]), (force16, T["c_force"])):
                sp.dma_start(dst[:, :, :], src.rearrange("(t p) n -> p t n", p=P)).then_inc(q["a_c"], 16)
            sp.dma_start(wpen[:, :], T["c_wpen"]).then_inc(q["a_c"], 16)
            sp.dma_start(lower16[:, :, :].rearrange("p a b -> p (a b)"), T["c_lower16"].broadcast_to([P, 256])).then_inc(q["a_c"], 16)

        @block.tensor
        def _(pe):
            def cmp_scores(s):
                i, kv = steps[s]
                if s:
                    pe.wait_ge(q["a_csd"], s)
                    pe.wait_ge(q["a_cod"], s)
                for g in (0, 2, 1, 3):
                    h = 4 * kv + g
                    r = slice(HD * (h % 2), HD * (h % 2) + HD)
                    if g == 1:
                        last.then_inc(q["a_half"], 1)
                        pe.wait_ge(q["a_half"], s + 1)
                    last = nc.tensor.matmul(PC[:, g * HD:g * HD + N_CMP], N["qT"][r, h // 2, i * P:(i + 1) * P],
                                            N["kcT"][r, kv, :], start=True, stop=True)
                last.then_inc(q["a_cs"], 1)

            def cmp_turn(s):
                i, kv = steps[s]
                pe.wait_ge(q["a_cp"], s + 1)
                turned = i - 1 if kv == 0 else i
                if turned > 0:
                    pe.wait_ge(q["a_oTe"], turned)
                for g in range(4):
                    last = nc.tensor.transpose(POc[0:N_CMP, g * P:(g + 1) * P], pc[:, g, :], T["ident"][:, :])
                last.then_inc(q["a_ct"], 1)

            def cmp_out(s):
                i, kv = steps[s]
                pe.wait_ge(q["a_cte"], s + 1)
                for g in range(4):
                    last = nc.tensor.matmul(PC[:, 256 + g * HD:256 + (g + 1) * HD], pcT[:, g, :], N["vcmp"][:, kv, :],
                                            start=True, stop=True)
                last.then_inc(q["a_co"], 1)

            def scores(u):
                i, kv, g = heads[u]
                h = 4 * kv + g
                r = slice(HD * (h % 2), HD * (h % 2) + HD)
                if u:
                    pe.wait_ge(q["a_sd"], u)
                lhs = N["qrT"][r, h // 2, i * P:(i + 1) * P]
                for b in range(0, (i + 1) * P, BANK):
                    n = min(BANK, (i + 1) * P - b)
                    nc.tensor.matmul(PSel[:, b // BANK, 0:n], lhs, N["kT"][r, kv, b:b + n], start=True, stop=True)
                lo = max(0, i - 2)
                last = nc.tensor.matmul(PSel[:, 2, (lo - i + 2) * P:3 * P], lhs, N["kT"][r, 2 + kv, lo * P:(i + 1) * P],
                                        start=True, stop=True)
                last.then_inc(q["a_sp"], 1)

            def turn(u, n):
                i, kv, g = heads[u]
                at = group_base[u] + n
                if n == 0:
                    pe.wait_ge(q["a_e"], 2 * u + 2)
                if at >= 2:
                    pe.wait_ge(q["a_te"], at - 1)
                for c, (_, _, col) in enumerate(banks_of(i)[n]):
                    last = nc.tensor.transpose(PT[:, at % 2, c * P:(c + 1) * P], Sc[:, u % 3, col:col + P], T["ident"][:, :])
                last.then_inc(q["a_tp"], 1)

            def values(u, kind):
                i, kv, g = heads[u]
                if kind == "s":
                    if u:
                        pe.wait_ge(q["a_pod"], u)
                    pe.wait_ge(q["a_te"], group_base[u] + len(banks_of(i)))
                flat = [x for grp in banks_of(i) for x in grp]
                V, dst = (N["vs"], 0) if kind == "s" else (N["vw"], HD)
                mine = [(c, j) for c, (k, j, _) in enumerate(flat) if k == kind]
                for m, (c, j) in enumerate(mine):
                    last = nc.tensor.matmul(PO[:, dst:dst + HD], pT[:, u % 2, c, :], V[:, j, kv * HD:(kv + 1) * HD],
                                            start=(m == 0), stop=(m == len(mine) - 1))
                if kind == "w":
                    last.then_inc(q["a_po"], 1)

            def turn_out(i):
                pe.wait_ge(q["a_od"], i + 1)
                pe.wait_ge(q["a_cte"], min(2 * i + 3, len(steps)) - 1)
                for p in range(4):
                    last = nc.tensor.transpose(POc[:, p * P:(p + 1) * P],
                                               oN[:, i % 2, 2 * p:2 * p + 2, :].rearrange("p a b -> p (a b)"), T["ident"][:, :])
                last.then_inc(q["a_oT"], 1)

            cmp_scores(0)
            cmp_turn(0)
            cmp_out(0)
            for u in range(-2, len(heads)):
                if u + 2 < len(heads):
                    scores(u + 2)
                if u >= 0 and u % 4 == 0 and u // 4 + 1 < len(steps):
                    cmp_scores(u // 4 + 1)
                groups = len(banks_of(heads[u + 1][0])) if 0 <= u + 1 < len(heads) else 0
                for n in range(min(2, groups)):
                    turn(u + 1, n)
                if u >= 0:
                    i, kv, g = heads[u]
                    s = u // 4
                    more = s + 1 < len(steps)
                    if g == 2 and more:
                        cmp_turn(s + 1)
                    values(u, "s")
                for n in range(2, groups):
                    turn(u + 1, n)
                if u >= 0:
                    if g == 3 and more:
                        cmp_out(s + 1)
                    values(u, "w")
                    if g == 0 and kv == 0 and i:
                        turn_out(i - 1)
            turn_out(NT - 1)

        @block.scalar
        def _(act):
            def cmp_exp(s):
                act.wait_ge(q["a_cm"], s + 1)
                for g in range(4):
                    last = nc.scalar.activation(sc[:, g, :], sc[:, g, :], ACT.Exp, bias=small[:, 1, g:g + 1])
                last.then_inc(q["a_ce"], 1)

            def cmp_evac(s):
                act.wait_ge(q["a_ct"], s + 1)
                if s:
                    act.wait_ge(q["a_co"], s)
                nc.scalar.activation(pcT[:, :, :], POc[0:N_CMP, :].rearrange("p (a b) -> p a b", b=P),
                                     ACT.Copy).then_inc(q["a_cte"], 1)

            def exps(u):
                i, kv, g = heads[u]
                b = u % 3
                act.wait_ge(q["a_m"], u + 1)
                nc.scalar.activation(Sc[:, b, 0:(i + 1) * P], Sc[:, b, 0:(i + 1) * P], ACT.Exp, bias=nm[:, b, 0:1],
                                     accum_out=dn[:, b, 0:1]).then_inc(q["a_e"], 1)
                lo = S + (max(0, i - 2) - i + 2) * P
                nc.scalar.activation(Sc[:, b, lo:KW], Sc[:, b, lo:KW], ACT.Exp, bias=nm[:, b, 1:2],
                                     accum_out=dn[:, b, 1:2]).then_inc(q["a_e"], 1)

            def evacs(u):
                i, kv, g = heads[u]
                if u >= 2:
                    act.wait_ge(q["a_po"], u - 1)
                for n, grp in enumerate(banks_of(i)):
                    at = group_base[u] + n
                    act.wait_ge(q["a_tp"], at + 1)
                    nc.scalar.activation(pT[:, u % 2, 4 * n:4 * n + len(grp), :],
                                         PT[:, at % 2, 0:len(grp) * P].rearrange("p (a b) -> p a b", b=P),
                                         ACT.Copy).then_inc(q["a_te"], 1)

            def out_evac(i):
                act.wait_ge(q["a_oT"], i + 1)
                nc.scalar.activation(T["yT"][:, 4:8, i * P:(i + 1) * P], POc[:, :].rearrange("p (a b) -> p a b", b=P),
                                     ACT.Copy).then_inc(q["a_oTe"], 1)

            cmp_exp(0)
            cmp_evac(0)
            for u in range(-2, len(heads)):
                if 0 <= u + 1 < len(heads):
                    evacs(u + 1)
                if u >= 0:
                    i, kv, g = heads[u]
                    s = u // 4
                    if g == 2 and s + 1 < len(steps):
                        cmp_evac(s + 1)
                if u >= 0 and g == 0 and s + 1 < len(steps):
                    cmp_exp(s + 1)
                if u + 2 < len(heads):
                    exps(u + 2)
                if u >= 0:
                    if g == 0 and kv == 0 and i:
                        out_evac(i - 1)
            out_evac(NT - 1)

        @block.vector
        def _(dve):
            link = chained(dve, q["a_dve"])
            dve.wait_ge(q["a_c"], 16 * 6)
            link(nc.vector.memset(ps[:, :], 0.0))

            def cmp_masked(s):
                i, kv = steps[s]
                dve.wait_ge(q["a_cs"], s + 1)
                view = PC[:, 0:4 * HD].rearrange("p (a b) -> p a b", b=HD)[:, :, 0:N_CMP]
                nc.vector.scalar_tensor_tensor(out=sc[:, :, :], in0=view, scalar=SCALE,
                                               in1=cpen[:, i, None, :].broadcast_to([P, 4, N_CMP]),
                                               op0=ALU.mult, op1=ALU.add).then_inc(q["a_csd"], 1)
                dve.wait_ge(q["a_csd"], s + 1)
                link(nc.vector.tensor_reduce(small[:, 0, :], sc[:, :, :], AX.X, ALU.max))
                nc.vector.tensor_scalar(small[:, 1, :], small[:, 0, :], -1.0, None, ALU.mult).then_inc(q["a_cm"], 1)

            def cmp_norm(s):
                i, kv = steps[s]
                dve.wait_ge(q["a_ce"], s + 1)
                if s:
                    dve.wait_ge(q["a_ct"], s)
                link(nc.vector.tensor_tensor(sc[:, :, :], sc[:, :, :], cmask[:, i, None, :].broadcast_to([P, 4, N_CMP]),
                                             ALU.mult))
                link(nc.vector.tensor_reduce(small[:, 2, :], sc[:, :, :], AX.X, ALU.add))
                link(nc.vector.tensor_scalar(small[:, 2, :], small[:, 2, :], 1e-30, None, ALU.max))
                link(nc.vector.reciprocal(small[:, 3, :], small[:, 2, :]))
                nc.vector.tensor_tensor(pc[:, :, :], sc[:, :, :], small[:, 3, :, None].broadcast_to([P, 4, N_CMP]),
                                        ALU.mult).then_inc(q["a_cp"], 1)
                dve.wait_ge(q["a_cp"], s + 1)

            def importance(s):
                i, kv = steps[s]
                if i >= 4:
                    link(nc.vector.tensor_reduce(ps[:, 1:64], pc[:, :, :].rearrange("p a b -> p b a"), AX.X, ALU.add))
                    link(nc.vector.tensor_reduce(imp[:, :], ps[:, 0:64].rearrange("p (a b) -> p a b", b=4), AX.X, ALU.add))
                    link(nc.vector.tensor_tensor(imp[:, :], imp[:, :], ps[:, 4:65:4], ALU.add))
                    link(nc.vector.tensor_tensor(imp[:, :], imp[:, :], free16[:, i, :], ALU.mult))
                    link(nc.vector.tensor_tensor(imp[:, :], imp[:, :], force16[:, i, :], ALU.add))

            def select(s):
                i, kv = steps[s]
                keys = (i + 1) * P
                causal = wpen[:, 2 * P:3 * P]
                if i < 4:
                    link(nc.vector.memset(bpen[:, :], 0.0))
                else:
                    other = imp[:, None, :].broadcast_to([P, 16, 16])
                    own = imp[:, :, None].broadcast_to([P, 16, 16])
                    link(nc.vector.tensor_tensor(c1[:, :, :], other, own, ALU.is_gt))
                    link(nc.vector.tensor_tensor(c2[:, :, :], other, own, ALU.is_equal))
                    link(nc.vector.tensor_tensor(c2[:, :, :], c2[:, :, :], lower16[:, :, :], ALU.mult))
                    link(nc.vector.tensor_tensor(c1[:, :, :], c1[:, :, :], c2[:, :, :], ALU.add))
                    link(nc.vector.tensor_reduce(bpen[:, :], c1[:, :, :], AX.X, ALU.add))
                    link(nc.vector.tensor_scalar(bpen[:, :], bpen[:, :], 7.5, NEG, ALU.is_gt, ALU.mult))
                nb = keys // HD
                link(nc.vector.tensor_copy(pen[:, 0:keys].rearrange("p (a b) -> p a b", b=HD),
                                           bpen[:, 0:nb, None].broadcast_to([P, nb, HD])))
                link(nc.vector.tensor_tensor(pen[:, i * P:keys], pen[:, i * P:keys], causal, ALU.add))

            def masked(u, between=None):
                i, kv, g = heads[u]
                b = u % 3
                keys = (i + 1) * P
                lo = (max(0, i - 2) - i + 2) * P
                dve.wait_ge(q["a_sp"], u + 1)
                nc.vector.scalar_tensor_tensor(
                    out=Sc[:, b, 0:keys], in0=PSel[:, 0:2, :].rearrange("p a b -> p (a b)")[:, 0:keys], scalar=SCALE,
                    in1=pen[:, 0:keys], op0=ALU.mult, op1=ALU.add)
                nc.vector.scalar_tensor_tensor(out=Sc[:, b, S + lo:KW], in0=PSel[:, 2, lo:3 * P], scalar=SCALE,
                                               in1=wpen[:, lo:3 * P], op0=ALU.mult, op1=ALU.add).then_inc(q["a_sd"], 1)
                if between is not None:
                    between()
                dve.wait_ge(q["a_sd"], u + 1)
                nc.vector.tensor_reduce(mm[:, b, 0:1], Sc[:, b, 0:keys], AX.X, ALU.max)
                link(nc.vector.tensor_reduce(mm[:, b, 1:2], Sc[:, b, S + lo:KW], AX.X, ALU.max))
                nc.vector.tensor_scalar(nm[:, b, :], mm[:, b, :], -1.0, None, ALU.mult).then_inc(q["a_m"], 1)

            def combine(u):
                i, kv, g = heads[u]
                h = 4 * kv + g
                b = u % 3
                o = oN[:, i % 2, h, :]
                dve.wait_ge(q["a_e"], 2 * u + 2)
                link(nc.vector.reciprocal(rd[:, b, :], dn[:, b, :]))
                link(nc.vector.tensor_tensor(gsc[:, b, :], rd[:, b, :], N["gates"][:, i, 3 * h + 1:3 * h + 3], ALU.mult))
                dve.wait_ge(q["a_po"], u + 1)
                link(nc.vector.scalar_tensor_tensor(out=o, in0=PO[:, 0:HD], scalar=gsc[:, b, 0:1], in1=o,
                                                    op0=ALU.mult, op1=ALU.add))
                nc.vector.scalar_tensor_tensor(out=o, in0=PO[:, HD:2 * HD], scalar=gsc[:, b, 1:2], in1=o,
                                               op0=ALU.mult, op1=ALU.add).then_inc(q["a_pod"], 1)
                dve.wait_ge(q["a_pod"], u + 1)

            def cmp_combine(s):
                i, kv = steps[s]
                dve.wait_ge(q["a_co"], s + 1)
                if i >= 2 and kv == 0:
                    dve.wait_ge(q["a_oT"], i - 1)
                for g in range(4):
                    h = 4 * kv + g
                    last = nc.vector.tensor_scalar(oN[:, i % 2, h, :], PC[:, 256 + g * HD:256 + (g + 1) * HD],
                                                   N["gates"][:, i, 3 * h:3 * h + 1], None, ALU.mult)
                last.then_inc(q["a_cod"], 1)
                dve.wait_ge(q["a_cod"], s + 1)

            cmp_masked(0)
            cmp_norm(0)
            importance(0)
            select(0)
            cmp_combine(0)
            for u in range(-2, len(heads)):
                if u + 2 < len(heads):
                    compressed = u >= 0 and u % 4 == 0 and u // 4 + 1 < len(steps)
                    masked(u + 2, (lambda: cmp_masked(u // 4 + 1)) if compressed else None)
                if u >= 0:
                    i, kv, g = heads[u]
                    s = u // 4
                    more = s + 1 < len(steps)
                    combine(u)
                    if g == 0 and more:
                        cmp_norm(s + 1)
                        importance(s + 1)
                    if g == 1 and more:
                        select(s + 1)
                    if g == 3 and more:
                        cmp_combine(s + 1)
                    if g == 3 and kv == 1:
                        dve.sem_inc(q["a_od"], 1)


HD = 64
RW = 512
PAIRS = 4
CH = 64
NCH = S // CH
LEVELS = 5
LAG = 2
LNX_EPS = 64e-5
E_HALF = float(np.exp(-0.5))
(MU_R, MU_K, MU_V, W0, A0, K_K, K_A, R_K) = range(8)


def lora_phase(nc, T, R):
    with ExitStack() as ctx:
        sb = lambda n, s, dt=F32: ctx.enter_context(nc.sbuf_tensor(n, s, dt))
        wl = sb("l_w", [P, DC, 256])
        wb = sb("l_wb", [P, DC, 256])
        mu = sb("l_mu", [P, 3, DC])
        PH = ctx.enter_context(nc.psum_tensor("l_PH", [P, 4, BANK], F32))
        q = sems(nc, ctx, "l_ld l_ldg l_rest l_d l_m")
        block = ctx.enter_context(nc.Block())
        parts = ((0, 0, 64), (1, 64, 128), (2, 128, 256))

        @block.sync
        def _(sp):
            sp.dma_start(mu[:, :, :], T["mu_wag_cols"]).then_inc(q["l_ld"], 16)
            for (_, a, b), src in zip(parts[:2], (T["rw_w1"], T["rw_a1"])):
                sp.dma_start(wl[:, :, a:b], src[0].rearrange("(k p) f -> p k f", p=P)).then_inc(q["l_ld"], 16)
            sp.dma_start(wl[:, :, P:2 * P], T["rw_g1"][0].rearrange("(k p) f -> p k f", p=P)).then_inc(q["l_ldg"], 16)
            sp.wait_ge(q["l_ldg"], 16)
            sp.dma_start(R["cols"][:, :, :], T["rw_cols"]).then_inc(q["l_rest"], 16)
            sp.dma_start(R["w2a2"][0:64, :], T["rw_w2"][0]).then_inc(q["l_rest"], 16)
            sp.dma_start(R["w2a2"][64:P, :], T["rw_a2"][0]).then_inc(q["l_rest"], 16)
            sp.dma_start(R["g2"][:, :], T["rw_g2"][0]).then_inc(q["l_rest"], 16)
            sp.dma_start(R["lng"][:, :], T["rw_lnx_g"].broadcast_to([P, RW])).then_inc(q["l_rest"], 16)
            sp.dma_start(R["lnb"][:, :], T["rw_lnx_b"].broadcast_to([P, RW])).then_inc(q["l_rest"], 16)
            sp.dma_start(R["masks"][:, :, :], T["c_masks"]).then_inc(q["l_rest"], 16)
            sp.dma_start(R["blockones"][:, :], T["c_blockones"]).then_inc(q["l_rest"], 16)
            sp.dma_start(R["ident2"][:, :], T["c_ident2"]).then_inc(q["l_rest"], 16)

        @block.vector
        def _(dve):
            def shifted(a, b, j):
                return nc.vector.tensor_tensor(wb[:, :, a:b], wl[:, :, a:b], mu[:, j, :, None].broadcast_to([P, DC, b - a]),
                                               ALU.mult)

            def rest(half):
                cols = slice(half * P, (half + 1) * P)
                dve.wait_ge(q["l_d"], 2 * half + 1)
                nc.vector.tensor_tensor(wl[:, :, cols], wl[:, :, cols], wb[:, :, cols], ALU.subtract).then_inc(q["l_d"], 1)

            dve.wait_ge(q["l_ld"], 16 * 3)
            shifted(0, 64, 0)
            shifted(64, P, 1).then_inc(q["l_d"], 1)
            rest(0)
            dve.wait_ge(q["l_ldg"], 16)
            shifted(P, 2 * P, 2).then_inc(q["l_d"], 1)
            rest(1)
            dve.wait_ge(q["l_rest"], 16 * 9)
            nc.vector.tensor_scalar(R["omcols"][:, :, :], R["cols"][:, :, :], -1.0, 1.0, ALU.mult, ALU.add)

        @block.tensor
        def _(pe):
            for m in range(2):
                pe.wait_ge(q["l_d"], 2 * m + 2)
                for n in range(2):
                    for k in range(DC):
                        nc.tensor.matmul(PH[:, 2 * m + n, :], wl[:, k, m * P:(m + 1) * P],
                                         T["xnT"][:, k, 1 + n * BANK:1 + (n + 1) * BANK], start=(k == 0), stop=False)
                        last = nc.tensor.matmul(PH[:, 2 * m + n, :], wb[:, k, m * P:(m + 1) * P],
                                                T["xnT"][:, k, n * BANK:(n + 1) * BANK], start=False, stop=(k == DC - 1))
                last.then_inc(q["l_m"], 1)

        @block.scalar
        def _(act):
            act.wait_ge(q["l_m"], 1)
            hid = PH[:, 0:2, :].rearrange("p a b -> p (a b)")
            nc.scalar.activation(R["hwa"][0:64, :], hid[0:64, :], ACT.Tanh)
            nc.scalar.activation(R["hwa"][64:P, :], hid[64:P, :], ACT.Copy)
            act.wait_ge(q["l_m"], 2)
            nc.scalar.activation(R["hg"][:, :], PH[:, 2:4, :].rearrange("p a b -> p (a b)"), ACT.Sigmoid)


def features_phase(nc, T, R, F, p):
    with ExitStack() as ctx:
        sb = lambda n, s, dt=F32: ctx.enter_context(nc.sbuf_tensor(f"f{p}_{n}", s, dt))
        W = sb("W", [P, DC, 3, P])
        raw = sb("raw", [P, 3, S + 1])
        mix = sb("mix", [P, 3, S])
        tmp = sb("tmp", [P, S])
        kk = sb("kk", [P, S])
        a = sb("a", [P, S])
        dec = sb("dec", [P, S])
        cum = sb("cum", [P, NCH, CH + 1])
        inv = sb("inv", [P, S])
        icum = sb("icum", [P, S])
        gain = sb("gain", [P, S])
        zero = sb("zero", [P, CH])
        PX = ctx.enter_context(nc.psum_tensor(f"f{p}_PX", [P, 4, 2, BANK], F32))
        q = sems(nc, ctx, "ld mm mv ev km sq ss nrm za sga dec d z", f"f{p}_")
        block = ctx.enter_context(nc.Block())
        col = lambda j: R["cols"][:, p, j:j + 1]
        om = lambda j: R["omcols"][:, p, j:j + 1]
        ch = slice(p * P, (p + 1) * P)
        wide = lambda n: PX[:, n, :, :].rearrange("p a b -> p (a b)")

        @block.sync
        def _(sp):
            for j in range(3):
                sp.dma_start(W[:, :, j, :], T["w_in"][0, :, j * RW + p * P:j * RW + (p + 1) * P]
                             .rearrange("(k p) f -> p k f", p=P)).then_inc(q["ld"], 16)

        @block.tensor
        def _(pe):
            for n in range(2):
                nc.tensor.matmul(PX[:, 0, n, :], R["w2a2"][0:64, ch], R["hwa"][0:64, n * BANK:(n + 1) * BANK], start=True, stop=True)
            for n in range(2):
                last = nc.tensor.matmul(PX[:, 1, n, :], R["w2a2"][64:P, ch], R["hwa"][64:P, n * BANK:(n + 1) * BANK],
                                        start=True, stop=True)
            last.then_inc(q["za"], 1)
            pe.wait_ge(q["ld"], 48)
            for j, bank in ((1, 2), (0, 3), (2, 0)):
                if bank == 0:
                    pe.wait_ge(q["sga"], 1)
                for n in range(2):
                    for k in range(DC):
                        last = nc.tensor.matmul(PX[:, bank, n, :], W[:, k, j, :], T["xnT"][:, k, 1 + n * BANK:1 + (n + 1) * BANK],
                                                start=(k == 0), stop=(k == DC - 1))
                    if bank == 3 and n == 0:
                        pe.wait_ge(q["sga"], 2)
                        pe.wait_ge(q["sq"], 1)
                        for m in range(2):
                            sums = nc.tensor.matmul(PX[:, 1, m, :], R["blockones"][:, :], tmp[:, m * BANK:(m + 1) * BANK],
                                                    start=True, stop=True)
                        sums.then_inc(q["ss"], 1)
                    if bank == 0:
                        last.then_inc(q["mv"], 1)
                if bank == 0:
                    continue
                last.then_inc(q["mm"], 1)

        @block.scalar
        def _(act):
            act.wait_ge(q["za"], 1)
            nc.scalar.activation(dec[:, :], wide(0), ACT.Sigmoid, bias=col(W0)).then_inc(q["sga"], 1)
            nc.scalar.activation(a[:, :], wide(1), ACT.Sigmoid, bias=col(A0)).then_inc(q["sga"], 1)
            act.wait_ge(q["sga"], 2)
            nc.scalar.activation(dec[:, :], dec[:, :], ACT.Exp, scale=-E_HALF).then_inc(q["dec"], 1)
            nc.scalar.activation(gain[:, :], a[:, :], ACT.Identity, bias=om(K_A), scale=col(K_A)).then_inc(q["sga"], 1)

            def evac(m, j, bank):
                act.wait_ge(q["mm"], m + 1)
                nc.scalar.activation(raw[:, j, 1:S + 1], wide(bank), ACT.Copy)
                nc.scalar.activation(mix[:, j, :], wide(bank), ACT.Copy, scale=om(j)).then_inc(q["ev"], 1)

            act.wait_ge(q["z"], 1)
            evac(0, 1, 2)
            act.wait_ge(q["km"], 1)
            nc.scalar.activation(tmp[:, :], mix[:, 1, :], ACT.Square, scale=col(K_K)).then_inc(q["sq"], 1)
            act.wait_ge(q["ss"], 1)
            nc.scalar.activation(inv[:, :], wide(1), ACT.Sqrt).then_inc(q["nrm"], 1)
            evac(1, 0, 3)
            for n in range(2):
                act.wait_ge(q["mv"], n + 1)
                nc.scalar.activation(raw[:, 2, 1 + n * BANK:1 + (n + 1) * BANK], PX[:, 0, n, :], ACT.Copy)
                nc.scalar.activation(mix[:, 2, n * BANK:(n + 1) * BANK], PX[:, 0, n, :], ACT.Copy,
                                     scale=om(2)).then_inc(q["ev"], 1)

        @block.vector
        def _(dve):
            link = chained(dve, q["d"])
            nc.vector.memset(raw[:, :, 0], 0.0)
            nc.vector.memset(cum[:, :, 0], 1.0)
            nc.vector.memset(zero[:, :], 0.0).then_inc(q["z"], 1)
            dve.wait_ge(q["z"], 1)
            r, k, v = mix[:, 0, :], mix[:, 1, :], mix[:, 2, :]
            cs = cum[:, :, 1:CH + 1]
            prev = cum[:, :, 0:CH]
            last_c = cum[:, :, CH:CH + 1].broadcast_to([P, NCH, CH])
            by = lambda t: t.rearrange("p (c t) -> p c t", t=CH)
            dve.wait_ge(q["dec"], 1)
            for c in range(NCH):
                last = nc.vector.tensor_tensor_scan(cum[:, c, 1:CH + 1], dec[:, c * CH:(c + 1) * CH], zero[:, :], 1.0,
                                                    ALU.mult, ALU.add)
            link(last)
            link(nc.vector.reciprocal(by(icum[:, :]), cs))
            link(nc.vector.tensor_tensor(F["dc"][:, :, :], R["ident2"][:, None, :].broadcast_to([P, NCH, CH]), last_c, ALU.mult))

            def mixed(j, m, out, a=0, b=S):
                dve.wait_ge(q["ev"], m)
                return nc.vector.scalar_tensor_tensor(out=out, in0=raw[:, j, a:b], scalar=col(j), in1=mix[:, j, a:b],
                                                      op0=ALU.mult, op1=ALU.add)

            mixed(1, 1, k).then_inc(q["km"], 1)
            dve.wait_ge(q["km"], 1)
            link(nc.vector.tensor_scalar(kk[:, :], k, col(K_K), None, ALU.mult))
            dve.wait_ge(q["sga"], 3)
            dve.wait_ge(q["sq"], 1)
            link(nc.vector.tensor_tensor(k, k, gain[:, :], ALU.mult))
            link(nc.vector.tensor_tensor(F["kt"][:, :], k, icum[:, :], ALU.mult))
            link(nc.vector.tensor_tensor(by(F["ke"][:, :]), by(F["kt"][:, :]), last_c, ALU.mult))
            dve.wait_ge(q["nrm"], 1)
            link(nc.vector.tensor_scalar(inv[:, :], inv[:, :], 1e-12, None, ALU.max))
            link(nc.vector.reciprocal(inv[:, :], inv[:, :]))
            link(nc.vector.tensor_tensor(kk[:, :], kk[:, :], inv[:, :], ALU.mult))
            link(nc.vector.scalar_tensor_tensor(out=by(F["ar"][:, 0, :]), in0=by(kk[:, :]), scalar=-1.0, in1=prev,
                                                op0=ALU.mult, op1=ALU.mult))
            link(nc.vector.tensor_tensor(kk[:, :], kk[:, :], a[:, :], ALU.mult))
            link(nc.vector.tensor_tensor(F["bt"][:, :], kk[:, :], icum[:, :], ALU.mult))
            link(nc.vector.tensor_tensor(by(F["be"][:, :]), by(F["bt"][:, :]), last_c, ALU.mult))
            link(mixed(0, 2, r))
            link(nc.vector.scalar_tensor_tensor(out=F["bonus"][:, :], in0=r, scalar=col(R_K), in1=k, op0=ALU.mult, op1=ALU.mult))
            link(nc.vector.tensor_tensor(by(F["ar"][:, 1, :]), by(r), cs, ALU.mult))
            for n in range(2):
                link(mixed(2, 3 + n, F["v"][:, n * BANK:(n + 1) * BANK], n * BANK, (n + 1) * BANK))


def chunks_phase(nc, T, R, F, p):
    with ExitStack() as ctx:
        names = ("turned turned_out scored masked rest_masked levels d_first d_turned p_done p_out d_done d_ready dt_done dt_ready "
                 "lv_done lv_out w_done w_out q_done q_out y_done y_out link").split()
        chain = sems(nc, ctx, " ".join(["state_done state_added"] + [f"{x}_{n}" for x in "ab" for n in names]), f"k{p}_")
        streams = []
        for x in "ab":
            sb = lambda n, s, dt=F32: ctx.enter_context(nc.sbuf_tensor(f"k{p}{x}_{n}", s, dt))
            pb = lambda n: ctx.enter_context(nc.psum_tensor(f"k{p}{x}_{n}", [P, BANK], F32))
            streams.append({
                "tk": sb("tk", [P, 4, P]), "sc": sb("sc", [P, 2, 4, P]), "mt": sb("mt", [P, LEVELS, 2, P]),
                "D": sb("D", [P, 2, P]), "Dt": sb("Dt", [P, 2, P]), "Ps": sb("Ps", [P, 2, P]),
                "LV": sb("LV", [P, 2, CH]), "WZ": sb("WZ", [P, 2, 2, CH]),
                "S": [pb("S0"), pb("S1")], "X": pb("X"), "DD": pb("DD"),
                "q": {n: chain[f"{x}_{n}"] for n in names}})
        block = ctx.enter_context(nc.Block())
        rows = lambda hh: slice(CH * hh, CH * hh + CH)
        quad = lambda bank: bank.rearrange("p (a b) -> p a b", b=P)
        K_LV, K_W, K_MAPS, K_STATE, K_OUT = range(3 + 2 * LEVELS, 8 + 2 * LEVELS)
        STAGES = K_OUT + 1
        ST = F["ST"]
        PER = NT // 2

        def schedule(stage_of):
            for step in range(PER * STAGES + LAG):
                for x in range(2):
                    at = step - LAG * x
                    if 0 <= at < PER * STAGES:
                        n, k = at // STAGES, at % STAGES
                        stage_of(streams[x], streams[x]["q"], n, 2 * n + x, k)

        @block.tensor
        def _(pe):
            def step(B, t, c):
                for hh in range(2):
                    last = nc.tensor.matmul(B["S"][1][0:CH, hh * CH:(hh + 1) * CH],
                                            F["gh"][:, t, c, 2 * hh * CH:(2 * hh + 1) * CH], ST[:, 2 * t + c, hh, :],
                                            start=True, stop=True)
                last.then_inc(chain["state_done"], 1)

            def stage(B, q, n, t, k):
                tok = slice(t * P, (t + 1) * P)
                tk, sc, WZ, Dt = B["tk"], B["sc"], B["WZ"], B["Dt"]
                if k == 0:
                    if n:
                        pe.wait_ge(q["q_out"], 3 * n)
                    for j, src in enumerate((F["ar"][:, 0, tok], F["be"][:, tok], F["ke"][:, tok], F["v"][:, tok])):
                        last = nc.tensor.transpose(B["X"][:, j * P:(j + 1) * P], src, T["ident"][:, :])
                    last.then_inc(q["turned"], 1)
                elif k == 1:
                    if n:
                        pe.wait_ge(chain["state_added"], 2 * t - 1)
                    for hh in range(2):
                        nc.tensor.matmul(B["S"][hh][:, 0:2 * P], F["bt"][rows(hh), tok], F["ar"][rows(hh), :, tok],
                                         start=True, stop=True)
                        last = nc.tensor.matmul(B["S"][hh][:, 2 * P:4 * P], F["kt"][rows(hh), tok], F["ar"][rows(hh), :, tok],
                                                start=True, stop=True)
                        last.then_inc(q["scored"], 1)
                elif k == 2:
                    if n:
                        pe.wait_ge(q["y_out"], n)
                    pe.wait_ge(q["d_first"], n + 1)
                    for hh in range(2):
                        last = nc.tensor.transpose(B["DD"][:, hh * P:(hh + 1) * P], Dt[:, hh, :], T["ident"][:, :])
                    last.then_inc(q["d_turned"], 1)
                elif k < 3 + 2 * LEVELS:
                    l, second = (k - 3) // 2, (k - 3) % 2
                    if not second:
                        pe.wait_ge(q["d_ready"], LEVELS * n + l + 1)
                        pe.wait_ge(q["levels"], LEVELS * n + l + 1)
                        if l == 0:
                            pe.wait_ge(q["turned_out"], n + 1)
                        for hh in range(2):
                            last = nc.tensor.matmul(B["X"][:, hh * P:(hh + 1) * P], B["mt"][:, l, hh, :], B["D"][:, hh, :],
                                                    start=True, stop=True)
                        last.then_inc(q["p_done"], 1)
                    else:
                        pe.wait_ge(q["p_out"], LEVELS * n + l + 1)
                        if l:
                            pe.wait_ge(q["dt_ready"], LEVELS * n + l)
                        if l < LEVELS - 1:
                            for hh in range(2):
                                last = nc.tensor.matmul(B["X"][:, (2 + hh) * P:(3 + hh) * P], Dt[:, hh, :], B["Ps"][:, hh, :],
                                                        start=True, stop=True)
                            last.then_inc(q["d_done"], 1)
                        for hh in range(2):
                            last = nc.tensor.matmul(B["DD"][:, hh * P:(hh + 1) * P], B["Ps"][:, hh, :], Dt[:, hh, :],
                                                    start=True, stop=True)
                        last.then_inc(q["dt_done"], 1)
                elif k == K_LV:
                    pe.wait_ge(q["rest_masked"], 2 * n + 2)
                    for hh in range(2):
                        last = nc.tensor.matmul(B["S"][0][:, hh * CH:(hh + 1) * CH], sc[:, hh, 2, :], tk[:, 3, rows(hh)],
                                                start=True, stop=True)
                    last.then_inc(q["lv_done"], 1)
                elif k == K_W:
                    pe.wait_ge(q["dt_ready"], LEVELS * (n + 1))
                    pe.wait_ge(q["lv_out"], n + 1)
                    for hh in range(2):
                        nc.tensor.matmul(B["S"][1][:, 2 * hh * CH:(2 * hh + 1) * CH], Dt[:, hh, :], tk[:, 0, rows(hh)],
                                         start=True, stop=True)
                        last = nc.tensor.matmul(B["S"][1][:, (2 * hh + 1) * CH:(2 * hh + 2) * CH], Dt[:, hh, :],
                                                B["LV"][:, hh, :], start=True, stop=True)
                    last.then_inc(q["w_done"], 1)
                elif k == K_MAPS:
                    pe.wait_ge(q["w_out"], n + 1)
                    for hh in range(2):
                        o = B["S"][0][0:CH, hh * P:(hh + 1) * P]
                        nc.tensor.matmul(o, WZ[:, hh, 0, :], sc[:, hh, 1, :], start=True, stop=False)
                        last = nc.tensor.matmul(o, T["ident"][:, rows(hh)], F["ar"][:, 1, tok], start=False, stop=True)
                    last.then_inc(q["q_done"], 1)
                    for c in range(2):
                        half = rows(c)
                        bank = B["X"] if c else B["S"][1]
                        for hh in range(2):
                            g = bank[0:CH, 2 * hh * CH:(2 * hh + 1) * CH]
                            nc.tensor.matmul(g, WZ[half, hh, 0, :], tk[half, 1, rows(hh)], start=True, stop=False)
                            nc.tensor.matmul(g, T["ident"][:, rows(hh)], F["dc"][:, 2 * t + c, :], start=False, stop=True)
                            h = bank[0:CH, (2 * hh + 1) * CH:(2 * hh + 2) * CH]
                            nc.tensor.matmul(h, tk[half, 1, rows(hh)], WZ[half, hh, 1, :], start=True, stop=False)
                            last = nc.tensor.matmul(h, tk[half, 2, rows(hh)], tk[half, 3, rows(hh)], start=False, stop=True)
                        last.then_inc(q["q_done"], 1)
                elif k == K_STATE:
                    pe.wait_ge(q["q_out"], 3 * n + 3)
                    pe.wait_ge(chain["state_added"], 2 * t + 1)
                    step(B, t, 0)
                else:
                    pe.wait_ge(chain["state_added"], 2 * t + 2)
                    if 2 * t + 1 < NCH - 1:
                        step(B, t, 1)
                    for hh in range(2):
                        o = B["DD"][:, hh * CH:(hh + 1) * CH]
                        nc.tensor.matmul(o, sc[:, hh, 1, :], WZ[:, hh, 1, :], start=True, stop=False)
                        nc.tensor.matmul(o, sc[:, hh, 3, :], tk[:, 3, rows(hh)], start=False, stop=False)
                        for c in range(2):
                            last = nc.tensor.matmul(B["DD"][rows(c), hh * CH:(hh + 1) * CH], F["qt"][:, t, hh, rows(c)],
                                                    ST[:, 2 * t + c, hh, :], start=False, stop=True)
                    last.then_inc(q["y_done"], 1)

            schedule(stage)

        @block.scalar
        def _(act):
            def stage(B, q, n, t, k):
                if k == 0:
                    act.wait_ge(q["turned"], n + 1)
                    if n:
                        act.wait_ge(q["y_done"], n)
                    nc.scalar.activation(F["vt"][:, t, :], B["X"][:, 3 * P:4 * P], ACT.Copy)
                    nc.scalar.activation(B["tk"][:, :, :], quad(B["X"][:, :]), ACT.Copy).then_inc(q["turned_out"], 1)
                elif 3 <= k < 3 + 2 * LEVELS and (k - 3) % 2 == 0:
                    l = (k - 3) // 2
                    act.wait_ge(q["p_done"], LEVELS * n + l + 1)
                    nc.scalar.activation(B["Ps"][:, :, :], quad(B["X"][:, 0:2 * P]), ACT.Copy).then_inc(q["p_out"], 1)
                elif k == K_LV:
                    act.wait_ge(q["lv_done"], n + 1)
                    nc.scalar.activation(B["LV"][:, :, :].rearrange("p a b -> p (a b)"), B["S"][0][:, 0:2 * CH], ACT.Copy
                                         ).then_inc(q["lv_out"], 1)
                elif k == K_W:
                    act.wait_ge(q["w_done"], n + 1)
                    nc.scalar.activation(B["WZ"][:, :, :, :].rearrange("p a b c -> p (a b c)"), B["S"][1][:, 0:4 * CH], ACT.Copy
                                         ).then_inc(q["w_out"], 1)
                elif k == K_MAPS:
                    act.wait_ge(q["q_done"], 3 * n + 1)
                    nc.scalar.activation(F["qt"][:, t, :, :], quad(B["S"][0][0:CH, 0:2 * P]), ACT.Copy).then_inc(q["q_out"], 1)
                    for c in range(2):
                        act.wait_ge(q["q_done"], 3 * n + 2 + c)
                        nc.scalar.activation(F["gh"][:, t, c, :], (B["X"] if c else B["S"][1])[0:CH, 0:4 * CH], ACT.Copy
                                             ).then_inc(q["q_out"], 1)

            schedule(stage)

        @block.vector
        def _(dve):
            links = [chained(dve, B["q"]["link"]) for B in streams]
            nc.vector.memset(ST[:, 0, :, :], 0.0).then_inc(chain["state_added"], 1)

            def add(B, t, c):
                at = 2 * t + c
                dve.wait_ge(chain["state_done"], at + 1)
                H = F["gh"][:, t, c, :].rearrange("p (a b c) -> p a b c", b=2, c=CH)[:, :, 1, :]
                nc.vector.tensor_tensor(ST[:, at + 1, :, :], B["S"][1][0:CH, 0:P].rearrange("p (a b) -> p a b", b=CH), H,
                                        ALU.add).then_inc(chain["state_added"], 1)

            def stage(B, q, n, t, k):
                link = links[t % 2]
                D, Dt, DD = B["D"], B["Dt"], B["DD"]
                if k == 1:
                    if n:
                        dve.wait_ge(q["y_done"], n)
                    for hh in range(2):
                        dve.wait_ge(q["scored"], 2 * n + hh + 1)
                        nc.vector.tensor_tensor(B["sc"][:, hh, 0, :], B["S"][hh][:, 0:P], R["masks"][:, 0, :],
                                                ALU.mult).then_inc(q["masked"], 1)
                    dve.wait_ge(q["masked"], 2 * n + 2)
                    link(nc.vector.tensor_tensor(Dt[:, :, :], B["sc"][:, :, 0, :],
                                                 R["masks"][:, 4, None, :].broadcast_to([P, 2, P]), ALU.mult))
                    nc.vector.tensor_tensor(Dt[:, :, :], Dt[:, :, :], T["ident"][:, None, :].broadcast_to([P, 2, P]),
                                            ALU.add).then_inc(q["d_first"], 1)
                    dve.wait_ge(q["d_first"], n + 1)
                elif k == 2:
                    dve.wait_ge(q["d_turned"], n + 1)
                    nc.vector.tensor_copy(D[:, :, :], quad(DD[:, 0:2 * P])).then_inc(q["d_ready"], 1)
                    for hh in range(2):
                        nc.vector.tensor_tensor(B["sc"][:, hh, 1:4, :], quad(B["S"][hh][:, :])[:, 1:4, :], R["masks"][:, 1:4, :],
                                                ALU.mult).then_inc(q["rest_masked"], 1)
                    dve.wait_ge(q["d_ready"], LEVELS * n + 1)
                elif 3 <= k < 3 + 2 * LEVELS and (k - 3) % 2:
                    l = (k - 3) // 2
                    if l < LEVELS - 1:
                        dve.wait_ge(q["d_done"], (LEVELS - 1) * n + l + 1)
                        nc.vector.tensor_tensor(D[:, :, :], quad(B["X"][:, 2 * P:4 * P]), D[:, :, :], ALU.add
                                                ).then_inc(q["d_ready"], 1)
                    dve.wait_ge(q["dt_done"], LEVELS * n + l + 1)
                    nc.vector.tensor_tensor(Dt[:, :, :], quad(DD[:, 0:2 * P]), Dt[:, :, :], ALU.add
                                            ).then_inc(q["dt_ready"], 1)
                    if l < LEVELS - 1:
                        dve.wait_ge(q["d_ready"], LEVELS * n + l + 2)
                    dve.wait_ge(q["dt_ready"], LEVELS * n + l + 1)
                elif k == K_STATE:
                    add(B, t, 0)
                elif k == K_OUT:
                    if 2 * t + 1 < NCH - 1:
                        add(B, t, 1)
                    dve.wait_ge(q["y_done"], n + 1)
                    nc.vector.tensor_copy(F["y"][:, t, :, :], B["DD"][:, 0:2 * CH].rearrange("p (a b) -> p a b", b=CH)
                                          ).then_inc(q["y_out"], 1)

            schedule(stage)

        @block.gpsimd
        def _(pool):
            def stage(B, q, n, t, k):
                if k == 1:
                    pool.wait_ge(q["masked"], 2 * n + 2)
                    if n:
                        pool.wait_ge(q["p_done"], LEVELS * n)
                    for l in range(LEVELS):
                        nc.gpsimd.tensor_tensor(B["mt"][:, l, :, :], B["sc"][:, :, 0, :],
                                                R["masks"][:, 5 + l, None, :].broadcast_to([P, 2, P]), ALU.mult
                                                ).then_inc(q["levels"], 1)

            schedule(stage)


def gated_phase(nc, T, R, F, p):
    with ExitStack() as ctx:
        sb = lambda n, s, dt=F32: ctx.enter_context(nc.sbuf_tensor(f"s{p}_{n}", s, dt))
        pb = lambda n, s: ctx.enter_context(nc.psum_tensor(f"s{p}_{n}", s, F32))
        tmp = sb("tmp", [P, NT, P])
        gs = sb("gs", [P, NT, P])
        bn = sb("bn", [P, NT, 2])
        mean = sb("mean", [P, NT, 2])
        var = sb("var", [P, NT, 2])
        PY = pb("PY", [P, 2, BANK])
        PG = pb("PG", [P, 2, BANK])
        PB = pb("PB", [P, BANK])
        q = sems(nc, ctx, "g d vs vq yd yt ge", f"s{p}_")
        block = ctx.enter_context(nc.Block())
        ch = slice(p * P, (p + 1) * P)

        @block.tensor
        def _(pe):
            def gates(i):
                nc.tensor.matmul(PG[:, i // 4, (i % 4) * P:(i % 4 + 1) * P], R["hg"][:, i * P:(i + 1) * P], R["g2"][:, ch],
                                 start=True, stop=True)
                last = nc.tensor.matmul(PB[:, 2 * i:2 * i + 2], F["bonus"][:, i * P:(i + 1) * P], R["blockones"][:, 0:P:CH],
                                        start=True, stop=True)
                if i == NT - 1:
                    last.then_inc(q["g"], 1)

            for i in range(NT):
                gates(i)
            for g in range(2):
                pe.wait_ge(q["yd"], 1)
                for t in range(4):
                    i = 4 * g + t
                    last = nc.tensor.transpose(PY[:, g, t * P:(t + 1) * P], F["y"][:, i, :, :].rearrange("p a b -> p (a b)"),
                                               T["ident"][:, :])
                last.then_inc(q["yt"], 1)

        @block.vector
        def _(dve):
            link = chained(dve, q["d"])
            Y = F["y"][:, :, :, :].rearrange("p a b c -> p (a b) c")
            flat = F["y"][:, :, :, :].rearrange("p a b c -> p a (b c)")
            G16 = lambda t: t.rearrange("p a b -> p (a b)")[:, :, None].broadcast_to([P, 2 * NT, CH])
            link(nc.vector.tensor_reduce(mean[:, :, :].rearrange("p a b -> p (a b)"), Y, AX.X, ALU.add))
            link(nc.vector.tensor_scalar(mean[:, :, :], mean[:, :, :], 1.0 / CH, None, ALU.mult))
            link(nc.vector.tensor_tensor(Y, Y, G16(mean[:, :, :]), ALU.subtract))
            t16 = tmp[:, :, :].rearrange("p a (b c) -> p (a b) c", c=CH)
            link(nc.vector.tensor_tensor(t16, Y, Y, ALU.mult))
            link(nc.vector.tensor_reduce(var[:, :, :].rearrange("p a b -> p (a b)"), t16, AX.X, ALU.add))
            nc.vector.tensor_scalar(var[:, :, :], var[:, :, :], 1.0 / CH, LNX_EPS, ALU.mult, ALU.add).then_inc(q["vs"], 1)
            dve.wait_ge(q["g"], 1)
            link(nc.vector.tensor_copy(bn[:, :, :], PB[:, 0:2 * NT].rearrange("p (a b) -> p a b", b=2)))
            link(nc.vector.tensor_tensor(t16, F["vt"][:, :, :].rearrange("p a (b c) -> p (a b) c", c=CH), G16(bn[:, :, :]), ALU.mult))
            dve.wait_ge(q["vq"], 1)
            link(nc.vector.reciprocal(var[:, :, :], var[:, :, :]))
            link(nc.vector.tensor_tensor(Y, Y, G16(var[:, :, :]), ALU.mult))
            link(nc.vector.tensor_tensor(flat, flat, R["lng"][:, None, ch].broadcast_to([P, NT, P]), ALU.mult))
            link(nc.vector.tensor_tensor(flat, flat, R["lnb"][:, None, ch].broadcast_to([P, NT, P]), ALU.add))
            link(nc.vector.tensor_tensor(flat, flat, tmp[:, :, :], ALU.add))
            dve.wait_ge(q["ge"], 1)
            nc.vector.tensor_tensor(flat, flat, gs[:, :, :], ALU.mult).then_inc(q["yd"], 1)

        @block.scalar
        def _(act):
            act.wait_ge(q["g"], 1)
            nc.scalar.activation(gs[:, :, :].rearrange("p a b -> p (a b)"), PG[:, :, :].rearrange("p a b -> p (a b)"),
                                 ACT.Copy).then_inc(q["ge"], 1)
            act.wait_ge(q["vs"], 1)
            nc.scalar.activation(var[:, :, :], var[:, :, :], ACT.Sqrt).then_inc(q["vq"], 1)
            for g in range(2):
                act.wait_ge(q["yt"], g + 1)
                nc.scalar.activation(T["yT"][:, p, g * BANK:(g + 1) * BANK], PY[:, g, :], ACT.Copy)


def rwkv(nc, T):
    with ExitStack() as ctx:
        sb = lambda n, s, dt=F32: ctx.enter_context(nc.sbuf_tensor(n, s, dt))
        R = {}
        R["cols"] = sb("rw_cols_sb", [P, PAIRS, 8])
        R["omcols"] = sb("rw_omcols", [P, PAIRS, 8])
        R["w2a2"] = sb("rw_w2a2", [P, RW])
        R["g2"] = sb("rw_g2_sb", [P, RW])
        R["lng"] = sb("rw_lng", [P, RW])
        R["lnb"] = sb("rw_lnb", [P, RW])
        R["masks"] = sb("rw_masks", [P, 10, P])
        R["blockones"] = sb("rw_blockones", [P, P])
        R["ident2"] = sb("rw_ident2", [P, CH])
        R["hwa"] = sb("rw_hwa", [P, S])
        R["hg"] = sb("rw_hg", [P, S])
        lora_phase(nc, T, R)
        F = {}
        F["ar"] = sb("rw_ar", [P, 2, S])
        F["bt"] = sb("rw_bt", [P, S])
        F["kt"] = sb("rw_kt", [P, S])
        F["be"] = sb("rw_be", [P, S])
        F["ke"] = sb("rw_ke", [P, S])
        F["v"] = sb("rw_v", [P, S])
        F["bonus"] = sb("rw_bonus", [P, S])
        F["dc"] = sb("rw_dc", [P, NCH, CH])
        for p in range(PAIRS):
            features_phase(nc, T, R, F, p)
            with ExitStack() as c2:
                sb2 = lambda n, s: c2.enter_context(nc.sbuf_tensor(f"{n}{p}", s, F32))
                F["qt"] = sb2("rw_qt", [CH, NT, 2, P])
                F["gh"] = sb2("rw_gh", [CH, NT, 2, 2 * P])
                F["y"] = sb2("rw_y", [P, NT, 2, CH])
                F["vt"] = sb2("rw_vt", [P, NT, P])
                F["ST"] = sb2("rw_ST", [CH, NCH, 2, CH])
                chunks_phase(nc, T, R, F, p)
                gated_phase(nc, T, R, F, p)


_NAMES = ["x", "w_in", "rw_w1", "rw_w2", "rw_a1", "rw_a2", "rw_g1", "rw_g2", "rw_lnx_g", "rw_lnx_b", "nsa_qn_g", "nsa_kn_g",
          "nsa_pe", "nsa_cmp_w1", "nsa_cmp_w2", "w_out", "ln2_g", "moe_wr", "moe_br", "moe_w1", "moe_w2"]


def hybrid_layer_kernel(nc, arrays):
    T = dict(arrays)
    T["h_rows"] = nc.dram_tensor("h_rows", [S + PAD_ROWS, D], F32).ap()
    T["token_list"] = nc.dram_tensor("token_list", [P, N_SLOTS, 2], I32).ap()
    with ExitStack() as ctx:
        sb = lambda n, s, dt=F32: ctx.enter_context(nc.sbuf_tensor(n, s, dt))
        T["ident"] = sb("ident", [P, P])
        T["slots"] = sb("slots", [P, N_SLOTS, 2], I32)
        T["counts"] = sb("counts", [1, N_EXP + 1], I32)
        T["yT"] = sb("yT", [P, DC, S])
        with ExitStack() as normed:
            T["xnT"] = normed.enter_context(nc.sbuf_tensor("xnT", [P, DC, S + 1], F32))
            with ExitStack() as attention:
                sa = lambda n, s: attention.enter_context(nc.sbuf_tensor(n, s, F32))
                N = dict(vs=sa("vs", [P, NT, P]), vw=sa("vw", [P, NT, P]), gates=sa("gates", [P, NT, 3 * QH]),
                          qT=sa("qT", [P, 4, S]), qrT=sa("qrT", [P, 4, S]), kT=sa("kT", [P, 4, S]),
                          vcmp=sa("vcmp", [N_CMP, 2, HD]), kcT=sa("kcT", [P, 2, N_CMP]))
                with ExitStack() as blocks:
                    N["cT"] = blocks.enter_context(nc.sbuf_tensor("cT", [P, 4, S + 2], F32))
                    with ExitStack() as projected:
                        T["w_nsa"] = projected.enter_context(nc.sbuf_tensor("w_nsa", [P, DC, NSA_COLS], F32))
                        norm_phase(nc, T)
                        nsa_project_phase(nc, T, N)
                    compress_phase(nc, T, N)
                attention_phase(nc, T, N)
            rwkv(nc, T)
        T["w1"] = [sb(f"w1_{j}", [P, DC, 2, 2 * P]) for j in range(4)]
        route_phase(nc, T)
        expert_pass(nc, T, True)
        expert_pass(nc, T, False)


def _constants():
    f32 = np.float32
    c = {}
    c["c_ident"] = np.eye(P, dtype=f32)
    c["c_upper"] = np.triu(np.ones((P, P), f32), 1)
    c["c_lower"] = np.tril(np.ones((N_EXP, N_EXP), f32), -1).reshape(1, -1)
    pos = np.arange(S)
    inv = (10000.0 ** (-np.arange(HD // 2, dtype=f32) / f32(HD // 2))).astype(f32)
    ang = pos.astype(f32)[:, None] * inv[None, :]
    c["c_cos"] = np.cos(ang).astype(f32)
    c["c_sin"] = np.sin(ang).astype(f32)
    whole = (16 * np.arange(N_CMP) + 31)[None, :] <= pos[:, None]
    c["c_cmask"] = whole.astype(f32)
    c["c_cpen"] = np.where(whole, 0, NEG).astype(f32)
    row, col = np.arange(P)[:, None], np.arange(P)[None, :]
    c["c_wpen"] = np.concatenate([np.where(col > row, 0, NEG), np.zeros((P, P)), np.where(col <= row, 0, NEG)], 1).astype(f32)
    block, cur = np.arange(16)[None, :], (pos // 64)[:, None]
    forced = (block == 0) | (block == cur) | (block == cur - 1)
    future = block > cur
    c["c_free"] = (~(forced | future)).astype(f32)
    c["c_force"] = np.where(future, -1e6, np.where(forced, 1e6, 0)).astype(f32)
    c["c_lower16"] = np.tril(np.ones((16, 16), f32), -1).reshape(1, -1)
    same = lambda n: (row // n) == (col // n)
    masks = [same(CH) & (row < col), same(CH) & (row <= col)] * 2
    for n in (1, 2, 4, 8, 16, 32):
        masks.append(same(2 * n) & ((col // n) % 2 == 1) & ((row // n) % 2 == 0))
    c["c_masks"] = np.stack(masks, 1).astype(f32)
    c["c_blockones"] = same(CH).astype(f32)
    c["c_ident2"] = np.concatenate([np.eye(CH)] * 2, 0).astype(f32)
    return c


def _columns(inputs):
    cols = lambda v: np.asarray(v).reshape(-1, P).T
    mu = np.asarray(inputs["rw_mu_rkv"])[0]
    per_channel = [mu[0], mu[1], mu[2]] + [np.asarray(inputs[k])[0] for k in ("rw_w0", "rw_a0", "rw_k_k", "rw_k_a", "rw_r_k")]
    return {
        "ln1_cols": cols(inputs["ln1_g"]),
        "mu_wag_cols": np.asarray(inputs["rw_mu_wag"])[0].reshape(3, DC, P).transpose(2, 0, 1),
        "moe_bias_cols": np.concatenate([np.asarray(inputs["moe_b1"])[0].reshape(N_EXP, 2 * FC, P),
                                         np.asarray(inputs["moe_b2"])[0].reshape(N_EXP, DC, P)], 1).transpose(2, 0, 1),
        "rw_cols": np.stack([cols(v) for v in per_channel], 2),
    }


def kernel(**inputs):
    import concourse.bacc as _bacc
    from concourse.bass_utils import run_bass_kernel_spmd as _run

    nc = _bacc.Bacc("TRN2", target_bir_lowering=False, num_devices=1)
    sent = {n: inputs[n] for n in _NAMES} | _columns(inputs) | _constants()
    arrays, aps = {}, {}
    for name, a in sent.items():
        a = np.ascontiguousarray(a)
        arrays[f"in_{name}"] = a
        aps[name] = nc.dram_tensor(f"in_{name}", a.shape, mybir.dt.from_np(a.dtype), kind="ExternalInput").ap()
    aps["out"] = nc.dram_tensor("out_rows", (S + PAD_ROWS, D), F32, kind="ExternalOutput").ap()
    hybrid_layer_kernel(nc, aps)
    r = _run(nc, [arrays], core_ids=[0])
    return r.results[0]["out_rows"][:S].reshape(1, S, D)
```
